# Optimizing a Trainium2 kernel written in Bass

```python
import jax, jax.numpy as jnp
from jax import lax
import numpy as np

D_MODEL = 1024
BATCH = 1
SEQ = 256
DEPTH = 1

ATT_HEADS = 8
ATT_HEAD_DIM = 128
ATT_WIDTH = ATT_HEADS * ATT_HEAD_DIM
MOBA_BLOCK = 256
MOBA_TOPK = 3
Q_CHUNK = 128
ROPE_THETA = 500000.0
ROPE_DIM = ATT_HEAD_DIM // 4

GDN_HEADS = 8
GDN_KDIM = 128
GDN_VDIM = 128
GDN_KWIDTH = GDN_HEADS * GDN_KDIM
GDN_VWIDTH = GDN_HEADS * GDN_VDIM
CONV_WIDTH = 4
GDN_CHUNK = 64

EPS = 1e-6
NEG = -1e30

IN_SPLITS = [ATT_WIDTH, ATT_WIDTH, ATT_WIDTH, ATT_WIDTH,
             GDN_KWIDTH, GDN_KWIDTH, GDN_VWIDTH, GDN_VWIDTH,
             GDN_HEADS, GDN_HEADS,
             D_MODEL, D_MODEL]
IN_COLS = int(sum(IN_SPLITS))
IN_OFFSETS = [int(o) for o in np.cumsum(IN_SPLITS)[:-1]]


def rmsnorm(x, w):
    xf = x.astype(jnp.float32)
    y = xf * lax.rsqrt(jnp.mean(xf * xf, axis=-1, keepdims=True) + EPS)
    return (y * w.astype(jnp.float32)).astype(x.dtype)

def l2norm(x):
    return x * lax.rsqrt(jnp.sum(x * x, axis=-1, keepdims=True) + EPS)

def partial_rope(x, pos):
    half = ROPE_DIM // 2
    inv_freq = jnp.power(ROPE_THETA, -jnp.arange(half, dtype=jnp.float32) * (2.0 / ROPE_DIM))
    ang = pos.astype(jnp.float32)[:, None] * inv_freq[None, :]
    cos, sin = jnp.cos(ang), jnp.sin(ang)
    xr = x[..., :ROPE_DIM].astype(jnp.float32)
    x1, x2 = xr[..., :half], xr[..., half:]
    rot = jnp.concatenate([x1 * cos - x2 * sin, x2 * cos + x1 * sin], axis=-1).astype(x.dtype)
    return jnp.concatenate([rot, x[..., ROPE_DIM:]], axis=-1)

def moba_attention(q, k, v):
    bsz, nh, s, dh = q.shape
    nb = -(-s // MOBA_BLOCK)
    pad = nb * MOBA_BLOCK - s
    nc = s // Q_CHUNK
    kk = min(MOBA_TOPK, nb)
    scale = dh ** -0.5
    padw = ((0, 0), (0, 0), (0, pad), (0, 0))
    kblk = jnp.pad(k, padw).reshape(bsz, nh, nb, MOBA_BLOCK, dh)
    vblk = jnp.pad(v, padw).reshape(bsz, nh, nb, MOBA_BLOCK, dh)
    kmean = jnp.mean(kblk.astype(jnp.float32), axis=3)
    qch = q.reshape(bsz, nh, nc, Q_CHUNK, dh)
    head_idx = jnp.arange(nh)[:, None, None]

    def per_batch(args):
        q_b, k_b, v_b, km_b = args

        def per_chunk(c):
            q_c = lax.dynamic_index_in_dim(q_b, c, axis=1, keepdims=False)
            q_pos = c * Q_CHUNK + jnp.arange(Q_CHUNK)
            blk = (c * Q_CHUNK) // MOBA_BLOCK
            gate = jnp.einsum('hqd,hnd->hqn', q_c.astype(jnp.float32), km_b)
            gate = jnp.where((jnp.arange(nb) < blk)[None, None, :], gate, -jnp.inf)
            _, idx = lax.top_k(gate, kk)
            sel_valid = jnp.arange(kk) < blk
            k_sel = k_b[head_idx, idx]
            v_sel = v_b[head_idx, idx]
            s_sel = jnp.einsum('hqd,hqjld->hqjl', q_c, k_sel).astype(jnp.float32) * scale
            s_sel = jnp.where(sel_valid[None, None, :, None], s_sel, NEG)
            k_own = lax.dynamic_index_in_dim(k_b, blk, axis=1, keepdims=False)
            v_own = lax.dynamic_index_in_dim(v_b, blk, axis=1, keepdims=False)
            s_own = jnp.einsum('hqd,hld->hql', q_c, k_own).astype(jnp.float32) * scale
            k_pos = blk * MOBA_BLOCK + jnp.arange(MOBA_BLOCK)
            s_own = jnp.where(k_pos[None, None, :] <= q_pos[None, :, None], s_own, NEG)
            scores = jnp.concatenate([s_sel.reshape(nh, Q_CHUNK, kk * MOBA_BLOCK), s_own], axis=-1)
            p = jax.nn.softmax(scores, axis=-1).astype(v_b.dtype)
            p_sel = p[..., :kk * MOBA_BLOCK].reshape(nh, Q_CHUNK, kk, MOBA_BLOCK)
            p_own = p[..., kk * MOBA_BLOCK:]
            return (jnp.einsum('hqjl,hqjld->hqd', p_sel, v_sel)
                    + jnp.einsum('hql,hld->hqd', p_own, v_own))

        return lax.map(per_chunk, jnp.arange(nc))

    out = lax.map(per_batch, (qch, kblk, vblk, kmean))
    return out.transpose(0, 1, 3, 2, 4).reshape(bsz, s, nh * dh)

def causal_dwconv(x, w):
    width = w.shape[0]
    return lax.conv_general_dilated(x, w[:, None, :], window_strides=(1,), padding=[(width - 1, 0)],
                                    dimension_numbers=('NWC', 'WIO', 'NWC'),
                                    feature_group_count=x.shape[-1])

def gated_deltanet(q, k, v, g, beta):
    bsz, s, nh, dk = q.shape
    dv = v.shape[-1]
    c = GDN_CHUNK
    n = s // c
    q = l2norm(q) * (dk ** -0.5)
    k = l2norm(k)

    def chunks(t):
        return t.reshape(bsz, n, c, nh, -1).transpose(0, 3, 1, 2, 4)

    qc, kc, vc = chunks(q), chunks(k), chunks(v)
    gc = g.reshape(bsz, n, c, nh).transpose(0, 3, 1, 2)
    bc = beta.reshape(bsz, n, c, nh).transpose(0, 3, 1, 2)
    G = jnp.cumsum(gc, axis=-1)
    causal = jnp.tril(jnp.ones((c, c), dtype=bool))
    strict = jnp.tril(jnp.ones((c, c), dtype=bool), k=-1)
    diff = G[..., :, None] - G[..., None, :]
    decay = jnp.where(causal, jnp.exp(jnp.where(causal, diff, 0.0)), 0.0)
    k_beta = kc * bc[..., None]
    m = jnp.where(strict, jnp.einsum('bhnid,bhnjd->bhnij', k_beta, kc) * decay, 0.0)
    a_mat = m + jnp.eye(c, dtype=m.dtype)
    rhs = jnp.concatenate([vc * bc[..., None], k_beta * jnp.exp(G)[..., None]], axis=-1)
    sol = lax.linalg.triangular_solve(a_mat, rhs, left_side=True, lower=True, unit_diagonal=True)
    u, w = sol[..., :dv], sol[..., dv:]
    qk = jnp.where(causal, jnp.einsum('bhnid,bhnjd->bhnij', qc, kc) * decay, 0.0)
    q_dec = qc * jnp.exp(G)[..., None]
    k_dec = kc * jnp.exp(G[..., -1:] - G)[..., None]
    g_last = jnp.exp(G[..., -1])

    def step(state, xs):
        u_i, w_i, q_i, qk_i, k_i, gl_i = xs
        v_new = u_i - jnp.einsum('bhcd,bhde->bhce', w_i, state)
        o_i = jnp.einsum('bhcd,bhde->bhce', q_i, state) + jnp.einsum('bhij,bhje->bhie', qk_i, v_new)
        state = state * gl_i[..., None, None] + jnp.einsum('bhcd,bhce->bhde', k_i, v_new)
        return state, o_i

    xs = tuple(jnp.moveaxis(t, 2, 0) for t in (u, w, q_dec, qk, k_dec, g_last))
    state0 = jnp.zeros((bsz, nh, dk, dv), dtype=jnp.float32)
    _, o = lax.scan(step, state0, xs)
    return o.transpose(1, 0, 3, 2, 4).reshape(bsz, s, nh, dv)

def hybrid_layer(x, pre_norm_w, w_in, conv_w, a_log, dt_bias, gdn_norm_w,
                 w_branch_a, w_branch_b, w_out, post_norm_w):
    bsz, s, _ = x.shape
    f32 = jnp.float32
    h = rmsnorm(x, pre_norm_w)
    proj = jnp.einsum('bsd,de->bse', h, w_in)
    (q_a, k_a, v_a, z_a, q_b, k_b, v_b, z_b,
     beta_logit, decay_logit, gate_a, gate_b) = jnp.split(proj, IN_OFFSETS, axis=-1)

    pos = jnp.arange(s)

    def heads(t):
        return t.reshape(bsz, s, ATT_HEADS, ATT_HEAD_DIM).transpose(0, 2, 1, 3)

    o_a = moba_attention(partial_rope(heads(q_a), pos), partial_rope(heads(k_a), pos), heads(v_a))
    y_a = jnp.einsum('bse,ed->bsd', o_a * jax.nn.silu(z_a), w_branch_a)

    qkv = jax.nn.silu(causal_dwconv(jnp.concatenate([q_b, k_b, v_b], axis=-1), conv_w))
    q_b, k_b, v_b = jnp.split(qkv, [GDN_KWIDTH, 2 * GDN_KWIDTH], axis=-1)
    g = -jnp.exp(a_log.astype(f32)) * jax.nn.softplus(decay_logit.astype(f32) + dt_bias.astype(f32))
    beta = jax.nn.sigmoid(beta_logit.astype(f32))
    o_b = gated_deltanet(q_b.reshape(bsz, s, GDN_HEADS, GDN_KDIM).astype(f32),
                         k_b.reshape(bsz, s, GDN_HEADS, GDN_KDIM).astype(f32),
                         v_b.reshape(bsz, s, GDN_HEADS, GDN_VDIM).astype(f32), g, beta)
    o_b = rmsnorm(o_b, gdn_norm_w).reshape(bsz, s, GDN_VWIDTH).astype(x.dtype)
    y_b = jnp.einsum('bse,ed->bsd', o_b * jax.nn.silu(z_b), w_branch_b)

    merged = jax.nn.sigmoid(gate_a) * y_a + jax.nn.sigmoid(gate_b) * y_b
    out = jnp.einsum('bsd,de->bse', merged, w_out)
    return x + rmsnorm(out, post_norm_w)

def first_inputs(seed: int = 0) -> dict:
    key = jax.random.key(seed)
    ks = jax.random.split(key, 12)
    conv_ch = 2 * GDN_KWIDTH + GDN_VWIDTH
    x = jax.random.normal(ks[0], (BATCH, SEQ, D_MODEL), jnp.float32)
    pre_norm_w = 1.0 + 0.05 * jax.random.normal(ks[1], (DEPTH, D_MODEL), jnp.float32)
    w_in = jax.random.normal(ks[2], (DEPTH, D_MODEL, IN_COLS), jnp.float32) * D_MODEL ** -0.5
    conv_w = jax.random.normal(ks[3], (DEPTH, CONV_WIDTH, conv_ch), jnp.float32) * CONV_WIDTH ** -0.5
    a_log = jnp.log(jax.random.uniform(ks[4], (DEPTH, GDN_HEADS), jnp.float32, 1.0, 16.0))
    dt = jnp.exp(jax.random.uniform(ks[5], (DEPTH, GDN_HEADS), jnp.float32,
                                    float(np.log(1e-3)), float(np.log(1e-1))))
    dt_bias = dt + jnp.log(-jnp.expm1(-dt))
    gdn_norm_w = 1.0 + 0.05 * jax.random.normal(ks[6], (DEPTH, GDN_VDIM), jnp.float32)
    w_branch_a = jax.random.normal(ks[7], (DEPTH, ATT_WIDTH, D_MODEL), jnp.float32) * ATT_WIDTH ** -0.5
    w_branch_b = jax.random.normal(ks[8], (DEPTH, GDN_VWIDTH, D_MODEL), jnp.float32) * GDN_VWIDTH ** -0.5
    w_out = jax.random.normal(ks[9], (DEPTH, D_MODEL, D_MODEL), jnp.float32) * D_MODEL ** -0.5
    post_norm_w = 1.0 + 0.05 * jax.random.normal(ks[10], (DEPTH, D_MODEL), jnp.float32)
    return {"x": x, "pre_norm_w": pre_norm_w, "w_in": w_in, "conv_w": conv_w,
            "a_log": a_log, "dt_bias": dt_bias, "gdn_norm_w": gdn_norm_w,
            "w_branch_a": w_branch_a, "w_branch_b": w_branch_b, "w_out": w_out,
            "post_norm_w": post_norm_w}

def first_block(x, pre_norm_w, w_in, conv_w, a_log, dt_bias, gdn_norm_w,
              w_branch_a, w_branch_b, w_out, post_norm_w):
    for layer in range(DEPTH):
        x = hybrid_layer(x, pre_norm_w[layer], w_in[layer], conv_w[layer], a_log[layer],
                         dt_bias[layer], gdn_norm_w[layer], w_branch_a[layer],
                         w_branch_b[layer], w_out[layer], post_norm_w[layer])
    return x


PLE_DIM = 256
MLA_HEADS = 8
MLA_NOPE_DIM = 64
MLA_ROPE_DIM = 32
MLA_V_DIM = 64
Q_LORA_RANK = 384
KV_LORA_RANK = 256
SB_HEADS = 8
SB_HEAD_DIM = 64
MLA_WIDTH = MLA_HEADS * MLA_V_DIM
SB_WIDTH = SB_HEADS * SB_HEAD_DIM
MIX_WIDTH = MLA_WIDTH + SB_WIDTH
IN_SPLITS_2 = (Q_LORA_RANK,
             Q_LORA_RANK + KV_LORA_RANK,
             Q_LORA_RANK + KV_LORA_RANK + MLA_ROPE_DIM,
             Q_LORA_RANK + KV_LORA_RANK + MLA_ROPE_DIM + SB_WIDTH,
             Q_LORA_RANK + KV_LORA_RANK + MLA_ROPE_DIM + 2 * SB_WIDTH)
IN_COLS_2 = Q_LORA_RANK + KV_LORA_RANK + MLA_ROPE_DIM + 3 * SB_WIDTH
ROPE_THETA_2 = 10000.0
Q_BLOCK = 128
N_EXPERTS = 32
TOP_K = 4
D_FF = 1024
SWIGLU_LIMIT = 7.0
SWIGLU_ALPHA = 1.702
EXPERT_BLOCK = 128
RMS_EPS = 1e-6
MAX_POS_OFFSET = 4096


def rmsnorm_2(x, g):
    xf = x.astype(jnp.float32)
    y = xf * lax.rsqrt(jnp.mean(xf * xf, axis=-1, keepdims=True) + RMS_EPS)
    return (y * g.astype(jnp.float32)).astype(x.dtype)

def rope_tables(positions):
    inv_freq = ROPE_THETA_2 ** (-jnp.arange(0, MLA_ROPE_DIM, 2, dtype=jnp.float32) / MLA_ROPE_DIM)
    ang = positions.astype(jnp.float32)[..., None] * inv_freq
    return jnp.cos(ang), jnp.sin(ang)

def apply_rope(x, cos, sin):
    xf = x.astype(jnp.float32)
    x1, x2 = jnp.split(xf, 2, axis=-1)
    return jnp.concatenate([x1 * cos - x2 * sin, x2 * cos + x1 * sin], axis=-1).astype(x.dtype)

def to_blocks(a):
    b, h, s, d = a.shape
    return jnp.moveaxis(a.reshape(b, h, s // Q_BLOCK, Q_BLOCK, d), 2, 0)

def from_blocks(o):
    n, b, h, qb, d = o.shape
    return jnp.moveaxis(o, 0, 2).reshape(b, h, n * qb, d).transpose(0, 2, 1, 3).reshape(b, n * qb, h * d)

def mixer_heads(q_nope, q_rope, k_nope, k_rope, v_mla, q_sb, k_sb, v_sb):
    seq = k_nope.shape[2]
    n_blk = seq // Q_BLOCK
    key_pos = jnp.arange(seq)
    mla_scale = (MLA_NOPE_DIM + MLA_ROPE_DIM) ** -0.5
    sb_scale = SB_HEAD_DIM ** -0.5

    def block(args):
        bi, qn, qr, qs = args
        q_pos = bi * Q_BLOCK + jnp.arange(Q_BLOCK)
        s = (jnp.einsum('bhqd,bhkd->bhqk', qn, k_nope, preferred_element_type=jnp.float32)
             + jnp.einsum('bhqr,bkr->bhqk', qr, k_rope, preferred_element_type=jnp.float32)) * mla_scale
        causal = key_pos[None, :] <= q_pos[:, None]
        w = jax.nn.softmax(jnp.where(causal, s, -jnp.inf), axis=-1)
        o_m = jnp.einsum('bhqk,bhkd->bhqd', w.astype(v_mla.dtype), v_mla)
        z = jnp.einsum('bhqd,bhkd->bhqk', qs, k_sb, preferred_element_type=jnp.float32) * sb_scale
        strict = key_pos[None, :] < q_pos[:, None]
        log_not = jnp.where(strict, jax.nn.log_sigmoid(-z), 0.0)
        after = lax.cumsum(log_not, axis=3, reverse=True) - log_not
        log_a = jnp.where(strict, jax.nn.log_sigmoid(z) + after, -jnp.inf)
        o_s = jnp.einsum('bhqk,bhkd->bhqd', jnp.exp(log_a).astype(v_sb.dtype), v_sb)
        return o_m, o_s

    o_m, o_s = lax.map(block, (jnp.arange(n_blk), to_blocks(q_nope), to_blocks(q_rope), to_blocks(q_sb)))
    return from_blocks(o_m), from_blocks(o_s)

def moe(u, w_router, b_router, w_gu, b_gu, w_dn, b_dn):
    b, s, d = u.shape
    t = b * s
    xt = u.reshape(t, d)
    logits = jnp.dot(xt, w_router, preferred_element_type=jnp.float32) + b_router.astype(jnp.float32)
    top_logit, top_e = lax.top_k(logits, TOP_K)
    gate = jax.nn.softmax(top_logit, axis=-1)
    n_pairs = t * TOP_K
    flat_e = top_e.reshape(-1)
    flat_tok = jnp.arange(n_pairs, dtype=jnp.int32) // TOP_K
    flat_g = gate.reshape(-1)
    order = jnp.argsort(flat_e)
    sorted_e = flat_e[order]
    counts = jnp.bincount(flat_e, length=N_EXPERTS)
    padded = (counts + EXPERT_BLOCK - 1) // EXPERT_BLOCK * EXPERT_BLOCK
    pad_end = jnp.cumsum(padded)
    pad_start = pad_end - padded
    start = jnp.cumsum(counts) - counts
    dest = pad_start[sorted_e] + jnp.arange(n_pairs) - start[sorted_e]
    n_blocks = -(-n_pairs // EXPERT_BLOCK) + N_EXPERTS
    n_rows = n_blocks * EXPERT_BLOCK
    row_tok = jnp.full((n_rows,), t, jnp.int32).at[dest].set(flat_tok[order])
    row_gate = jnp.zeros((n_rows,), jnp.float32).at[dest].set(flat_g[order])
    block_e = jnp.minimum(jnp.searchsorted(pad_end, jnp.arange(n_blocks) * EXPERT_BLOCK, side='right'),
                          N_EXPERTS - 1)
    x_pad = jnp.concatenate([xt, jnp.zeros((1, d), xt.dtype)], axis=0)
    xb = x_pad[row_tok].reshape(n_blocks, EXPERT_BLOCK, d)

    def expert_block(args):
        e, xs = args
        hh = jnp.dot(xs, w_gu[e]) + b_gu[e]
        glu, lin = jnp.split(hh, 2, axis=-1)
        glu = jnp.minimum(glu, SWIGLU_LIMIT)
        lin = jnp.clip(lin, -SWIGLU_LIMIT, SWIGLU_LIMIT)
        act = glu * jax.nn.sigmoid(SWIGLU_ALPHA * glu) * (lin + 1.0)
        return jnp.dot(act, w_dn[e]) + b_dn[e]

    yb = lax.map(expert_block, (block_e, xb))
    yr = yb.reshape(n_rows, d) * row_gate[:, None].astype(yb.dtype)
    y = jax.ops.segment_sum(yr, row_tok, num_segments=t + 1)[:t]
    return y.reshape(b, s, d)

def second_inputs(seed: int = 0) -> dict:
    key = jax.random.key(seed)
    ks = jax.random.split(key, 24)

    def nrm(k, shape, scale):
        return jax.random.normal(k, shape, jnp.float32) * scale

    def gain(k, shape):
        return 1.0 + 0.05 * jax.random.normal(k, shape, jnp.float32)

    offsets = jax.random.randint(ks[2], (BATCH, 1), 0, MAX_POS_OFFSET, dtype=jnp.int32)
    positions = offsets + jnp.arange(SEQ, dtype=jnp.int32)[None, :]
    return {
        'x': nrm(ks[0], (BATCH, SEQ, D_MODEL), 1.0),
        'p': nrm(ks[1], (DEPTH, BATCH, SEQ, PLE_DIM), 1.0),
        'positions': positions,
        'w_in': nrm(ks[3], (DEPTH, D_MODEL, IN_COLS_2), D_MODEL ** -0.5),
        'g_attn': gain(ks[4], (DEPTH, D_MODEL)),
        'g_cq': gain(ks[5], (DEPTH, Q_LORA_RANK)),
        'w_uq': nrm(ks[6], (DEPTH, Q_LORA_RANK, MLA_HEADS * (MLA_NOPE_DIM + MLA_ROPE_DIM)), Q_LORA_RANK ** -0.5),
        'g_ckv': gain(ks[7], (DEPTH, KV_LORA_RANK)),
        'w_ukv': nrm(ks[8], (DEPTH, KV_LORA_RANK, MLA_HEADS * (MLA_NOPE_DIM + MLA_V_DIM)), KV_LORA_RANK ** -0.5),
        'g_out_mla': gain(ks[9], (DEPTH, MLA_WIDTH)),
        'g_out_sb': gain(ks[10], (DEPTH, SB_WIDTH)),
        'w_o': nrm(ks[11], (DEPTH, MIX_WIDTH, D_MODEL), MIX_WIDTH ** -0.5),
        'g_moe': gain(ks[12], (DEPTH, D_MODEL)),
        'w_router': nrm(ks[13], (DEPTH, D_MODEL, N_EXPERTS), D_MODEL ** -0.5),
        'b_router': nrm(ks[14], (DEPTH, N_EXPERTS), 0.01),
        'w_gu': nrm(ks[15], (DEPTH, N_EXPERTS, D_MODEL, 2 * D_FF), D_MODEL ** -0.5),
        'b_gu': nrm(ks[16], (DEPTH, N_EXPERTS, 2 * D_FF), 0.01),
        'w_dn': nrm(ks[17], (DEPTH, N_EXPERTS, D_FF, D_MODEL), D_FF ** -0.5),
        'b_dn': nrm(ks[18], (DEPTH, N_EXPERTS, D_MODEL), 0.01),
        'g_ple': gain(ks[19], (DEPTH, D_MODEL)),
        'w_ple_gate': nrm(ks[20], (DEPTH, D_MODEL, D_MODEL), D_MODEL ** -0.5),
        'w_ple_proj': nrm(ks[21], (DEPTH, PLE_DIM, D_MODEL), PLE_DIM ** -0.5),
        'g_final': gain(ks[22], (D_MODEL,)),
    }

def second_block(x, p, positions, w_in, g_attn, g_cq, w_uq, g_ckv, w_ukv, g_out_mla, g_out_sb, w_o,
              g_moe, w_router, b_router, w_gu, b_gu, w_dn, b_dn, g_ple, w_ple_gate, w_ple_proj, g_final):
    b, s, _ = x.shape
    cos, sin = rope_tables(positions)

    def heads_first(a):
        return jnp.swapaxes(a, 1, 2)

    h = x
    for i in range(DEPTH):
        u = rmsnorm_2(h, g_attn[i])
        c_q, c_kv, k_r, q_s, k_s, v_s = jnp.split(u @ w_in[i], IN_SPLITS_2, axis=-1)
        q = (rmsnorm_2(c_q, g_cq[i]) @ w_uq[i]).reshape(b, s, MLA_HEADS, MLA_NOPE_DIM + MLA_ROPE_DIM)
        kv = (rmsnorm_2(c_kv, g_ckv[i]) @ w_ukv[i]).reshape(b, s, MLA_HEADS, MLA_NOPE_DIM + MLA_V_DIM)
        q_nope = q[..., :MLA_NOPE_DIM]
        q_rope = apply_rope(q[..., MLA_NOPE_DIM:], cos[:, :, None, :], sin[:, :, None, :])
        k_nope = kv[..., :MLA_NOPE_DIM]
        v_m = kv[..., MLA_NOPE_DIM:]
        k_rope = apply_rope(k_r, cos, sin)
        sb_shape = (b, s, SB_HEADS, SB_HEAD_DIM)
        o_m, o_s = mixer_heads(heads_first(q_nope), heads_first(q_rope), heads_first(k_nope), k_rope,
                               heads_first(v_m), heads_first(q_s.reshape(sb_shape)),
                               heads_first(k_s.reshape(sb_shape)), heads_first(v_s.reshape(sb_shape)))
        mixed = jnp.concatenate([rmsnorm_2(o_m, g_out_mla[i]), rmsnorm_2(o_s, g_out_sb[i])], axis=-1)
        h = h + mixed @ w_o[i]
        h = h + moe(rmsnorm_2(h, g_moe[i]), w_router[i], b_router[i], w_gu[i], b_gu[i], w_dn[i], b_dn[i])
        u = rmsnorm_2(h, g_ple[i])
        h = h + jax.nn.sigmoid(u @ w_ple_gate[i]) * (p[i] @ w_ple_proj[i])
    return rmsnorm_2(h, g_final)


def setup_inputs(seed=0):
    out = dict(first_inputs(seed))
    for name, value in second_inputs(seed + 1).items():
        if name != "x":
            out[name + "_2"] = value
    return out


def reference(
    x, pre_norm_w, w_in, conv_w, a_log, dt_bias, gdn_norm_w, w_branch_a, w_branch_b, w_out,
    post_norm_w, p_2, positions_2, w_in_2, g_attn_2, g_cq_2, w_uq_2, g_ckv_2, w_ukv_2,
    g_out_mla_2, g_out_sb_2, w_o_2, g_moe_2, w_router_2, b_router_2, w_gu_2, b_gu_2, w_dn_2,
    b_dn_2, g_ple_2, w_ple_gate_2, w_ple_proj_2, g_final_2,
):
    x = first_block(
        x, pre_norm_w, w_in, conv_w, a_log, dt_bias, gdn_norm_w, w_branch_a, w_branch_b, w_out,
        post_norm_w,
    )
    return second_block(
        x, p_2, positions_2, w_in_2, g_attn_2, g_cq_2, w_uq_2, g_ckv_2, w_ukv_2, g_out_mla_2,
        g_out_sb_2, w_o_2, g_moe_2, w_router_2, b_router_2, w_gu_2, b_gu_2, w_dn_2, b_dn_2,
        g_ple_2, w_ple_gate_2, w_ple_proj_2, g_final_2,
    )


_drawn_inputs = setup_inputs


def setup_inputs(seed=0):
    import zlib

    import numpy as np

    out = dict(_drawn_inputs(seed))
    spreads = {}
    factors = {'b_router_2': 2.797, 'b_gu_2': 8.0, 'b_dn_2': 8.0, 'g_ple_2': 22.497}
    for name, (base, spread) in spreads.items():
        noise = np.random.default_rng([zlib.crc32(name.encode()), seed]).standard_normal(out[name].shape)
        drawn = base * np.exp(spread * noise) if base else spread * noise
        out[name] = __import__('jax').numpy.asarray(drawn.astype(out[name].dtype))
    for name, factor in factors.items():
        out[name] = (out[name] * factor).astype(out[name].dtype)
    return out
```

```python
from contextlib import ExitStack

import numpy as np

import concourse.bass as bass
from concourse import mybir

P = 128
T = 256
NT = T // P
D = 1024
KD = D // P
HEADS = 8
CHUNK = 64
CONV = 4
BANK = 512
NEXP = 32
CAP = 64
LAST_STAGE = 27
SMALL_LOADS = 16
MAXROUND = T // CAP
MAXOVER = 1024 // CAP
QR, KVR = 384, 256
TWO_PI = 2.0 * np.pi
EPS = 1e-6
NEG = -1e30

F32 = mybir.dt.float32
BF16 = mybir.dt.bfloat16
I32 = mybir.dt.int32
U32 = mybir.dt.uint32
ALU = mybir.AluOpType
ACT = mybir.ActivationFunctionType
AX = mybir.AxisListType.X

PI_A, PI_B = 6.28125, 0.00193023681640625
PI_C = TWO_PI - PI_A - PI_B
PI_IN = 3.1415925
ROUND = 1.5 * 2.0 ** 23

LEVELS = (1, 2, 4, 8, 16, 32)


def constants():
    r, c = np.arange(P)[:, None], np.arange(P)[None, :]
    same = (r // CHUNK) == (c // CHUNK)
    causal = np.where(c <= r, 0.0, NEG)
    parts = {
        "ident": r == c,
        "ones": np.ones((P, P)),
        "causal": np.concatenate([causal, np.zeros((P, P)), causal], 1),
        "strict": np.concatenate([r < c, np.ones((P, P)), r < c], 1),
        "upto": same & (r <= c),
        "chunk": same,
        "later": r > c,
        "earlier": r < c,
    }
    for s in LEVELS:
        parts[f"level{s}"] = (c // s % 2 == 1) & (r // s == c // s - 1)
    rot = np.zeros((P, 32))
    for base in (0, 64):
        for i in range(16):
            rot[base + 16 + i, i] = -1.0
            rot[base + i, 16 + i] = 1.0
    parts["rot"] = rot
    half = np.arange(P) % 16
    inv1 = np.power(np.float32(500000.0), -half.astype(np.float32) * np.float32(2.0 / 32)).astype(np.float32)
    ang = np.arange(T, dtype=np.float32)[None, :] * inv1[:, None]
    parts["cos"], parts["sin"] = np.cos(ang), np.sin(ang)
    parts["freq"] = np.power(np.float32(10000.0), -(2 * half).astype(np.float32) / np.float32(32))[:, None]
    parts["slots"] = np.broadcast_to(np.arange(CAP * (MAXROUND + 1)), (P, CAP * (MAXROUND + 1)))
    parts["row"] = np.arange(P)[:, None]
    parts["small"] = np.broadcast_to([EPS, P * EPS, 1.0, CAP, 2.0 * CAP, 3.0 * CAP], (P, 6))
    parts["codes"] = np.concatenate([np.arange(P)[:, None] + NEXP * k for k in (1, 2, 3)], 1)
    parts["bsel"] = (r % NEXP == c[:, :NEXP]) & (r < 3 * NEXP)
    at, cols = 0, {}
    for name, a in parts.items():
        cols[name] = (at, at + a.shape[1])
        at += a.shape[1]
    return np.concatenate([np.asarray(a, np.float32) for a in parts.values()], 1), cols


class Steps:

    def __init__(self, eng, sem):
        self.eng, self.sem, self.n = eng, sem, 0

    def __call__(self, ins):
        self.n += 1
        ins.then_inc(self.sem, 1)
        self.eng.wait_ge(self.sem, self.n)


class Stage:

    def __init__(self, eng, sem):
        self.eng, self.sem, self.n = eng, sem, 0

    def end(self):
        self.n += 1
        self.eng.drain().then_inc(self.sem, 1)
        self.eng.wait_ge(self.sem, 4 * self.n)


def hybrid_two_block_kernel(nc, I, out):
    const_np, CC = constants()
    with ExitStack() as ctx:
        def sb(name, shape, dt=F32):
            return ctx.enter_context(nc.sbuf_tensor(name, shape, dt))

        class Sems(dict):
            def __missing__(self, name):
                self[name] = ctx.enter_context(nc.semaphore(name))
                return self[name]

        S = Sems()

        ring = sb("ring", [P, 6, 4096])
        fm = sb("fm", [P, 24, T])
        va = sb("va", [P, NT, D])
        zb = sb("zb", [P, NT, D])
        oat = sb("oat", [P, HEADS, T])
        xs = sb("xs", [P, NT, D])
        ht = sb("ht", [P, KD, T])
        extra = sb("extra", [P, 3, 2048])
        cst = sb("cst", [P, const_np.shape[1]])
        cw = sb("cw", [P, 96])
        wbd = sb("wbd", [P, KD, 16])
        cols = sb("cols", [P, 64])
        hsc = sb("hsc", [P, 16])
        ssq = sb("ssq", [P, 32])
        rsd = sb("rsd", [P, 32])
        nmx = sb("nmx", [P, HEADS, 2])
        sums = sb("sums", [P, HEADS, 2])
        rsum = sb("rsum", [P, HEADS, 2])
        bd = sb("bd", [P, 6, NT * HEADS])
        ps = ctx.enter_context(nc.psum_tensor("ps", [P, 8, BANK], F32))

        def con(name, rows=slice(0, P)):
            a, b = CC[name]
            return cst[rows, a:b]

        def con_at(name, first, n):
            return cst[:, bass.ds(first + CC[name][0], n)]

        def arena(i):
            return ring[:, 2 + i // 2, 2048 * (i % 2):2048 * (i % 2) + 2048]

        ident = con("ident")
        gates = fm[:, 0:16, :].rearrange("p a b -> p (a b)").rearrange("p (g t d) -> p g t d", g=2, t=NT)
        w_pre, w_gdn, g_attn, g_cq, g_ckv = (cols[:, a:b] for a, b in ((0, 8), (8, 9), (10, 18), (18, 21), (21, 23)))
        g_mix, g_moe, g_ple = (cols[:, a:b] for a, b in ((24, 32), (32, 40), (40, 48)))
        brow = sb("brow", [P, NEXP])
        posi = sb("posi", [P, T], I32)

        w_in = I["w_in"][0].rearrange("(p k) n -> p k n", k=KD)

        def pk_rows(name, k):
            return I[name][0].rearrange("(p k) n -> p k n", k=k)

        def head_rows(name):
            return I[name][0].rearrange("(h p) n -> p h n", p=P)

        plan = []

        def stream(src, c0, units, n=BANK, k=KD):
            g = len(plan)
            dst = ring[:, g % 2, 0:k * n].rearrange("p (k n) -> p k n", k=k)
            done = units + (plan[-1][2] if plan else 0)
            plan.append((dst, src[:, :, c0:c0 + n], done))

        for c in (0, 1, 2, 3, 6, 7):
            stream(w_in, BANK * c, 4)
        for c in (4, 5):
            stream(w_in, BANK * c, 2)
        for c in range(8, 14):
            stream(w_in, BANK * c, 4)
        for c in (14, 15):
            stream(w_in, BANK * c, 2)
        for c in range(4):
            stream(w_in, 16 * BANK + 16 + BANK * c, 2)
        for name in ("w_branch_a", "w_branch_b"):
            for c in (0, 1):
                stream(head_rows(name), BANK * c, 2)
        for c in (0, 1):
            stream(pk_rows("w_out", KD), BANK * c, 2)
        w_in2 = pk_rows("w_in_2", KD)
        stream(w_in2, 0, 2, QR)
        stream(w_in2, QR, 3, KVR + 32)
        stream(w_in2, QR + KVR + 32, 4)
        stream(w_in2, QR + KVR + 32 + BANK, 4)
        stream(w_in2, QR + KVR + 32 + 2 * BANK, 2)
        stream(pk_rows("w_uq_2", QR // P), 0, 8, 96 * HEADS, QR // P)
        stream(pk_rows("w_ukv_2", KVR // P), 0, 10, P * HEADS, KVR // P)
        for c in (0, 1):
            stream(pk_rows("w_o_2", KD), BANK * c, 2)

        before_experts = len(plan)
        for c in (0, 1):
            stream(pk_rows("w_ple_gate_2", KD), BANK * c, 2)
        stream(pk_rows("w_ple_proj_2", 2), 0, 4, D, 2)

        block = ctx.enter_context(nc.Block())

        def bank(b, lo=0, hi=BANK):
            return ps[:, b, lo:hi]

        class Products:

            def __init__(self, pe):
                self.pe, self.g, self.u = pe, 0, 0

            def chunk(self, units, k, n=BANK):
                w = ring[:, self.g % 2, 0:k * n].rearrange("p (k n) -> p k n", k=k)
                self.pe.wait_ge(S[f"chunk_in{self.g % 2}"], 16 * (self.g // 2 + 1))
                for r0, rows, width, lhs, rhs in units:
                    if self.u >= 8:
                        self.pe.wait_ge(S[f"moved{self.u % 2}"], (self.u - 8) // 2 + 1)
                    for j in range(k):
                        last = self.pe.matmul(ps[r0:r0 + rows, self.u % 8, 0:width], lhs(w, j), rhs(w, j), start=(j == 0), stop=(j == k - 1))
                    last.then_inc(S["unit"], 1)
                    self.u += 1
                self.g += 1

            def fm_units(self, act_t, tiles=4, m=P, at=0, step=None, r0=0):
                return [(r0, m, T, lambda w, j, f=f: w[:, j, at + (step or m) * f:at + (step or m) * f + m],
                         lambda w, j: act_t[:, j, :]) for f in range(tiles)]

            def tm_units(self, act_t, width=BANK, cols=lambda w, j: w[:, j, :]):
                return [(0, P, width, lambda w, j, t=t: act_t[:, j, P * t:P * t + P], cols) for t in range(NT)]

            def feature_major(self, act_t, tiles=4):
                self.chunk(self.fm_units(act_t, tiles), KD)

            def token_major(self, act_t, n=BANK):
                self.chunk(self.tm_units(act_t, n), KD, n)

        class Moves:

            def __init__(self, eng, parity):
                self.eng, self.parity, self.u = eng, parity, 0

            def take(self, n, move, whole=False):
                for i in range(n):
                    if whole or self.u % 2 == self.parity:
                        self.eng.wait_ge(S["unit"], self.u + 1)
                        move(i, self.u % 8).then_inc(S[f"moved{self.u % 2}"], 1)
                    self.u += 1

            def skip(self, n):
                self.u += n

        def copy_out(eng, dst, src):
            if eng is nc.scalar:
                return nc.scalar.activation(dst, src, ACT.Copy)
            return nc.vector.tensor_copy(dst, src)

        def as_token_major(buf):
            return buf.rearrange("p a b -> p (a b)").rearrange("p (t d) -> p t d", t=NT)

        oat_tm = as_token_major(oat[:, :, :])

        norm_calls = {"act": 0, "dve": 0, "pe": 0}

        def norm_act(act, src, segs, junk, t0=0):
            n = norm_calls["act"]; norm_calls["act"] += 1
            for t in range(NT):
                for s, (c0, w) in enumerate(segs):
                    last = nc.scalar.activation(junk[:, 0:w], src[:, t, c0:c0 + w], ACT.Square,
                                                accum_out=ssq[:, t * len(segs) + s:t * len(segs) + s + 1])
                    act_step(last)
            m = NT * len(segs)
            w = segs[0][1]
            nc.scalar.activation(rsd[:, 0:m], ssq[:, 0:m], ACT.Sqrt, scale=1.0 / w,
                                 bias=con("small")[:, 0:1]).then_inc(S["rms_root"], 1)

        def norm_dve(dve, src, segs, dst):
            n = norm_calls["dve"]; norm_calls["dve"] += 1
            m = NT * len(segs)
            dve.wait_ge(S["rms_root"], n + 1)
            dve_step(nc.vector.reciprocal(ssq[:, 0:m], rsd[:, 0:m]))
            if dst is None:
                return
            for t in range(NT):
                for s, (c0, w) in enumerate(segs):
                    i = t * len(segs) + s
                    last = nc.vector.tensor_scalar(dst[:, t, c0:c0 + w], src[:, t, c0:c0 + w], ssq[:, i:i + 1], None, ALU.mult)
            last.then_inc(S["normed"], 1)

        turn_calls = {"pe": 0, "dve": 0}

        def turn_pe(pe, src, K, b0=0):
            for k in range(K):
                for t in range(NT):
                    last = pe.transpose(ps[:, b0 + k // 2, (k % 2) * T + P * t:(k % 2) * T + P * t + P],
                                        src[:, t, k:k + K * (P - 1) + 1:K], ident)
            last.then_inc(S["turned"], 1)
            turn_calls["pe"] += 1

        def turn_dve(dve, dst, K, w_col=None, b0=0, done=None):
            turn_calls["dve"] += 1
            dve.wait_ge(S["turned"], turn_calls["dve"])
            for k in range(K):
                src = ps[:, b0 + k // 2, (k % 2) * T:(k % 2) * T + T]
                if w_col is None:
                    last = nc.vector.tensor_copy(dst[:, k, :], src)
                else:
                    last = nc.vector.tensor_scalar(dst[:, k, :], src, w_col[:, k:k + 1], None, ALU.mult)
            if done:
                last.then_inc(S[done], 1)

        dve_steps, act_steps = [None], [None]

        def dve_step(ins):
            dve_steps[0](ins)

        def act_step(ins):
            act_steps[0](ins)

        sc_buf, pt_buf = [extra[:, 0, 384 * i:384 * i + 384] for i in range(2)], [extra[:, 0, 768 + 384 * i:1152 + 384 * i] for i in range(2)]

        def attention_pe(pe, h0, q, k, out_product):
            for i in range(HEADS + 2):
                if i < HEADS:
                    if h0 + i >= 2:
                        pe.wait_ge(S["scores_read"], h0 + i - 1)
                    b = ps[:, i % 2, :]
                    pe.matmul(b[:, 0:P], q(i)[:, 0:P], k(i)[:, 0:P], start=True, stop=True)
                    pe.matmul(b[:, P:3 * P], q(i)[:, P:T], k(i)[:, 0:T], start=True, stop=True).then_inc(S["scores"], 1)
                if 1 <= i <= HEADS:
                    h = i - 1
                    pe.wait_ge(S["weights"], h0 + h + 1)
                    if h0 + h >= 2:
                        pe.wait_ge(S["weights_t"], h0 + h - 1)
                    for j in range(3):
                        last = pe.transpose(ps[:, 2 + h % 2, P * j:P * j + P], sc_buf[h % 2][:, P * j:P * j + P], ident)
                    last.then_inc(S["weights_turned"], 1)
                if i >= 2:
                    h = i - 2
                    pe.wait_ge(S["weights_t"], h0 + h + 1)
                    out_product(h, pt_buf[h % 2]).then_inc(S["head_out"], 1)

        def attention_act(act, h0):
            for i in range(HEADS + 1):
                if i < HEADS:
                    act.wait_ge(S["maxima"], h0 + i + 1)
                    for t, (a, b) in enumerate(((0, P), (P, 3 * P))):
                        last = nc.scalar.activation(sc_buf[i % 2][:, a:b], sc_buf[i % 2][:, a:b], ACT.Exp,
                                                    bias=nmx[:, i, t:t + 1], accum_out=sums[:, i, t:t + 1])
                    last.then_inc(S["exps"], 1)
                if i >= 1:
                    h = i - 1
                    act.wait_ge(S["weights_turned"], h0 + h + 1)
                    if h0 + h >= 2:
                        act.wait_ge(S["head_out"], h0 + h - 1)
                    nc.scalar.activation(pt_buf[h % 2], ps[:, 2 + h % 2, 0:3 * P], ACT.Copy).then_inc(S["weights_t"], 1)

        def attention_dve(dve, h0, scale, take_out):
            for i in range(HEADS + 2):
                if i < HEADS:
                    dve.wait_ge(S["scores"], h0 + i + 1)
                    if h0 + i >= 2:
                        dve.wait_ge(S["weights_turned"], h0 + i - 1)
                    nc.vector.scalar_tensor_tensor(out=sc_buf[i % 2], in0=ps[:, i % 2, 0:3 * P], scalar=scale,
                                                   in1=con("causal"), op0=ALU.mult, op1=ALU.add).then_inc(S["scores_read"], 1)
                    dve.wait_ge(S["scores_read"], h0 + i + 1)
                    dve_step(nc.vector.tensor_reduce(nmx[:, i, 0:1], sc_buf[i % 2][:, 0:P], AX, ALU.max, negate=True))
                    nc.vector.tensor_reduce(nmx[:, i, 1:2], sc_buf[i % 2][:, P:3 * P], AX, ALU.max, negate=True).then_inc(S["maxima"], 1)
                if 1 <= i <= HEADS:
                    h = i - 1
                    dve.wait_ge(S["exps"], h0 + h + 1)
                    dve_step(nc.vector.reciprocal(rsum[:, h, :], sums[:, h, :]))
                    b = sc_buf[h % 2]
                    nc.vector.tensor_scalar(b[:, 0:P], b[:, 0:P], rsum[:, h, 0:1], None, ALU.mult)
                    nc.vector.tensor_scalar(b[:, P:3 * P], b[:, P:3 * P], rsum[:, h, 1:2], None, ALU.mult).then_inc(S["weights"], 1)
                if i >= 2:
                    take_out(i - 2)

        bt, gd, Gc, Gd, eG, bG = (bd[:, i, :] for i in range(6))
        gl = sb("gl", [P, 4, HEADS])
        SYS = NT * HEADS

        def systems(buf):
            return buf.rearrange("p (s i) -> p s i", s=SYS)

        kbg, kdec, vbt = (systems(extra[:, i, :]) for i in range(3))
        egr, dk, mt, qkt = (systems(arena(i)) for i in range(4))
        xi, xt, yy, bb = (systems(arena(i)) for i in range(4, 8))
        nwt, uu = yy, bb
        vnew = arena(2)[:, 0:D].rearrange("p (h i) -> p h i", h=HEADS)
        state = arena(2)[:, D:2 * D].rearrange("p (h i) -> p h i", h=HEADS)
        oo = xi
        obt = arena(5).rearrange("p (h n) -> p h n", h=HEADS)

        def four(b):
            return ps[:, b, :].rearrange("p (s i) -> p s i", s=4)

        def over4(col, g):
            return col[:, 4 * g:4 * g + 4].unsqueeze(2).to_broadcast([P, 4, P])

        def wide(buf):
            return buf.rearrange("p (c n) -> p c n", c=HEADS)

        def seen_by(t, h):
            return lambda base: fm[:, base + h, P * t:P * t + P]

        def gdn_pool(pool, stage):
            stage.end()
            pool.wait_ge(S["decay"], 1)
            nc.gpsimd.tensor_tensor(dk, dk, con("upto").unsqueeze(1).to_broadcast([P, SYS, P]), ALU.mult).then_inc(S["decay_masked"], 1)
            pool.wait_ge(S["glast"], 1)
            nc.gpsimd.tensor_tensor(egr.rearrange("p (t h) i -> p h t i", t=NT), egr.rearrange("p (t h) i -> p h t i", t=NT),
                                    fm[:, 0:8, :].rearrange("p h (t i) -> p h t i", t=NT), ALU.mult)
            stage.end()
            for n in range(len(LEVELS) * 4):
                l, g = n // 4, n % 4
                if n >= 8:
                    pool.wait_ge(S["y_ps"], n - 7)
                elif n >= 4:
                    pool.wait_ge(S["x_done"], n - 3)
                nc.gpsimd.tensor_tensor(bb[:, 4 * g:4 * g + 4, :], mt[:, 4 * g:4 * g + 4, :],
                                        con(f"level{LEVELS[l]}").unsqueeze(1).to_broadcast([P, 4, P]), ALU.mult).then_inc(S["b_ready"], 1)
            stage.end()
            nc.gpsimd.memset(arena(2), 0.0).then_inc(S["zeroed"], 1)
            stage.end()
            stage.end()

        def gdn_pe(pe, stage):
            for G in range(2):
                pe.wait_ge(S["squares"], G + 1)
                for m in range(4):
                    last = pe.matmul(ps[:, 4 * G + m, :], con("ones"), wide(arena(3 + G))[:, 2 * m:2 * m + 2, :], start=True, stop=True)
                last.then_inc(S["sq_sums"], 1)
            stage.end()
            for t in range(NT):
                cs = slice(HEADS * t, HEADS * t + HEADS)
                pe.matmul(ps[:, 0, HEADS * t:HEADS * t + HEADS], con("upto"), gd[:, cs], start=True, stop=True)
                last = pe.matmul(ps[:, 0, 16 + HEADS * t:16 + HEADS * t + HEADS], con("chunk"), gd[:, cs], start=True, stop=True)
            last.then_inc(S["g_sums"], 1)
            for s in range(SYS):
                t, h = s // HEADS, s % HEADS
                last = pe.transpose(four(4 + s // 4)[:, s % 4, :], seen_by(t, h)(8), ident)
                if s % 4 == 3:
                    last.then_inc(S["k_turned"], 1)
            pe.wait_ge(S["g_read"], 1)
            for s in range(SYS):
                t, h = s // HEADS, s % HEADS
                last = pe.transpose(four(s // 4)[:, s % 4, :], seen_by(t, h)(16), ident)
                if s % 4 == 3:
                    last.then_inc(S["v_turned"], 1)
            for s in range(SYS):
                if s % 4 == 0:
                    pe.wait_ge(S["k_read"], s // 4 + 1)
                last = pe.matmul(four(4 + s // 4)[:, s % 4, :], gd[:, s:s + 1].to_broadcast([P, P]), con("upto"), start=True, stop=True)
                if s % 4 == 3:
                    last.then_inc(S["g_rows"], 1)
            for s in range(SYS):
                if s % 4 == 0:
                    pe.wait_ge(S["v_read"], s // 4 + 1)
                last = pe.matmul(four(s // 4)[:, s % 4, :], bt[:, s:s + 1].to_broadcast([P, P]), ident, start=True, stop=True)
            last.then_inc(S["beta_rows"], 1)
            for s in range(SYS):
                t, h = s // HEADS, s % HEADS
                if s % 4 == 0:
                    pe.wait_ge(S["rows_read_act"], s // 4 + 1)
                    pe.wait_ge(S["rows_read_dve"], s // 4 + 1)
                last = pe.matmul(four(4 + s // 4)[:, s % 4, :], seen_by(t, h)(8), seen_by(t, h)(8), start=True, stop=True)
                if s % 4 == 3:
                    last.then_inc(S["kk"], 1)
            for s in range(SYS):
                t, h = s // HEADS, s % HEADS
                if s % 4 == 0:
                    pe.wait_ge(S["kk_read"], s // 4 + 1)
                last = pe.matmul(four(4 + s // 4)[:, s % 4, :], seen_by(t, h)(8), seen_by(t, h)(0), start=True, stop=True)
                if s % 4 == 3:
                    last.then_inc(S["qk"], 1)
            stage.end()
            for l in range(len(LEVELS)):
                for i in range(5):
                    if i < 4 and l > 0:
                        g = i
                        pe.wait_ge(S["b_ready"], 4 * l + g + 1)
                        pe.wait_ge(S["x_done"], 4 * (l - 1) + g + 1)
                        for q in range(4):
                            last = pe.matmul(four(g)[:, q, :], bb[:, 4 * g + q, :], xi[:, 4 * g + q, :], start=True, stop=True)
                        last.then_inc(S["y_ps"], 1)
                    if i >= 1:
                        g = i - 1
                        n = 4 * l + g
                        if n >= 2:
                            pe.wait_ge(S["x_done"], n - 1)
                        if l == 0:
                            pe.wait_ge(S["b_ready"], g + 1)
                            for q in range(4):
                                last = pe.matmul(four(4 + g % 2)[:, q, :], bb[:, 4 * g + q, :], ident, start=True, stop=True)
                        else:
                            pe.wait_ge(S["y_copied"], n - 3)
                            for q in range(4):
                                sys = 4 * g + q
                                if l < len(LEVELS) - 1:
                                    pe.matmul(four(4 + g % 2)[:, q, :], xt[:, sys, :], yy[:, sys, :], start=True, stop=True)
                                last = pe.matmul(four(6 + g % 2)[:, q, :], yy[:, sys, :], xt[:, sys, :], start=True, stop=True)
                        last.then_inc(S["z_ps"], 1)
            stage.end()
            for s in range(SYS):
                last = pe.matmul(four(s // 4)[:, s % 4, :], kbg[:, s, :], xt[:, s, :], start=True, stop=True)
                if s % 4 == 3:
                    last.then_inc(S["w_ps"], 1)
            for s in range(SYS):
                last = pe.matmul(four(4 + s // 4)[:, s % 4, :], xt[:, s, :], vbt[:, s, :], start=True, stop=True)
                if s % 4 == 3:
                    last.then_inc(S["u_ps"], 1)
            pe.wait_ge(S["w_moved"], 4)
            pe.wait_ge(S["u_moved"], 4)
            pe.wait_ge(S["zeroed"], 1)
            for c in range(4):
                t, r = c // 2, CHUNK * (c % 2)
                rows = slice(r, r + CHUNK)

                def at(b, h):
                    return ps[rows, b + h // 4, P * (h % 4):P * (h % 4) + P]

                if c:
                    pe.wait_ge(S["state"], c)
                for h in range(HEADS):
                    last = pe.matmul(at(0, h), nwt[:, HEADS * t + h, rows], state[:, h, :], start=True, stop=True)
                last.then_inc(S["ws"], 1)
                if c:
                    pe.wait_ge(S["o_moved"], c)
                for h in range(HEADS):
                    last = pe.matmul(at(2, h), egr[:, HEADS * t + h, rows], state[:, h, :], start=(h % 4 == 0), stop=False, skip_group_check=True)
                last.then_inc(S["state_read"], 1)
                pe.wait_ge(S["vnew"], c + 1)
                for h in range(HEADS):
                    last = pe.matmul(ps[:, 4 + h // 4, P * (h % 4):P * (h % 4) + P], kdec[rows, HEADS * t + h, :], vnew[rows, h, :], start=True, stop=True)
                last.then_inc(S["kv"], 1)
                for h in range(HEADS):
                    last = pe.matmul(at(2, h), qkt[:, HEADS * t + h, rows], vnew[:, h, :], start=False, stop=True, skip_group_check=True)
                last.then_inc(S["o_ps"], 1)
            stage.end()
            pe.wait_ge(S["o_gated"], 1)
            for s in range(SYS):
                t, h = s // HEADS, s % HEADS
                last = pe.transpose(ps[:, h // 2, T * (h % 2) + P * t:T * (h % 2) + P * t + P], oo[:, s, :], ident)
            last.then_inc(S["o_turned"], 1)
            stage.end()

        def gdn_act(act, stage):
            act.wait_ge(S["abs_z"], 1)
            act_step(nc.scalar.activation(Gd, Gd, ACT.Exp, scale=-1.0))
            nc.scalar.activation(hsc[:, 8:16], hsc[:, 8:16], ACT.Exp)
            nc.scalar.activation(Gd, Gd, ACT.Ln, bias=con("small")[:, 2:3]).then_inc(S["log_part"], 1)
            for G in range(3):
                for c in range(HEADS):
                    last = nc.scalar.activation(wide(arena(G))[:, c, :], fm[:, 8 * G + c, :], ACT.Copy, scale=cw[:, 72 + 8 * G + c:73 + 8 * G + c])
                last.then_inc(S["tap3"], 1)
            for G in range(3):
                act.wait_ge(S["conv"], G + 1)
                last = nc.scalar.activation(fm[:, 8 * G:8 * G + 8, :], wide(arena(G)), ACT.Silu)
                act_step(last)
            nc.scalar.activation(bt, bt, ACT.Sigmoid)
            for G in range(2):
                nc.scalar.activation(wide(arena(3 + G)), fm[:, 8 * G:8 * G + 8, :], ACT.Square).then_inc(S["squares"], 1)
            for G in range(2):
                act.wait_ge(S["sq_sums"], G + 1)
                nc.scalar.activation(arena(3 + G), ps[:, 4 * G:4 * G + 4, :].rearrange("p b n -> p (b n)"), ACT.Sqrt,
                                     scale=(float(P), 1.0)[G], bias=con("small")[:, 1 - G:2 - G]).then_inc(S["roots"], 1)
            stage.end()
            act.wait_ge(S["g_read"], 1)
            nc.scalar.activation(eG, Gc, ACT.Exp)
            nc.scalar.activation(Gd, Gd, ACT.Exp).then_inc(S["g_exp"], 1)
            for g in range(4):
                act.wait_ge(S["rows_read_dve"], g + 1)
                nc.scalar.activation(egr[:, 4 * g:4 * g + 4, :], four(4 + g), ACT.Exp).then_inc(S["rows_read_act"], 1)
            act.wait_ge(S["diffs"], 1)
            nc.scalar.activation(dk, dk, ACT.Exp).then_inc(S["decay"], 1)
            stage.end()
            for n in range(4 * (len(LEVELS) - 1)):
                g = n % 4
                act.wait_ge(S["y_ps"], n + 1)
                nc.scalar.activation(yy[:, 4 * g:4 * g + 4, :], four(g), ACT.Copy).then_inc(S["y_copied"], 1)
            stage.end()
            for g in range(4):
                act.wait_ge(S["w_ps"], g + 1)
                nc.scalar.activation(nwt[:, 4 * g:4 * g + 4, :], four(g), ACT.Copy, scale=-1.0).then_inc(S["w_moved"], 1)
            for c in range(4):
                t, r = c // 2, CHUNK * (c % 2)
                act.wait_ge(S["o_ps"], c + 1)
                nc.scalar.activation(oo[r:r + CHUNK, HEADS * t:HEADS * t + HEADS, :],
                                     ps[r:r + CHUNK, 2:4, :].rearrange("p b (h i) -> p (b h) i", h=4), ACT.Copy).then_inc(S["o_moved"], 1)
            stage.end()
            nc.scalar.activation(egr, oo, ACT.Square).then_inc(S["o_sq"], 1)
            nc.scalar.activation(zb[:, :, :], zb[:, :, :], ACT.Silu).then_inc(S["silu_zb"], 1)
            act.wait_ge(S["o_sums"], 1)
            nc.scalar.activation(rsd[:, 0:SYS], ssq[:, 0:SYS], ACT.Sqrt, scale=1.0 / P, bias=con("small")[:, 0:1]).then_inc(S["o_root"], 1)
            stage.end()

        def gdn_dve(dve, stage):
            heads2 = [P, NT, HEADS]

            def by_head(a):
                return a.unsqueeze(1).to_broadcast(heads2)

            def th(a):
                return a.rearrange("p (t h) -> p t h", t=NT)

            dve_step(nc.vector.tensor_tensor(th(Gc), th(gd), by_head(hsc[:, 0:8]), ALU.add))
            nc.vector.scalar_tensor_tensor(out=Gd, in0=Gc, scalar=-1.0, in1=Gc, op0=ALU.mult, op1=ALU.max).then_inc(S["abs_z"], 1)
            dve_step(nc.vector.tensor_scalar(Gc, Gc, 0.0, None, ALU.max))
            dve.wait_ge(S["log_part"], 1)
            dve_step(nc.vector.tensor_tensor(Gc, Gc, Gd, ALU.add))
            nc.vector.scalar_tensor_tensor(out=th(gd), in0=th(Gc), scalar=-1.0, in1=by_head(hsc[:, 8:16]), op0=ALU.mult, op1=ALU.mult)
            for G in range(3):
                dve.wait_ge(S["tap3"], G + 1)
                acc = wide(arena(G))
                for back in (1, 2, 3):
                    for c in range(HEADS):
                        k = 24 * (3 - back) + 8 * G + c
                        last = nc.vector.scalar_tensor_tensor(out=acc[:, c, back:T], in0=fm[:, 8 * G + c, 0:T - back], scalar=cw[:, k:k + 1],
                                                              in1=acc[:, c, back:T], op0=ALU.mult, op1=ALU.add)
                    if back < 3:
                        dve_step(last)
                last.then_inc(S["conv"], 1)
            for G in range(2):
                dve.wait_ge(S["roots"], G + 1)
                dve_step(nc.vector.reciprocal(arena(3 + G), arena(3 + G)))
                nc.vector.tensor_tensor(fm[:, 8 * G:8 * G + 8, :], fm[:, 8 * G:8 * G + 8, :], wide(arena(3 + G)), ALU.mult)
            stage.end()
            dve.wait_ge(S["g_sums"], 1)
            dve_step(nc.vector.tensor_copy(Gc, ps[:, 0, 0:16]))
            nc.vector.tensor_tensor(Gd, ps[:, 0, 16:32], Gc, ALU.subtract).then_inc(S["g_read"], 1)
            dve.wait_ge(S["g_exp"], 1)
            dve_step(nc.vector.tensor_tensor(bG, bt, eG, ALU.mult))
            for g in range(4):
                dve.wait_ge(S["k_turned"], g + 1)
                nc.vector.tensor_tensor(kbg[:, 4 * g:4 * g + 4, :], four(4 + g), over4(bG, g), ALU.mult)
                nc.vector.tensor_tensor(kdec[:, 4 * g:4 * g + 4, :], four(4 + g), over4(Gd, g), ALU.mult).then_inc(S["k_read"], 1)
            for g in range(4):
                dve.wait_ge(S["v_turned"], g + 1)
                nc.vector.tensor_tensor(vbt[:, 4 * g:4 * g + 4, :], four(g), over4(bt, g), ALU.mult).then_inc(S["v_read"], 1)
            for g in range(4):
                dve.wait_ge(S["g_rows"], g + 1)
                nc.vector.tensor_tensor(dk[:, 4 * g:4 * g + 4, :], four(4 + g), over4(Gc, g), ALU.subtract).then_inc(S["rows_read_dve"], 1)
            dve.wait_ge(S["rows_read_dve"], 4)
            nc.vector.tensor_scalar(dk, dk, 0.0, None, ALU.min).then_inc(S["diffs"], 1)
            dve.wait_ge(S["decay_masked"], 1)
            dve.wait_ge(S["beta_rows"], 1)
            for g in range(4):
                dve.wait_ge(S["kk"], g + 1)
                nc.vector.tensor_tensor(mt[:, 4 * g:4 * g + 4, :], four(4 + g), dk[:, 4 * g:4 * g + 4, :], ALU.mult).then_inc(S["kk_read"], 1)
                dve.wait_ge(S["kk_read"], g + 1)
                nc.vector.tensor_tensor(mt[:, 4 * g:4 * g + 4, :], four(g), mt[:, 4 * g:4 * g + 4, :], ALU.mult)
            for g in range(4):
                dve.wait_ge(S["qk"], g + 1)
                nc.vector.tensor_tensor(qkt[:, 4 * g:4 * g + 4, :], four(4 + g), dk[:, 4 * g:4 * g + 4, :], ALU.mult)
            dve.wait_ge(S["rows_read_act"], 4)
            nc.vector.tensor_copy(gl[:, :, :].rearrange("p (t c) h -> p t h c", t=NT),
                                  egr.rearrange("p (t h) (c i) -> p t h c i", t=NT, c=2)[:, :, :, :, CHUNK - 1]).then_inc(S["glast"], 1)
            stage.end()
            eye4 = ident.unsqueeze(1).to_broadcast([P, 4, P])
            for n in range(4 * len(LEVELS)):
                g = n % 4
                gs = slice(4 * g, 4 * g + 4)
                dve.wait_ge(S["z_ps"], n + 1)
                if n < 4:
                    nc.vector.tensor_tensor(xt[:, gs, :], eye4, bb[:, gs, :], ALU.subtract)
                    last = nc.vector.tensor_tensor(xi[:, gs, :], eye4, four(4 + g % 2), ALU.subtract)
                else:
                    if n < 4 * (len(LEVELS) - 1):
                        nc.vector.tensor_tensor(xi[:, gs, :], xi[:, gs, :], four(4 + g % 2), ALU.subtract)
                    last = nc.vector.tensor_tensor(xt[:, gs, :], xt[:, gs, :], four(6 + g % 2), ALU.subtract)
                last.then_inc(S["x_done"], 1)
            stage.end()
            for g in range(4):
                dve.wait_ge(S["u_ps"], g + 1)
                nc.vector.tensor_copy(uu[:, 4 * g:4 * g + 4, :], four(4 + g)).then_inc(S["u_moved"], 1)
            dve.wait_ge(S["u_moved"], 4)
            dve.wait_ge(S["zeroed"], 1)
            for c in range(4):
                t, r = c // 2, CHUNK * (c % 2)
                rows = slice(r, r + CHUNK)
                dve.wait_ge(S["ws"], c + 1)
                if c:
                    dve.wait_ge(S["o_ps"], c)
                nc.vector.tensor_tensor(vnew[rows, :, :], uu[rows, HEADS * t:HEADS * t + HEADS, :],
                                        ps[rows, 0:2, :].rearrange("p b (h i) -> p (b h) i", h=4), ALU.add).then_inc(S["vnew"], 1)
                dve.wait_ge(S["state_read"], c + 1)
                dve_step(nc.vector.tensor_tensor(state, state, gl[:, c, :].unsqueeze(2).to_broadcast([P, HEADS, P]), ALU.mult))
                dve.wait_ge(S["kv"], c + 1)
                nc.vector.tensor_tensor(state, state, ps[:, 4:6, :].rearrange("p b (h i) -> p (b h) i", h=4), ALU.add).then_inc(S["state"], 1)
                dve.wait_ge(S["state"], c + 1)
            stage.end()
            dve.wait_ge(S["o_sq"], 1)
            nc.vector.tensor_reduce(ssq[:, 0:SYS], egr, AX, ALU.add).then_inc(S["o_sums"], 1)
            dve.wait_ge(S["o_root"], 1)
            dve_step(nc.vector.reciprocal(ssq[:, 0:SYS], rsd[:, 0:SYS]))
            dve_step(nc.vector.tensor_tensor(oo, oo, ssq[:, 0:SYS].unsqueeze(2).to_broadcast([P, SYS, P]), ALU.mult))
            dve.wait_ge(S["silu_zb"], 1)
            nc.vector.tensor_tensor(oo, oo, zb[:, :, :].rearrange("p t (h i) -> p (t h) i", h=HEADS), ALU.mult).then_inc(S["o_gated"], 1)
            dve.wait_ge(S["o_turned"], 1)
            for h in range(HEADS):
                nc.vector.tensor_scalar(obt[:, h, :], ps[:, h // 2, T * (h % 2):T * (h % 2) + T], w_gdn, None, ALU.mult)
            stage.end()

        rs = slice(64, 96)
        kr, posf, s_arg, c_arg = (arena(4)[rs, T * i:T * i + T] for i in range(4))
        turns, angle = (arena(5)[rs, T * i:T * i + T] for i in range(2))
        cq, ckv = extra[:, 0, 0:NT * QR].rearrange("p (t n) -> p t n", t=NT), extra[:, 0, 768:768 + NT * KVR].rearrange("p (t n) -> p t n", t=NT)
        cqn, ckvn = extra[:, 1, 0:NT * QR].rearrange("p (t n) -> p t n", t=NT), extra[:, 1, 768:768 + NT * KVR].rearrange("p (t n) -> p t n", t=NT)
        cqt, ckvt = extra[:, 2, 0:768].rearrange("p (k n) -> p k n", k=3), extra[:, 2, 768:1280].rearrange("p (k n) -> p k n", k=2)

        def stick(h, i):
            return arena(h % 4)[:, 384 * i:384 * i + 384]

        def block2_pool(pool, stage):
            for _ in range(14, 19):
                stage.end()
            for i in range(HEADS + 2):
                if 1 <= i <= HEADS:
                    h = i - 1
                    pool.wait_ge(S["softplus"], h + 1)
                    if h >= 4:
                        pool.wait_ge(S["after"], h - 3)
                    nc.gpsimd.tensor_tensor(stick(h, 2), stick(h, 1), con("strict"), ALU.mult).then_inc(S["masked_sp"], 1)
                if i >= 2:
                    h = i - 2
                    pool.wait_ge(S["stick_exp"], h + 1)
                    nc.gpsimd.tensor_tensor(stick(h, 3), stick(h, 3), con("strict"), ALU.mult).then_inc(S["stick_w"], 1)
            stage.end()
            stage.end()
            stage.end()

        def block2_pe(pe, stage, prod):
            pe.wait_ge(S["normed"], 2)
            turn_pe(pe, oat_tm, KD)
            stage.end()
            prod.token_major(ht, QR)
            prod.chunk(prod.tm_units(ht, KVR, lambda w, j: w[:, j, 0:KVR]) + prod.fm_units(ht, 1, 32, at=KVR, r0=64), KD, KVR + 32)
            prod.feature_major(ht)
            prod.feature_major(ht)
            prod.token_major(ht)
            stage.end()
            pe.wait_ge(S["normed"], 3)
            turn_pe(pe, cqn, QR // P)
            pe.wait_ge(S["normed"], 4)
            turn_pe(pe, ckvn, KVR // P, 2)
            stage.end()
            prod.chunk(prod.fm_units(cqt, 8, 96), QR // P, 96 * HEADS)
            prod.chunk(prod.fm_units(ckvt, 8, 64, step=P) +
                       prod.tm_units(ckvt, BANK, lambda w, j: w[:, j, :].rearrange("p (h n) -> p h n", h=HEADS)[:, :, 64:P]), KVR // P, P * HEADS)
            stage.end()
            for m in range(4):
                pe.matmul(ps[rs, m, :], con("rot", rs), fm[rs, 8 + 2 * m:10 + 2 * m, :], start=True, stop=True).then_inc(S["rotated2"], 1)
            pe.matmul(ps[rs, 4, 0:T], con("rot", rs), kr, start=True, stop=True).then_inc(S["rotated2"], 1)
            pe.wait_ge(S["roped2"], 5)

            def out_mla(h, pt):
                v = [va[:, t, 512 + 64 * h:576 + 64 * h] for t in range(NT)]
                pe.matmul(ps[:, 4, 64 * h:64 * h + 64], pt[:, 0:P], v[0], start=True, stop=True)
                pe.matmul(ps[:, 5, 64 * h:64 * h + 64], pt[:, P:T], v[0], start=True, stop=False)
                return pe.matmul(ps[:, 5, 64 * h:64 * h + 64], pt[:, T:3 * P], v[1], start=False, stop=True)

            attention_pe(pe, HEADS, lambda h: fm[0:96, 8 + h, :], lambda h: fm[0:96, 16 + h, :], out_mla)
            stage.end()
            for i in range(HEADS + 3):
                if i < HEADS:
                    r = slice(64 * (i % 2), 64 * (i % 2) + 64)
                    q, k, b = fm[r, i // 2, :], fm[r, 4 + i // 2, :], ps[:, i % 2, :]
                    if i >= 2:
                        pe.wait_ge(S["z_read"], i - 1)
                    pe.matmul(b[:, 0:T], k[:, 0:P], q[:, 0:T], start=True, stop=True)
                    pe.matmul(b[:, T:3 * P], k[:, P:T], q[:, P:T], start=True, stop=True).then_inc(S["stick_z"], 1)
                if 1 <= i <= HEADS:
                    h = i - 1
                    b, sp = ps[:, 2 + h % 2, :], stick(h, 2)
                    pe.wait_ge(S["masked_sp"], h + 1)
                    if h >= 2:
                        pe.wait_ge(S["after_read"], h - 1)
                    pe.matmul(b[:, 0:T], con("later"), sp[:, 0:T], start=True, stop=False, skip_group_check=True)
                    pe.matmul(b[:, P:T], con("ones"), sp[:, T:3 * P], start=False, stop=False, skip_group_check=True)
                    pe.matmul(b[:, T:3 * P], con("later"), sp[:, T:3 * P], start=False, stop=True, skip_group_check=True).then_inc(S["after"], 1)
                if i >= 3:
                    h = i - 3
                    pe.wait_ge(S["stick_w"], h + 1)
                    w = stick(h, 3)
                    v = [va[:, t, 64 * h:64 * h + 64] for t in range(NT)]
                    pe.matmul(ps[:, 4, 64 * h:64 * h + 64], w[:, 0:P], v[0], start=True, stop=True)
                    pe.matmul(ps[:, 5, 64 * h:64 * h + 64], w[:, P:T], v[0], start=True, stop=False)
                    pe.matmul(ps[:, 5, 64 * h:64 * h + 64], w[:, T:3 * P], v[1], start=False, stop=True).then_inc(S["stick_out"], 1)
            stage.end()
            pe.wait_ge(S["normed"], 5)
            turn_pe(pe, oat_tm, KD)
            stage.end()
            for c in range(2):
                prod.token_major(ht)
            stage.end()

        def block2_act(act, stage, moves):
            norm_act(act, xs, [(0, D)], extra[:, 0, :])
            stage.end()
            moves.take(2, lambda i, b: copy_out(act, cq[:, i, :], ps[:, b, 0:QR]))
            moves.take(2, lambda i, b: copy_out(act, ckv[:, i, :], ps[:, b, 0:KVR]))
            moves.take(1, lambda i, b: copy_out(act, kr, ps[rs, b, 0:T]))
            moves.take(8, lambda i, b: copy_out(act, fm[:, i, :], ps[:, b, 0:T]))
            moves.take(2, lambda i, b: copy_out(act, va[:, i, 0:BANK], ps[:, b, :]))
            stage.end()
            norm_act(act, cq, [(0, QR)], arena(0))
            act.wait_ge(S["normed"], 3)
            norm_act(act, ckv, [(0, KVR)], arena(0))
            act.wait_ge(S["angles"], 1)
            nc.scalar.activation(s_arg, s_arg, ACT.Sin)
            nc.scalar.activation(c_arg, c_arg, ACT.Sin)
            stage.end()
            moves.take(8, lambda i, b: copy_out(act, fm[0:96, 8 + i, :], ps[0:96, b, 0:T]))
            moves.take(8, lambda i, b: copy_out(act, fm[0:64, 16 + i, :], ps[0:64, b, 0:T]))
            moves.take(2, lambda i, b: copy_out(act, va[:, i, BANK:D], ps[:, b, :]))
            stage.end()
            attention_act(act, HEADS)
            stage.end()
            for i in range(HEADS + 2):
                if i < HEADS:
                    act.wait_ge(S["minus_abs"], i + 1)
                    act_step(nc.scalar.activation(stick(i, 1), stick(i, 1), ACT.Exp))
                    nc.scalar.activation(stick(i, 1), stick(i, 1), ACT.Ln, bias=con("small")[:, 2:3]).then_inc(S["log1p"], 1)
                if i >= 2:
                    h = i - 2
                    act.wait_ge(S["after_read"], h + 1)
                    nc.scalar.activation(stick(h, 3), stick(h, 0), ACT.Exp).then_inc(S["stick_exp"], 1)
            stage.end()
            norm_act(act, zb, [(0, BANK), (BANK, BANK)], extra[:, 0, :])
            stage.end()
            moves.skip(4)
            stage.end()

        def block2_dve(dve, stage, moves):
            norm_dve(dve, xs, [(0, D)], oat_tm)
            turn_dve(dve, ht, KD, g_attn)
            stage.end()
            moves.take(2, lambda i, b: copy_out(dve, cq[:, i, :], ps[:, b, 0:QR]))
            moves.take(2, lambda i, b: copy_out(dve, ckv[:, i, :], ps[:, b, 0:KVR]))
            moves.take(1, lambda i, b: copy_out(dve, kr, ps[rs, b, 0:T]))
            moves.take(8, lambda i, b: copy_out(dve, fm[:, i, :], ps[:, b, 0:T]))
            moves.take(2, lambda i, b: copy_out(dve, va[:, i, 0:BANK], ps[:, b, :]))
            stage.end()
            norm_dve(dve, cq, [(0, QR)], cqn)
            norm_dve(dve, ckv, [(0, KVR)], ckvn)
            turn_dve(dve, cqt, QR // P, g_cq)
            turn_dve(dve, ckvt, KVR // P, g_ckv, 2)
            dve_step(nc.vector.tensor_copy(posf, posi[rs, :]))
            dve_step(nc.vector.tensor_scalar(angle, posf, con("freq", rs), None, ALU.mult))
            for arg, quarter in ((s_arg, 0.0), (c_arg, 0.25)):
                dve_step(nc.vector.tensor_scalar(turns, angle, 1.0 / TWO_PI, quarter, ALU.mult, ALU.add))
                dve_step(nc.vector.tensor_scalar(turns, turns, ROUND, None, ALU.add))
                dve_step(nc.vector.tensor_scalar(turns, turns, ROUND, None, ALU.subtract))
                dve_step(nc.vector.scalar_tensor_tensor(out=arg, in0=turns, scalar=-PI_A, in1=angle, op0=ALU.mult, op1=ALU.add))
                dve_step(nc.vector.scalar_tensor_tensor(out=arg, in0=turns, scalar=-PI_B, in1=arg, op0=ALU.mult, op1=ALU.add))
                dve_step(nc.vector.scalar_tensor_tensor(out=arg, in0=turns, scalar=-PI_C, in1=arg, op0=ALU.mult, op1=ALU.add))
                if quarter:
                    dve_step(nc.vector.tensor_scalar(arg, arg, np.pi / 2, None, ALU.add))
                last = nc.vector.tensor_scalar(arg, arg, PI_IN, -PI_IN, ALU.min, ALU.max)
            last.then_inc(S["angles"], 1)
            stage.end()
            moves.take(8, lambda i, b: copy_out(dve, fm[0:96, 8 + i, :], ps[0:96, b, 0:T]))
            moves.take(8, lambda i, b: copy_out(dve, fm[0:64, 16 + i, :], ps[0:64, b, 0:T]))
            moves.take(2, lambda i, b: copy_out(dve, va[:, i, BANK:D], ps[:, b, :]))
            stage.end()
            r1, r2 = (arena(5)[rs, 512 * i:512 * i + 512].rearrange("p (a b) -> p a b", a=2) for i in range(2))
            sin2, cos2 = (a.unsqueeze(1).to_broadcast([32, 2, T]) for a in (s_arg, c_arg))
            for m in range(4):
                q2 = fm[rs, 8 + 2 * m:10 + 2 * m, :]
                dve.wait_ge(S["rotated2"], m + 1)
                nc.vector.tensor_tensor(r1, ps[rs, m, :].rearrange("p (a b) -> p a b", a=2), sin2, ALU.mult)
                dve_step(nc.vector.tensor_tensor(r2, q2, cos2, ALU.mult))
                nc.vector.tensor_tensor(q2, r1, r2, ALU.add).then_inc(S["roped2"], 1)
                dve.wait_ge(S["roped2"], m + 1)
            dve.wait_ge(S["rotated2"], 5)
            nc.vector.tensor_tensor(r1[:, 0, :], ps[rs, 4, 0:T], s_arg, ALU.mult)
            dve_step(nc.vector.tensor_tensor(r2[:, 0, :], kr, c_arg, ALU.mult))
            nc.vector.tensor_tensor(fm[rs, 16:24, :], r1[:, 0, :].unsqueeze(1).to_broadcast([32, HEADS, T]),
                                    r2[:, 0, :].unsqueeze(1).to_broadcast([32, HEADS, T]), ALU.add).then_inc(S["roped2"], 1)
            attention_dve(dve, HEADS, 96.0 ** -0.5, lambda h: None)
            dve.wait_ge(S["head_out"], 2 * HEADS)
            for t in range(NT):
                nc.vector.tensor_copy(zb[:, t, 0:BANK], ps[:, 4 + t, :])
            stage.end()
            for i in range(HEADS + 2):
                if i < HEADS:
                    dve.wait_ge(S["stick_z"], i + 1)
                    if i >= 4:
                        dve.wait_ge(S["stick_out"], i - 3)
                    nc.vector.tensor_scalar(stick(i, 0), ps[:, i % 2, 0:3 * P], 0.125, None, ALU.mult).then_inc(S["z_read"], 1)
                    dve.wait_ge(S["z_read"], i + 1)
                    nc.vector.scalar_tensor_tensor(out=stick(i, 1), in0=stick(i, 0), scalar=-1.0, in1=stick(i, 0), op0=ALU.mult, op1=ALU.min).then_inc(S["minus_abs"], 1)
                if 1 <= i <= HEADS:
                    h = i - 1
                    dve.wait_ge(S["log1p"], h + 1)
                    nc.vector.scalar_tensor_tensor(out=stick(h, 1), in0=stick(h, 0), scalar=0.0, in1=stick(h, 1), op0=ALU.max, op1=ALU.add).then_inc(S["softplus"], 1)
                    dve.wait_ge(S["softplus"], h + 1)
                    dve_step(nc.vector.tensor_tensor(stick(h, 0), stick(h, 0), stick(h, 1), ALU.subtract))
                if i >= 2:
                    h = i - 2
                    dve.wait_ge(S["after"], h + 1)
                    nc.vector.tensor_tensor(stick(h, 0), stick(h, 0), ps[:, 2 + h % 2, 0:3 * P], ALU.subtract).then_inc(S["after_read"], 1)
            dve.wait_ge(S["stick_out"], HEADS)
            for t in range(NT):
                nc.vector.tensor_copy(zb[:, t, BANK:D], ps[:, 4 + t, :])
            stage.end()
            norm_dve(dve, zb, [(0, BANK), (BANK, BANK)], oat_tm)
            turn_dve(dve, ht, KD, g_mix)
            stage.end()
            moves.take(4, lambda i, b: nc.vector.tensor_tensor(xs[:, i % 2, BANK * (i // 2):BANK * (i // 2) + BANK], ps[:, b, :],
                                                               xs[:, i % 2, BANK * (i // 2):BANK * (i // 2) + BANK], ALU.add), whole=True)
            stage.end()

        NLIST = NEXP + MAXOVER + 1
        ub = fm[:, :, :].rearrange("p a b -> p (a b)").bitcast(BF16)[:, 0:3 * NT * D].rearrange("p (s t d) -> p s t d", s=3, t=NT)
        u_tok, rest = va, zb
        g_row = extra[:, 2, 0:D]
        bdn = extra[0:NEXP, 2, D:2 * D]
        bgu, bgu_rest = extra[0:3 * NEXP, 0, :], extra[0:3 * NEXP, 1, :]
        bgp = sb("bgp", [3 * NEXP, 2048], BF16)
        wr = sb("wr", [P, KD, NEXP])
        lg, gate, pick, posx = (sb(n, [P, NT, NEXP]) for n in ("lg", "gate", "pick", "posx"))
        mx8 = sb("mx8", [P, NT, 8])
        ix8 = sb("ix8", [P, NT, 8], U32)
        ixf = sb("ixf", [P, NT, 8])
        gsm = sb("gsm", [P, NT])
        over = sb("over", [NEXP, 8])
        hot = extra[0:NEXP, 1, 0:3 * MAXOVER].rearrange("p (r k) -> p r k", r=3)
        wlist = sb("wlist", [1, 2, NLIST], I32)
        wcount = sb("wcount", [1, 1], I32)
        tmp4 = zb[:, 1, 0:512].rearrange("p (a j e) -> p a j e", a=4, j=4)
        gate_t = zb[0:NEXP, 1, 512:512 + T]
        xst = zb[:, 0, 0:KD * CAP].rearrange("p (k s) -> p k s", k=KD)
        glu, lin, sig, act_b = extra[:, 0, 0:512], extra[:, 0, 512:1024], extra[:, 0, 1024:1536], extra[:, 0, 1536:2048]
        act_t = extra[:, 1, 0:512].rearrange("p (j m) -> p j m", j=4)
        pgt = extra[:, 1, 512:512 + T]
        y_sb = extra[:, 1, 1024:1536]
        pg = extra[:, 1, 1536:1536 + NT * 2 * CAP].rearrange("p (t a s) -> p t a s", t=NT, a=2)
        pick_s = sb("pick_s", [P, NT, CAP], BF16)
        bsel = sb("bsel", [3 * NEXP, CAP], BF16)
        w_gu, w_dn = I["w_gu_2"][0], I["w_dn_2"][0]

        def expert_chunk(e, c):
            if c < 4:
                src = w_gu[e].rearrange("(p k) n -> p k n", k=KD)[:, 2 * c:2 * c + 2, :]
                return ring[:, c, :].rearrange("p (k n) -> p k n", k=2), src
            src = w_dn[e].rearrange("(a p j) n -> a p j n", a=2, j=4)[c - 4]
            return ring[:, c, :].rearrange("p (j n) -> p j n", j=4), src

        class LoopSteps:

            def __init__(self, eng, sem, it, per):
                self.eng, self.sem, self.it, self.per, self.n = eng, sem, it, per, 0

            def __call__(self, ins):
                self.n += 1
                ins.then_inc(self.sem, 1)
                self.eng.wait_ge(self.sem, self.it * self.per + self.n)

            def close(self):
                assert self.n == self.per, self.n

        def item_count(eng):
            return eng.value_load(wcount[0:1, 0:1], min_val=NEXP, max_val=NEXP + MAXOVER)

        def moe_pool(pool, stage):
            pool.dma_start(g_row, I["g_moe_2"][0].partition_broadcast(P)).then_inc(S["row_in"], 16)
            pool.dma_start(bdn, I["b_dn_2"][0]).then_inc(S["row_in"], 16)
            for i in range(3):
                pool.dma_start(extra[NEXP * i:NEXP * i + NEXP, 0, :], I["b_gu_2"][0]).then_inc(S["bias_in"], 16)
            stage.end()
            stage.end()
            pool.dma_start(p_tok, I["p_2"][0, 0].rearrange("(t p) n -> p t n", p=P)).then_inc(S["p_in"], 16)
            stage.end()

        def moe_pe(pe, stage):
            pe.wait_ge(S["normed"], 6)
            turn_pe(pe, oat_tm, KD)
            pe.wait_ge(S["u_t"], 1)
            for t in range(NT):
                for j in range(KD):
                    last = pe.matmul(ps[:, 4, NEXP * t:NEXP * t + NEXP], ht[:, j, P * t:P * t + P], wr[:, j, :], start=(j == 0), stop=(j == KD - 1))
            last.then_inc(S["logits"], 1)
            stage.end()
            pe.wait_ge(S["picked"], 1)
            pe.matmul(ps[:, 0, 0:NEXP], con("earlier"), pick[:, 0, :], start=True, stop=True)
            pe.matmul(ps[:, 0, NEXP:2 * NEXP], con("earlier"), pick[:, 1, :], start=True, stop=False)
            pe.matmul(ps[:, 0, NEXP:2 * NEXP], con("ones"), pick[:, 0, :], start=False, stop=True).then_inc(S["positions"], 1)
            for t in range(NT):
                last = pe.matmul(ps[0:NEXP, 1, 0:1], pick[:, t, :], con("ones")[:, 0:1], start=(t == 0), stop=(t == NT - 1))
            last.then_inc(S["counts"], 1)
            pe.wait_ge(S["gated"], 1)
            for t in range(NT):
                last = pe.transpose(ps[0:NEXP, 5, P * t:P * t + P], gate[:, t, :], ident)
            last.then_inc(S["gate_turned"], 1)
            pe.wait_ge(S["overs"], 1)
            pe.matmul(ps[0:NEXP, 2, 0:3], con("earlier", slice(0, NEXP))[:, 0:NEXP], over[:, 0:3], start=True, stop=True).then_inc(S["before"], 1)
            pe.wait_ge(S["hots"], 1)
            for a in range(2):
                for r in range(3):
                    lhs = con("row", slice(0, NEXP)) if a == 0 else con("small", slice(0, NEXP))[:, 3 + r:4 + r]
                    pe.matmul(ps[0:1, 3, MAXOVER * a:MAXOVER * a + MAXOVER], lhs, hot[:, r, :], start=(r == 0), stop=(r == 2))
            for r in range(3):
                last = pe.matmul(ps[0:1, 3, 2 * MAXOVER:2 * MAXOVER + 1], over[:, r:r + 1], con("ones", slice(0, NEXP))[:, 0:1], start=(r == 0), stop=(r == 2))
            last.then_inc(S["listed"], 1)
            stage.end()
            for t in range(NT):
                for n in range(2):
                    pe.matmul(ps[:, 2 * t + n, :], gate_t[:, P * t:P * t + P], bdn[:, BANK * n:BANK * n + BANK], start=True, stop=False, skip_group_check=True)
            total = item_count(pe)

            def gather():
                for k in range(KD):
                    for i in range(3 * NT):
                        last = pe.matmul(ps[:, 7, CAP * k:CAP * k + CAP], ub[:, i // NT, i % NT, k:k + KD * (P - 1) + 1:KD], pick_s[:, i % NT, :],
                                         start=(i == 0), stop=(i == 3 * NT - 1))
                last.then_inc(S["gathered"], 1)

            def spread(wait):
                wait()
                for t in range(NT):
                    for n in range(2):
                        r = slice(64 * n, 64 * n + CAP)
                        last = pe.matmul(ps[:, 2 * t + n, :], pgt[r, P * t:P * t + P], y_sb[r, :], start=False, stop=False, skip_group_check=True)
                last.then_inc(S["spread"], 1)

            pe.wait_ge(S["pick_s"], 1)
            gather()
            with pe.Fori(0, total) as it:
                pe.wait_ge(S["xst"], it + 1)
                pe.wait_ge(S["bsel"], it + 1)
                pe.wait_ge(S["act_t"], it)
                pe.wait_ge(S["pgt"], it)
                for n in range(4):
                    pe.matmul(ps[64 * (n % 2):64 * (n % 2) + CAP, 4 + n // 2, :], bsel[:, :], bgp[:, BANK * n:BANK * n + BANK], start=True, stop=False, skip_group_check=True)
                for c in range(4):
                    pe.wait_ge(S[f"expert_in{c}"], it * 16 + 16)
                    for k in (2 * c, 2 * c + 1):
                        for n in range(4):
                            last = pe.matmul(ps[64 * (n % 2):64 * (n % 2) + CAP, 4 + n // 2, :], xst[:, k, :],
                                             ring[:, c, 2048 * (k % 2) + BANK * n:2048 * (k % 2) + BANK * n + BANK], start=False, stop=(k == KD - 1), skip_group_check=True)
                    last.then_inc(S["w_used"], 1)
                pe.wait_ge(S["pick_s"], it + 2)
                gather()
                spread(lambda: pe.wait_ge(S["y_sb"], it + 1))
                pe.wait_ge(S["act"], it + 1)
                for j in range(4):
                    last = pe.transpose(ps[:, 4, P * j:P * j + P], act_b[:, j:j + 4 * (P - 1) + 1:4], ident)
                last.then_inc(S["act_turned"], 1)
                pe.wait_ge(S["pg"], it + 1)
                for t in range(NT):
                    last = pe.transpose(ps[:, 5, P * t:P * t + P], pg[:, t, :, :].rearrange("p a s -> p (a s)"), ident)
                last.then_inc(S["pg_turned"], 1)
                pe.wait_ge(S["act_t"], it + 1)
                for c in range(2):
                    pe.wait_ge(S[f"expert_in{4 + c}"], it * 16 + 16)
                    for j in range(4):
                        for n in range(2):
                            last = pe.matmul(ps[64 * n:64 * n + CAP, 6, :], act_t[:, j, 64 * c:64 * c + CAP],
                                             ring[:, 4 + c, D * j + BANK * n:D * j + BANK * n + BANK], start=(c == 0 and j == 0), stop=(c == 1 and j == 3), skip_group_check=True)
                    last.then_inc(S["w_used"], 1)
            spread(lambda: (pe.wait_ge(S["y_sb"], total + 1), pe.wait_ge(S["pgt"], total)))
            stage.end()

        def moe_act(act, stage):
            norm_act(act, xs, [(0, D)], zb[:, 0, :])
            act.wait_ge(S["u_tok"], 1)
            nc.scalar.activation(ub[:, 0], u_tok[:, :, :], ACT.Copy).then_inc(S["part"], 1)
            act.wait_ge(S["rest"], 1)
            nc.scalar.activation(ub[:, 1], rest[:, :, :], ACT.Copy).then_inc(S["part"], 1)
            act.wait_ge(S["rest"], 2)
            nc.scalar.activation(ub[:, 2], rest[:, :, :], ACT.Copy)
            stage.end()
            act.wait_ge(S["less_max"], 1)
            nc.scalar.activation(mx8[:, :, 0:4], mx8[:, :, 0:4], ACT.Exp).then_inc(S["gate_exp"], 1)
            act.wait_ge(S["gate_turned"], 1)
            nc.scalar.activation(gate_t, ps[0:NEXP, 5, 0:T], ACT.Copy)
            nc.scalar.activation(y_sb, con("causal")[:, 0:1].to_broadcast([P, 512]), ACT.Copy, scale=0.0).then_inc(S["y_sb"], 1)
            nc.scalar.activation(pgt, con("causal")[:, 0:1].to_broadcast([P, T]), ACT.Copy, scale=0.0)
            stage.end()
            total = item_count(act)
            act.wait_ge(S["gathered"], 1)
            nc.scalar.activation(xst, ps[:, 7, 0:KD * CAP].rearrange("p (k s) -> p k s", k=KD), ACT.Copy).then_inc(S["xst"], 1)
            with act.Fori(0, total) as it:
                act.wait_ge(S["glu"], it + 1)
                nc.scalar.activation(sig, glu, ACT.Sigmoid, scale=1.702).then_inc(S["sig"], 1)
                act.wait_ge(S["gathered"], it + 2)
                nc.scalar.activation(xst, ps[:, 7, 0:KD * CAP].rearrange("p (k s) -> p k s", k=KD), ACT.Copy).then_inc(S["xst"], 1)
                act.wait_ge(S["pg_turned"], it + 1)
                nc.scalar.activation(pgt, ps[:, 5, 0:T], ACT.Copy).then_inc(S["pgt"], 1)
                act.wait_ge(S["w_used"], it * 6 + 6)
                nc.scalar.activation(y_sb, ps[:, 6, :], ACT.Copy).then_inc(S["y_sb"], 1)
            stage.end()

        def moe_dve(dve, stage):
            norm_dve(dve, xs, [(0, D)], oat_tm)
            dve.wait_ge(S["row_in"], 16 * 3)
            dve.wait_ge(S["normed"], 6)
            for t in range(NT):
                last = nc.vector.tensor_tensor(u_tok[:, t, :], oat_tm[:, t, :], g_row, ALU.mult)
            last.then_inc(S["u_tok"], 1)
            turn_dve(dve, ht, KD, g_moe, done="u_t")
            dve.wait_ge(S["part"], 1)
            nc.vector.tensor_tensor(rest[:, :, :], u_tok[:, :, :], ub[:, 0], ALU.subtract).then_inc(S["rest"], 1)
            dve.wait_ge(S["rest"], 1)
            dve.wait_ge(S["part"], 2)
            nc.vector.tensor_tensor(rest[:, :, :], rest[:, :, :], ub[:, 1], ALU.subtract).then_inc(S["rest"], 1)
            dve.wait_ge(S["bias_in"], 48)
            dve_step(nc.vector.tensor_copy(bgp[:, :], bgu))
            for g in (1, 2):
                dve_step(nc.vector.tensor_tensor(bgu_rest, (bgu, bgu_rest)[g - 1], bgp[:, :], ALU.subtract))
                for q in range(g, 3):
                    last = nc.vector.tensor_copy(bgp[NEXP * q:NEXP * q + NEXP, :], bgu_rest[NEXP * q:NEXP * q + NEXP, :])
                dve_step(last)
            dve.wait_ge(S["logits"], 1)
            dve_step(nc.vector.tensor_tensor(lg[:, :, :], ps[:, 4, 0:2 * NEXP].rearrange("p (t e) -> p t e", t=NT), brow[:, :].unsqueeze(1).to_broadcast([P, NT, NEXP]), ALU.add))
            stage.end()
            for t in range(NT):
                dve_step(nc.vector.max(mx8[:, t, :], lg[:, t, :]))
                dve_step(nc.vector.max_index(ix8[:, t, :], mx8[:, t, :], lg[:, t, :]))
            dve_step(nc.vector.tensor_copy(ixf[:, :, :], ix8[:, :, :]))
            dve_step(nc.vector.tensor_copy(gsm[:, :], mx8[:, :, 0]))
            for t in range(NT):
                last = nc.vector.tensor_scalar(mx8[:, t, 0:4], mx8[:, t, 0:4], gsm[:, t:t + 1], None, ALU.subtract)
            last.then_inc(S["less_max"], 1)
            number = con("slots")[:, 0:NEXP]
            for t in range(NT):
                for j in range(4):
                    last = nc.vector.tensor_scalar(tmp4[:, t, j, :], number, ixf[:, t, j:j + 1], None, ALU.is_equal)
            dve_step(last)
            for t in range(NT):
                last = nc.vector.tensor_reduce(pick[:, t, :], tmp4[:, t].rearrange("p j e -> p e j"), AX, ALU.add)
            last.then_inc(S["picked"], 1)
            dve.wait_ge(S["gate_exp"], 1)
            dve_step(nc.vector.tensor_reduce(gsm[:, :], mx8[:, :, 0:4], AX, ALU.add))
            dve_step(nc.vector.reciprocal(gsm[:, :], gsm[:, :]))
            for t in range(NT):
                last = nc.vector.tensor_scalar(mx8[:, t, 0:4], mx8[:, t, 0:4], gsm[:, t:t + 1], None, ALU.mult)
            dve_step(last)
            for t in range(NT):
                for j in range(4):
                    last = nc.vector.tensor_scalar(tmp4[:, 2 + t, j, :], number, ixf[:, t, j:j + 1], mx8[:, t, j:j + 1], ALU.is_equal, ALU.mult)
            dve_step(last)
            for t in range(NT):
                last = nc.vector.tensor_reduce(gate[:, t, :], tmp4[:, 2 + t].rearrange("p j e -> p e j"), AX, ALU.add)
            last.then_inc(S["gated"], 1)
            dve.wait_ge(S["picked"], 1)
            dve_step(nc.vector.tensor_scalar(posx[:, :, :], pick[:, :, :], -4096.0, 4096.0, ALU.mult, ALU.add))
            dve.wait_ge(S["positions"], 1)
            dve_step(nc.vector.tensor_tensor(posx[:, :, :], posx[:, :, :], ps[:, 0, 0:2 * NEXP].rearrange("p (t e) -> p t e", t=NT), ALU.add))
            dve.wait_ge(S["counts"], 1)
            dve_step(nc.vector.tensor_copy(over[:, 7:8], ps[0:NEXP, 1, 0:1]))
            nc.vector.tensor_scalar(over[:, 0:3], con("small", slice(0, NEXP))[:, 3:6], over[:, 7:8], None, ALU.is_lt).then_inc(S["overs"], 1)
            dve.wait_ge(S["before"], 1)
            dve_step(nc.vector.tensor_reduce(over[:, 6:7], ps[0:NEXP, 2, 0:3], AX, ALU.add))
            dve_step(nc.vector.tensor_scalar(over[:, 3:6], con("slots", slice(0, NEXP))[:, 0:3], over[:, 6:7], None, ALU.add))
            for r in range(3):
                last = nc.vector.tensor_scalar(hot[:, r, :], con("slots", slice(0, NEXP))[:, 0:MAXOVER], over[:, 3 + r:4 + r], over[:, r:r + 1], ALU.is_equal, ALU.mult)
            last.then_inc(S["hots"], 1)
            dve_step(nc.vector.memset(wlist[:, :, :], 0))
            nc.vector.tensor_copy(wlist[:, 0, 0:NEXP], con("slots", slice(0, 1))[:, 0:NEXP])
            dve.wait_ge(S["listed"], 1)
            nc.vector.tensor_copy(wlist[:, :, NEXP:NEXP + MAXOVER], ps[0:1, 3, 0:2 * MAXOVER].rearrange("p (a k) -> p a k", a=2))
            nc.vector.tensor_scalar(wcount[:, :], ps[0:1, 3, 2 * MAXOVER:2 * MAXOVER + 1], float(NEXP), None, ALU.add).then_inc(S["items"], 1)
            stage.end()
            total = item_count(dve)

            def item(i):
                return (dve.value_load(wlist[0:1, 0, bass.ds(i, 1)], min_val=0, max_val=NEXP - 1),
                        dve.value_load(wlist[0:1, 1, bass.ds(i, 1)], min_val=0, max_val=T))

            def pick_tokens(e, base):
                for t in range(NT):
                    last = nc.vector.tensor_scalar(pick_s[:, t, :], con_at("slots", base, CAP), posx[:, t, bass.ds(e, 1)], None, ALU.is_equal)
                last.then_inc(S["pick_s"], 1)

            def pick_bias(e):
                nc.vector.tensor_copy(bsel[:, :], con("bsel", slice(0, 3 * NEXP))[:, bass.ds(e, 1)].to_broadcast([3 * NEXP, CAP])).then_inc(S["bsel"], 1)

            pick_tokens(0, 0)
            pick_bias(0)
            with dve.Fori(0, total) as it:
                e, base = item(it)
                e1, base1 = item(it + 1)
                step = LoopSteps(dve, S["moe_step"], it, 2)
                dve.wait_ge(S["pg_turned"], it)
                dve.wait_ge(S["pick_s"], it + 1)
                for t in range(NT):
                    last = nc.vector.tensor_scalar(pg[:, t, :, :], pick_s[:, t, :].unsqueeze(1).to_broadcast([P, 2, CAP]), gate[:, t, bass.ds(e, 1)], None, ALU.mult)
                last.then_inc(S["pg"], 1)
                dve.wait_ge(S["gathered"], it + 1)
                dve.wait_ge(S["pg"], it + 1)
                pick_tokens(e1, base1)
                dve.wait_ge(S["w_used"], it * 6 + 4)
                nc.vector.tensor_scalar(glu, ps[:, 4, :], 7.0, None, ALU.min).then_inc(S["glu"], 1)
                step(nc.vector.tensor_scalar(lin, ps[:, 5, :], 7.0, -7.0, ALU.min, ALU.max))
                pick_bias(e1)
                step(nc.vector.scalar_tensor_tensor(out=lin, in0=lin, scalar=1.0, in1=glu, op0=ALU.add, op1=ALU.mult))
                dve.wait_ge(S["sig"], it + 1)
                nc.vector.tensor_tensor(act_b, lin, sig, ALU.mult).then_inc(S["act"], 1)
                dve.wait_ge(S["act_turned"], it + 1)
                nc.vector.tensor_copy(act_t, ps[:, 4, :].rearrange("p (j m) -> p j m", j=4)).then_inc(S["act_t"], 1)
                step.close()
            stage.end()

        p_tok = va[:, 0, 0:NT * 256].rearrange("p (t n) -> p t n", t=NT)
        p_t = zb[:, 1, 0:2 * T].rearrange("p (k n) -> p k n", k=2)
        ple_gate = gates[:, 0]

        def tail_pool(pool, stage):
            pool.dma_start(g_row, I["g_final_2"].partition_broadcast(P)).then_inc(S["row_in"], 16)
            stage.end()
            stage.end()
            stage.end()

        def tail_pe(pe, stage, prod):
            pe.wait_ge(S["p_in"], 16)
            turn_pe(pe, p_tok, 2, 4)
            pe.wait_ge(S["normed"], 7)
            turn_pe(pe, oat_tm, KD)
            stage.end()
            for c in range(2):
                prod.token_major(ht)
            prod.chunk(prod.tm_units(p_t, BANK, lambda w, j: w[:, j, 0:BANK]) + prod.tm_units(p_t, BANK, lambda w, j: w[:, j, BANK:D]), 2, D)
            stage.end()
            stage.end()

        def tail_act(act, stage, moves):
            act.wait_ge(S["summed"], NT)
            norm_act(act, xs, [(0, D)], zb[:, 0, :])
            stage.end()
            moves.take(4, lambda i, b: nc.scalar.activation(ple_gate[:, i % 2, BANK * (i // 2):BANK * (i // 2) + BANK], ps[:, b, :], ACT.Sigmoid), whole=True)
            moves.skip(4)
            stage.end()
            norm_act(act, xs, [(0, D)], zb[:, 0, :])
            stage.end()

        def tail_dve(dve, stage, moves):
            for t in range(NT):
                nc.vector.tensor_tensor(xs[:, t, :], xs[:, t, :], ps[:, 2 * t:2 * t + 2, :].rearrange("p b n -> p (b n)"), ALU.add).then_inc(S["summed"], 1)
            turn_dve(dve, p_t, 2, None, 4)
            norm_dve(dve, xs, [(0, D)], oat_tm)
            turn_dve(dve, ht, KD, g_ple)
            stage.end()
            moves.skip(4)
            dve.wait_ge(S["moved0"], moves.u // 2 + moves.u % 2)
            dve.wait_ge(S["moved1"], moves.u // 2)
            moves.take(4, lambda i, b: nc.vector.tensor_tensor(oat_tm[:, i % 2, BANK * (i // 2):BANK * (i // 2) + BANK], ps[:, b, :],
                                                               ple_gate[:, i % 2, BANK * (i // 2):BANK * (i // 2) + BANK], ALU.mult), whole=True)
            dve.wait_ge(S["moved0"], moves.u // 2 + moves.u % 2)
            dve.wait_ge(S["moved1"], moves.u // 2)
            nc.vector.tensor_tensor(xs[:, :, :], xs[:, :, :], oat_tm, ALU.add)
            stage.end()
            norm_dve(dve, xs, [(0, D)], None)
            dve.wait_ge(S["row_in"], 16 * 4)
            for t in range(NT):
                nc.vector.scalar_tensor_tensor(out=xs[:, t, :], in0=xs[:, t, :], scalar=ssq[:, t:t + 1], in1=g_row, op0=ALU.mult, op1=ALU.mult)
            stage.end()

        @block.sync
        def _(sp):
            def load_chunk(g):
                if g >= 2:
                    sp.wait_ge(S["unit"], plan[g - 2][2])
                sp.dma_start(plan[g][0], plan[g][1]).then_inc(S[f"chunk_in{g % 2}"], 16)

            for g in range(before_experts):
                load_chunk(g)
            sp.wait_ge(S["stage"], 4 * 20)
            sp.wait_ge(S["unit"], plan[before_experts - 1][2])
            for c in range(6):
                sp.dma_start(*expert_chunk(0, c)).then_inc(S[f"expert_in{c}"], 16)
            sp.wait_ge(S["stage"], 4 * 23)
            total = item_count(sp)
            with sp.Fori(1, total) as it:
                e = sp.value_load(wlist[0:1, 0, bass.ds(it, 1)], min_val=0, max_val=NEXP - 1)
                for c in range(6):
                    sp.wait_ge(S["w_used"], it * 6 + (c - 5))
                    sp.dma_start(*expert_chunk(e, c)).then_inc(S[f"expert_in{c}"], 16)
            sp.wait_ge(S["w_used"], total * 6)
            for g in range(before_experts, len(plan)):
                load_chunk(g)
            sp.wait_ge(S["stage"], 4 * LAST_STAGE)
            sp.dma_start(out[0].rearrange("(t p) d -> p t d", p=P), xs[:, :, :]).then_inc(S["stored"], 16)
            sp.wait_ge(S["stored"], 16)

        @block.gpsimd
        def _(pool):
            stage = Stage(pool, S["stage"])
            pool.dma_start(xs[:, :, :], I["x"][0].rearrange("(t p) d -> p t d", p=P)).then_inc(S["x_in"], 16)
            pool.dma_start(cst[:, :], I["const"]).then_inc(S["const_in"], 16)
            pool.dma_start(w_pre, I["pre_norm_w"][0].rearrange("(p k) -> p k", k=KD)).then_inc(S["small_in"], 16)
            pool.dma_start(w_gdn, I["gdn_norm_w"][0].rearrange("(p k) -> p k", k=1)).then_inc(S["small_in"], 16)
            pool.dma_start(wbd[:, :, :], w_in[:, :, 16 * BANK:16 * BANK + 16]).then_inc(S["small_in"], 16)
            pool.dma_start(extra[0:96, 2, 0:P], I["conv_w"][0].rearrange("j (c p) -> (j c) p", p=P)).then_inc(S["small_in"], 16)
            pool.dma_start(hsc[:, 0:8], I["dt_bias"][0].partition_broadcast(P)).then_inc(S["small_in"], 16)
            pool.dma_start(hsc[:, 8:16], I["a_log"][0].partition_broadcast(P)).then_inc(S["small_in"], 16)
            pool.dma_start(g_attn, I["g_attn_2"][0].rearrange("(p k) -> p k", k=KD)).then_inc(S["small_in"], 16)
            pool.dma_start(g_cq, I["g_cq_2"][0].rearrange("(p k) -> p k", k=QR // P)).then_inc(S["small_in"], 16)
            pool.dma_start(g_ckv, I["g_ckv_2"][0].rearrange("(p k) -> p k", k=KVR // P)).then_inc(S["small_in"], 16)
            pool.dma_start(g_mix[0:64, :], I["g_out_mla_2"][0].rearrange("(p k) -> p k", k=KD)).then_inc(S["small_in"], 16)
            pool.dma_start(g_mix[64:P, :], I["g_out_sb_2"][0].rearrange("(p k) -> p k", k=KD)).then_inc(S["small_in"], 16)
            pool.dma_start(g_moe, I["g_moe_2"][0].rearrange("(p k) -> p k", k=KD)).then_inc(S["small_in"], 16)
            pool.dma_start(g_ple, I["g_ple_2"][0].rearrange("(p k) -> p k", k=KD)).then_inc(S["small_in"], 16)
            pool.dma_start(posi[64:96, :], I["positions_2"][0].partition_broadcast(32)).then_inc(S["small_in"], 16)
            pool.dma_start(wr[:, :, :], pk_rows("w_router_2", KD)).then_inc(S["small_in"], 16)
            pool.dma_start(brow[:, :], I["b_router_2"][0].partition_broadcast(P)).then_inc(S["small_in"], 16)
            pool.wait_ge(S["small_in"], SMALL_LOADS * 16)
            pool.wait_ge(S["const_in"], 16)
            stage.end()
            stage.end()
            stage.end()
            stage.end()
            gdn_pool(pool, stage)
            stage.end()
            stage.end()
            pool.dma_start(extra[:, 2, 0:D], I["post_norm_w"][0].partition_broadcast(P)).then_inc(S["row_in"], 16)
            stage.end()
            stage.end()
            block2_pool(pool, stage)
            moe_pool(pool, stage)
            tail_pool(pool, stage)

        @block.tensor
        def _(pe):
            stage = Stage(pe, S["stage"])
            prod = Products(pe)
            pe.wait_ge(S["const_in"], 16)
            pe.wait_ge(S["small_in"], SMALL_LOADS * 16)
            pe.transpose(ps[:, 4, 0:96], extra[0:96, 2, 0:P], ident[0:96, 0:96]).then_inc(S["conv_turned"], 1)
            pe.wait_ge(S["normed"], 1)
            turn_pe(pe, oat_tm, KD)
            stage.end()
            for c in range(6):
                prod.feature_major(ht)
            for c in range(2):
                prod.token_major(ht)
            stage.end()
            for m in range(8):
                pe.matmul(ps[0:32, m, :], con("rot", slice(0, 32)), fm[0:32, 2 * m:2 * m + 2, :], start=True, stop=True).then_inc(S["rotated"], 1)
            pe.wait_ge(S["roped"], 8)

            def out_a(h, pt):
                b = ps[:, 4 + h % 2, :]
                if h >= 2:
                    pe.wait_ge(S["head_taken"], h - 1)
                pe.matmul(b[:, 0:T], va[:, 0, P * h:P * h + P], pt[:, 0:T], start=True, stop=False, skip_group_check=True)
                return pe.matmul(b[:, P:T], va[:, 1, P * h:P * h + P], pt[:, T:3 * P], start=False, stop=True, skip_group_check=True)

            attention_pe(pe, 0, lambda h: fm[:, h, :], lambda h: fm[:, 8 + h, :], out_a)
            stage.end()
            for c in range(6):
                prod.feature_major(ht)
            for c in range(2):
                prod.token_major(ht)
            pe.wait_ge(S["moved1"], prod.u // 2)
            for t in range(NT):
                for j in range(KD):
                    last = pe.matmul(ps[:, 7, 16 * t:16 * t + 16], ht[:, j, P * t:P * t + P], wbd[:, j, :], start=(j == 0), stop=(j == KD - 1))
            last.then_inc(S["bd_logits"], 1)
            stage.end()
            gdn_pe(pe, stage)
            for c in range(4):
                prod.token_major(ht)
            for c in range(2):
                prod.token_major(oat)
            for c in range(2):
                prod.token_major(obt)
            stage.end()
            turn_pe(pe, va, KD)
            stage.end()
            for c in range(2):
                prod.token_major(ht)
            stage.end()
            stage.end()
            block2_pe(pe, stage, prod)
            moe_pe(pe, stage)
            tail_pe(pe, stage, prod)

        @block.scalar
        def _(act):
            act_steps[0] = Steps(act, S["act_step"])
            stage = Stage(act, S["stage"])
            moves = Moves(act, 0)
            act.wait_ge(S["x_in"], 16)
            act.wait_ge(S["const_in"], 16)
            norm_act(act, xs, [(0, D)], extra[:, 0, :])
            stage.end()
            moves.take(24, lambda i, b: copy_out(act, fm[:, i, :], ps[:, b, 0:T]))
            moves.take(4, lambda i, b: copy_out(act, va[:, i % 2, BANK * (i // 2):BANK * (i // 2) + BANK], ps[:, b, :]))
            stage.end()
            nc.scalar.activation(fm[:, 16:24, :], fm[:, 16:24, :], ACT.Silu).then_inc(S["silu_za"], 1)
            attention_act(act, 0)
            stage.end()
            moves.take(24, lambda i, b: copy_out(act, fm[:, i, :], ps[:, b, 0:T]))
            moves.take(4, lambda i, b: copy_out(act, zb[:, i % 2, BANK * (i // 2):BANK * (i // 2) + BANK], ps[:, b, :]))
            stage.end()
            gdn_act(act, stage)
            moves.take(8, lambda i, b: nc.scalar.activation(gates[:, i // 4, i % 2, BANK * (i % 4 // 2):BANK * (i % 4 // 2) + BANK], ps[:, b, :], ACT.Sigmoid), whole=True)
            moves.skip(8)
            stage.end()
            stage.end()
            moves.take(4, lambda i, b: copy_out(act, va[:, i % 2, BANK * (i // 2):BANK * (i // 2) + BANK], ps[:, b, :]))
            stage.end()
            norm_act(act, va, [(0, D)], extra[:, 0, :])
            stage.end()
            block2_act(act, stage, moves)
            moe_act(act, stage)
            tail_act(act, stage, moves)

        @block.vector
        def _(dve):
            dve_steps[0] = Steps(dve, S["dve_step"])
            stage = Stage(dve, S["stage"])
            moves = Moves(dve, 1)
            dve.wait_ge(S["small_in"], SMALL_LOADS * 16)
            norm_dve(dve, xs, [(0, D)], oat_tm)
            turn_dve(dve, ht, KD, w_pre)
            dve.wait_ge(S["conv_turned"], 1)
            nc.vector.tensor_copy(cw[:, :], ps[:, 4, 0:96])
            stage.end()
            moves.take(24, lambda i, b: copy_out(dve, fm[:, i, :], ps[:, b, 0:T]))
            moves.take(4, lambda i, b: copy_out(dve, va[:, i % 2, BANK * (i // 2):BANK * (i // 2) + BANK], ps[:, b, :]))
            stage.end()
            cosb = con("cos", slice(0, 32)).unsqueeze(1).to_broadcast([32, 2, T])
            sinb = con("sin", slice(0, 32)).unsqueeze(1).to_broadcast([32, 2, T])
            r1, r2 = (extra[0:32, 1, 512 * i:512 * i + 512].rearrange("p (a b) -> p a b", a=2) for i in range(2))
            for m in range(8):
                dve.wait_ge(S["rotated"], m + 1)
                nc.vector.tensor_tensor(r1, ps[0:32, m, :].rearrange("p (a b) -> p a b", a=2), sinb, ALU.mult)
                dve_step(nc.vector.tensor_tensor(r2, fm[0:32, 2 * m:2 * m + 2, :], cosb, ALU.mult))
                nc.vector.tensor_tensor(fm[0:32, 2 * m:2 * m + 2, :], r1, r2, ALU.add).then_inc(S["roped"], 1)
                dve.wait_ge(S["roped"], m + 1)

            def take_a(h):
                if h == 0:
                    dve.wait_ge(S["silu_za"], 1)
                dve.wait_ge(S["head_out"], h + 1)
                nc.vector.tensor_tensor(oat[:, h, :], ps[:, 4 + h % 2, 0:T], fm[:, 16 + h, :], ALU.mult).then_inc(S["head_taken"], 1)

            attention_dve(dve, 0, float(P) ** -0.5, take_a)
            stage.end()
            moves.take(24, lambda i, b: copy_out(dve, fm[:, i, :], ps[:, b, 0:T]))
            moves.take(4, lambda i, b: copy_out(dve, zb[:, i % 2, BANK * (i // 2):BANK * (i // 2) + BANK], ps[:, b, :]))
            dve.wait_ge(S["bd_logits"], 1)
            nc.vector.tensor_copy(bd[:, 0, :].rearrange("p (t h) -> p t h", t=NT), ps[:, 7, 0:32].rearrange("p (t a h) -> p t a h", t=NT, a=2)[:, :, 0, :])
            nc.vector.tensor_copy(bd[:, 1, :].rearrange("p (t h) -> p t h", t=NT), ps[:, 7, 0:32].rearrange("p (t a h) -> p t a h", t=NT, a=2)[:, :, 1, :])
            stage.end()
            gdn_dve(dve, stage)
            moves.skip(8)
            dve.wait_ge(S["moved0"], moves.u // 2)
            dve.wait_ge(S["moved1"], moves.u // 2)

            def gated(i, b):
                t, c = i % 2, BANK * (i % 4 // 2)
                return nc.vector.tensor_tensor((va, zb)[i // 4][:, t, c:c + BANK], ps[:, b, :], gates[:, i // 4, t, c:c + BANK], ALU.mult)

            moves.take(8, gated, whole=True)
            dve.wait_ge(S["moved1"], moves.u // 2)
            nc.vector.tensor_tensor(va[:, :, :], va[:, :, :], zb[:, :, :], ALU.add)
            stage.end()
            turn_dve(dve, ht, KD)
            stage.end()
            moves.take(4, lambda i, b: copy_out(dve, va[:, i % 2, BANK * (i // 2):BANK * (i // 2) + BANK], ps[:, b, :]))
            stage.end()
            norm_dve(dve, va, [(0, D)], None)
            dve.wait_ge(S["row_in"], 16)
            for t in range(NT):
                dve_step(nc.vector.scalar_tensor_tensor(out=va[:, t, :], in0=va[:, t, :], scalar=ssq[:, t:t + 1], in1=extra[:, 2, 0:D], op0=ALU.mult, op1=ALU.mult))
            nc.vector.tensor_tensor(xs[:, :, :], xs[:, :, :], va[:, :, :], ALU.add)
            stage.end()
            block2_dve(dve, stage, moves)
            moe_dve(dve, stage)
            tail_dve(dve, stage, moves)


_INS = ["x", "pre_norm_w", "w_in", "conv_w", "a_log", "dt_bias", "gdn_norm_w", "w_branch_a", "w_branch_b", "w_out",
        "post_norm_w", "p_2", "positions_2", "w_in_2", "g_attn_2", "g_cq_2", "w_uq_2", "g_ckv_2", "w_ukv_2",
        "g_out_mla_2", "g_out_sb_2", "w_o_2", "g_moe_2", "w_router_2", "b_router_2", "w_gu_2", "b_gu_2", "w_dn_2",
        "b_dn_2", "g_ple_2", "w_ple_gate_2", "w_ple_proj_2", "g_final_2"]
_OUT = ((1, T, D), "float32")


def kernel(**inputs):
    import numpy as _np
    import concourse.bacc as _bacc
    from concourse import mybir as _mybir
    from concourse.bass_utils import run_bass_kernel_spmd as _run

    nc = _bacc.Bacc("TRN2", target_bir_lowering=False, num_devices=1)
    arrays, tensors = {}, {}
    for name in _INS + ["const"]:
        a = constants()[0] if name == "const" else _np.ascontiguousarray(inputs[name])
        arrays[f"in_{name}_dram"] = a
        tensors[name] = nc.dram_tensor(f"in_{name}_dram", a.shape, _mybir.dt.from_np(a.dtype), kind="ExternalInput").ap()
    shape, dtype = _OUT
    out = nc.dram_tensor("out_0_dram", shape, _mybir.dt.from_np(_np.dtype(dtype)), kind="ExternalOutput").ap()
    hybrid_two_block_kernel(nc, tensors, out)
    r = _run(nc, [arrays], core_ids=[0])
    return r.results[0]["out_0_dram"]
```

```python
from contextlib import ExitStack

import numpy as np

import concourse.bass as bass
from concourse import mybir

P = 128
T = 256
NT = T // P
D = 1024
KD = D // P
HEADS = 8
CHUNK = 64
CONV = 4
BANK = 512
NEXP = 32
CAP = 64
LAST_STAGE = 27
SMALL_LOADS = 15
MAXROUND = T // CAP
MAXOVER = 1024 // CAP
QR, KVR = 384, 256
TWO_PI = 2.0 * np.pi
EPS = 1e-6
NEG = -1e30

F32 = mybir.dt.float32
BF16 = mybir.dt.bfloat16
F32R = mybir.dt.float32r
I32 = mybir.dt.int32
U32 = mybir.dt.uint32
ALU = mybir.AluOpType
ACT = mybir.ActivationFunctionType
AX = mybir.AxisListType.X

PI_A, PI_B = 6.28125, 0.00193023681640625
PI_C = TWO_PI - PI_A - PI_B
PI_IN = 3.1415925
ROUND = 1.5 * 2.0 ** 23

LEVELS = (1, 2, 4, 8, 16, 32)


def constants():
    r, c = np.arange(P)[:, None], np.arange(P)[None, :]
    same = (r // CHUNK) == (c // CHUNK)
    causal = np.where(c <= r, 0.0, NEG)
    parts = {
        "ident": r == c,
        "ones": np.ones((P, P)),
        "causal": np.concatenate([causal, np.zeros((P, P)), causal], 1),
        "strict": np.concatenate([r < c, np.ones((P, P)), r < c], 1),
        "upto": same & (r <= c),
        "chunk": same,
        "later": r > c,
        "earlier": r < c,
    }
    for s in LEVELS:
        parts[f"level{s}"] = (c // s % 2 == 1) & (r // s == c // s - 1)
    rot = np.zeros((P, 32))
    for base in (0, 64):
        for i in range(16):
            rot[base + 16 + i, i] = -1.0
            rot[base + i, 16 + i] = 1.0
    parts["rot"] = rot
    half = np.arange(P) % 16
    inv1 = np.power(np.float32(500000.0), -half.astype(np.float32) * np.float32(2.0 / 32)).astype(np.float32)
    ang = np.arange(T, dtype=np.float32)[None, :] * inv1[:, None]
    parts["cos"], parts["sin"] = np.cos(ang), np.sin(ang)
    parts["freq"] = np.power(np.float32(10000.0), -(2 * half).astype(np.float32) / np.float32(32))[:, None]
    parts["slots"] = np.broadcast_to(np.arange(CAP * (MAXROUND + 1)), (P, CAP * (MAXROUND + 1)))
    parts["row"] = np.arange(P)[:, None]
    parts["small"] = np.broadcast_to([EPS, P * EPS, 1.0, CAP, 2.0 * CAP, 3.0 * CAP], (P, 6))
    parts["codes"] = np.concatenate([np.arange(P)[:, None] + NEXP * k for k in (1, 2, 3)], 1)
    parts["bsel"] = (r % NEXP == c[:, :NEXP]) & (r < 3 * NEXP)
    at, cols = 0, {}
    for name, a in parts.items():
        cols[name] = (at, at + a.shape[1])
        at += a.shape[1]
    return np.concatenate([np.asarray(a, np.float32) for a in parts.values()], 1), cols


class Steps:

    def __init__(self, eng, sem):
        self.eng, self.sem, self.n = eng, sem, 0

    def __call__(self, ins):
        self.n += 1
        ins.then_inc(self.sem, 1)
        self.eng.wait_ge(self.sem, self.n)


class Stage:

    def __init__(self, eng, sem):
        self.eng, self.sem, self.n = eng, sem, 0

    def end(self):
        self.n += 1
        self.eng.drain().then_inc(self.sem, 1)
        self.eng.wait_ge(self.sem, 4 * self.n)


def hybrid_two_block_kernel(nc, I, out):
    const_np, CC = constants()
    with ExitStack() as ctx:
        def sb(name, shape, dt=F32):
            return ctx.enter_context(nc.sbuf_tensor(name, shape, dt))

        def sb_both(name, shape):
            at = nc.sbuf_base + -nc.sbuf_base % 32
            plain = sb(name, shape)
            return plain, nc.alloc_sbuf_tensor_at(name + "_r", shape, F32R, offset=at)

        class Sems(dict):
            def __missing__(self, name):
                self[name] = ctx.enter_context(nc.semaphore(name))
                return self[name]

        S = Sems()

        ring, ring_r = sb_both("ring", [P, 6, 4096])
        fm, fm_r = sb_both("fm", [P, 24, T])
        va, va_r = sb_both("va", [P, NT, D])
        zb, zb_r = sb_both("zb", [P, NT, D])
        oat, oat_r = sb_both("oat", [P, HEADS, T])
        xs = sb("xs", [P, NT, D])
        ht, ht_r = sb_both("ht", [P, KD, T])
        extra, extra_r = sb_both("extra", [P, 3, 2048])
        cst = sb("cst", [P, const_np.shape[1]])
        cw = sb("cw", [P, 96])
        wbd = sb("wbd", [P, KD, 16])
        cols = sb("cols", [P, 64])
        hsc = sb("hsc", [P, 16])
        ssq = sb("ssq", [P, 32])
        rsd = sb("rsd", [P, 32])
        nmx = sb("nmx", [P, HEADS, 2])
        sums = sb("sums", [P, HEADS, 2])
        rsum = sb("rsum", [P, HEADS, 2])
        bd = sb("bd", [P, 6, NT * HEADS])
        ps = ctx.enter_context(nc.psum_tensor("ps", [P, 8, BANK], F32))

        def con(name, rows=slice(0, P)):
            a, b = CC[name]
            return cst[rows, a:b]

        def con_at(name, first, n):
            return cst[:, bass.ds(first + CC[name][0], n)]

        def arena(i):
            return ring[:, 2 + i // 2, 2048 * (i % 2):2048 * (i % 2) + 2048]

        ident = con("ident")
        gates = fm[:, 0:16, :].rearrange("p a b -> p (a b)").rearrange("p (g t d) -> p g t d", g=2, t=NT)
        w_pre, w_gdn, g_attn, g_cq, g_ckv = (cols[:, a:b] for a, b in ((0, 8), (8, 9), (10, 18), (18, 21), (21, 23)))
        g_mix, g_moe, g_ple = (cols[:, a:b] for a, b in ((24, 32), (32, 40), (40, 48)))
        brow = sb("brow", [P, NEXP])
        posi = sb("posi", [P, T], I32)

        w_in = I["w_in"][0].rearrange("(p k) n -> p k n", k=KD)

        def pk_rows(name, k):
            return I[name][0].rearrange("(p k) n -> p k n", k=k)

        def head_rows(name):
            return I[name][0].rearrange("(h p) n -> p h n", p=P)

        class Chunk:
            pass

        plan = []
        slot_user, slot_loads = {}, {}

        def stream(src, c0, units, n=BANK, k=KD, split=True):
            c = Chunk()
            g = c.g = len(plan)
            c.k, c.n, c.split = k, n, split
            c.first = plan[-1].done if plan else 0
            c.done = c.first + units
            c.slot = (g + 2) % 3 if split else g % 2
            c.high_slot = 3 + (g + 1) % 3 if split else None
            c.free = slot_user.get(c.slot)
            c.high_free = slot_user.get(c.high_slot)
            slot_user[c.slot] = c.done
            if split:
                slot_user[c.high_slot] = c.done
            c.load = slot_loads[c.slot] = slot_loads.get(c.slot, 0) + 1
            c.flat = ring[:, c.slot, 0:k * n]
            c.dst = c.flat.rearrange("p (k n) -> p k n", k=k)
            c.src = src[:, :, c0:c0 + n]
            c.nth = sum(q.split for q in plan) + 1
            plan.append(c)

        for c in (0, 1, 2, 3, 6, 7):
            stream(w_in, BANK * c, 4)
        for c in (4, 5):
            stream(w_in, BANK * c, 2)
        for c in range(8, 14):
            stream(w_in, BANK * c, 4)
        for c in (14, 15):
            stream(w_in, BANK * c, 2)
        after_gdn = len(plan)
        for c in range(4):
            stream(w_in, 16 * BANK + 16 + BANK * c, 2)
        for name in ("w_branch_a", "w_branch_b"):
            for c in (0, 1):
                stream(head_rows(name), BANK * c, 2)
        for c in (0, 1):
            stream(pk_rows("w_out", KD), BANK * c, 2)
        w_in2 = pk_rows("w_in_2", KD)
        stream(w_in2, 0, 2, QR)
        stream(w_in2, QR, 3, KVR + 32)
        stream(w_in2, QR + KVR + 32, 4)
        stream(w_in2, QR + KVR + 32 + BANK, 4)
        stream(w_in2, QR + KVR + 32 + 2 * BANK, 2)
        stream(pk_rows("w_uq_2", QR // P), 0, 8, 96 * HEADS, QR // P, split=False)
        stream(pk_rows("w_ukv_2", KVR // P), 0, 10, P * HEADS, KVR // P, split=False)
        for c in (0, 1):
            stream(pk_rows("w_o_2", KD), BANK * c, 2, split=False)

        before_experts = len(plan)
        for c in (0, 1):
            stream(pk_rows("w_ple_gate_2", KD), BANK * c, 2, split=False)
        stream(pk_rows("w_ple_proj_2", 2), 0, 4, D, 2, split=False)

        block = ctx.enter_context(nc.Block())

        def bank(b, lo=0, hi=BANK):
            return ps[:, b, lo:hi]

        class Products:

            def __init__(self, pe):
                self.pe, self.g, self.u = pe, 0, 0

            def chunk(self, units, a):
                c = plan[self.g]
                if c.split:
                    self.pe.wait_ge(S["split_low"], c.nth)
                    high, low = (ring_r[:, q, 0:c.k * c.n].rearrange("p (k n) -> p k n", k=c.k) for q in (c.high_slot, c.slot))
                    terms = ((high, a[0]), (high, a[1]), (low, a[0]))
                else:
                    self.pe.wait_ge(S[f"chunk_in{c.slot}"], 16 * c.load)
                    terms = ((c.dst, a),)
                for r0, rows, width, lhs, rhs in units:
                    if self.u >= 8:
                        self.pe.wait_ge(S[f"moved{self.u % 2}"], (self.u - 8) // 2 + 1)
                    for j in range(c.k):
                        for i, (w, x) in enumerate(terms):
                            last = self.pe.matmul(ps[r0:r0 + rows, self.u % 8, 0:width], lhs(w, x, j), rhs(w, x, j),
                                                  start=(j == 0 and i == 0), stop=(j == c.k - 1 and i == len(terms) - 1))
                    last.then_inc(S["unit"], 1)
                    self.u += 1
                assert self.u == c.done
                self.g += 1

            def fm_units(self, tiles=4, m=P, at=0, step=None):
                return [(0, m, T, lambda w, x, j, f=f: w[:, j, at + (step or m) * f:at + (step or m) * f + m],
                         lambda w, x, j: x[:, j, :]) for f in range(tiles)]

            def tm_units(self, width=BANK, cols=lambda w, j: w[:, j, :]):
                return [(0, P, width, lambda w, x, j, t=t: x[:, j, P * t:P * t + P], lambda w, x, j: cols(w, j)) for t in range(NT)]

            def feature_major(self, a, tiles=4):
                self.chunk(self.fm_units(tiles), a)

            def token_major(self, a, n=BANK):
                self.chunk(self.tm_units(n), a)

        class Moves:

            def __init__(self, eng, parity):
                self.eng, self.parity, self.u = eng, parity, 0

            def split(self, g):
                c = plan[g]
                high_r, low_r = (ring_r[:, q, 0:c.k * c.n] for q in (c.high_slot, c.slot))
                if self.parity == 0:
                    self.eng.wait_ge(S[f"chunk_in{c.slot}"], 16 * c.load)
                    if c.high_free:
                        self.eng.wait_ge(S["unit"], c.high_free)
                    nc.scalar.activation(high_r, c.flat, ACT.Copy).then_inc(S["split_high"], 1)
                else:
                    self.eng.wait_ge(S["split_high"], c.nth)
                    nc.vector.tensor_tensor(low_r, c.flat, high_r.bitcast(F32), ALU.subtract).then_inc(S["split_low"], 1)

            def ahead(self):
                for c in plan:
                    if c.first == self.u and c.g + 2 < len(plan) and plan[c.g + 2].split and not c.g < after_gdn <= c.g + 2:
                        self.split(c.g + 2)

            def take(self, n, move, whole=False):
                for i in range(n):
                    self.ahead()
                    if whole or self.u % 2 == self.parity:
                        self.eng.wait_ge(S["unit"], self.u + 1)
                        move(i, self.u % 8).then_inc(S[f"moved{self.u % 2}"], 1)
                    self.u += 1

            def skip(self, n):
                for _ in range(n):
                    self.ahead()
                    self.u += 1

        def copy_out(eng, dst, src):
            if eng is nc.scalar:
                return nc.scalar.activation(dst, src, ACT.Copy)
            return nc.vector.tensor_copy(dst, src)

        def as_token_major(buf):
            return buf.rearrange("p a b -> p (a b)").rearrange("p (t d) -> p t d", t=NT)

        oat_tm = as_token_major(oat[:, :, :])

        norm_calls = {"act": 0, "dve": 0, "pe": 0}

        def norm_act(act, src, segs, junk, t0=0):
            n = norm_calls["act"]; norm_calls["act"] += 1
            for t in range(NT):
                for s, (c0, w) in enumerate(segs):
                    last = nc.scalar.activation(junk[:, 0:w], src[:, t, c0:c0 + w], ACT.Square,
                                                accum_out=ssq[:, t * len(segs) + s:t * len(segs) + s + 1])
                    act_step(last)
            m = NT * len(segs)
            w = segs[0][1]
            nc.scalar.activation(rsd[:, 0:m], ssq[:, 0:m], ACT.Sqrt, scale=1.0 / w,
                                 bias=con("small")[:, 0:1]).then_inc(S["rms_root"], 1)

        def norm_dve(dve, src, segs, dst):
            n = norm_calls["dve"]; norm_calls["dve"] += 1
            m = NT * len(segs)
            dve.wait_ge(S["rms_root"], n + 1)
            dve_step(nc.vector.reciprocal(ssq[:, 0:m], rsd[:, 0:m]))
            if dst is None:
                return
            for t in range(NT):
                for s, (c0, w) in enumerate(segs):
                    i = t * len(segs) + s
                    last = nc.vector.tensor_scalar(dst[:, t, c0:c0 + w], src[:, t, c0:c0 + w], ssq[:, i:i + 1], None, ALU.mult)
            last.then_inc(S["normed"], 1)

        turn_calls = {"pe": 0, "dve": 0}

        def turn_pe(pe, src, K, b0=0):
            for k in range(K):
                for t in range(NT):
                    last = pe.transpose(ps[:, b0 + k // 2, (k % 2) * T + P * t:(k % 2) * T + P * t + P],
                                        src[:, t, k:k + K * (P - 1) + 1:K], ident)
            last.then_inc(S["turned"], 1)
            turn_calls["pe"] += 1

        def turn_dve(dve, dst, K, w_col=None, b0=0, done=None, low=None):
            turn_calls["dve"] += 1
            dve.wait_ge(S["turned"], turn_calls["dve"])
            for k in range(K):
                src = ps[:, b0 + k // 2, (k % 2) * T:(k % 2) * T + T]
                if low is not None:
                    split_dve(dst[:, k, :], low[:, k, :], src, con("ones")[:, 0:1] if w_col is None else w_col[:, k:k + 1])
                elif w_col is None:
                    last = nc.vector.tensor_copy(dst[:, k, :], src)
                else:
                    last = nc.vector.tensor_scalar(dst[:, k, :], src, w_col[:, k:k + 1], None, ALU.mult)
            if done:
                last.then_inc(S[done], 1)

        def split_dve(high_r, low_r, src, w):
            dve_step(nc.vector.tensor_scalar(high_r, src, w, None, ALU.mult))
            nc.vector.scalar_tensor_tensor(out=low_r, in0=src, scalar=w, in1=high_r.bitcast(F32), op0=ALU.mult, op1=ALU.subtract)

        def as_feature_major(buf):
            return buf.rearrange("p t d -> p (t d)").rearrange("p (k n) -> p k n", k=KD)

        ht_low_r, ht_low2_r = (as_feature_major(b[:, :, :]) for b in (va_r, zb_r))
        ht_parts, ht_parts2 = (ht_r, ht_low_r), (ht_r, ht_low2_r)

        dve_steps, act_steps = [None], [None]

        def dve_step(ins):
            dve_steps[0](ins)

        def act_step(ins):
            act_steps[0](ins)

        sc_buf, pt_buf = [extra[:, 0, 384 * i:384 * i + 384] for i in range(2)], [extra[:, 0, 768 + 384 * i:1152 + 384 * i] for i in range(2)]

        def attention_pe(pe, h0, q, k, out_product):
            for i in range(HEADS + 2):
                if i < HEADS:
                    if h0 + i >= 2:
                        pe.wait_ge(S["scores_read"], h0 + i - 1)
                    b = ps[:, i % 2, :]
                    pe.matmul(b[:, 0:P], q(i)[:, 0:P], k(i)[:, 0:P], start=True, stop=True)
                    pe.matmul(b[:, P:3 * P], q(i)[:, P:T], k(i)[:, 0:T], start=True, stop=True).then_inc(S["scores"], 1)
                if 1 <= i <= HEADS:
                    h = i - 1
                    pe.wait_ge(S["weights"], h0 + h + 1)
                    if h0 + h >= 2:
                        pe.wait_ge(S["weights_t"], h0 + h - 1)
                    for j in range(3):
                        last = pe.transpose(ps[:, 2 + h % 2, P * j:P * j + P], sc_buf[h % 2][:, P * j:P * j + P], ident)
                    last.then_inc(S["weights_turned"], 1)
                if i >= 2:
                    h = i - 2
                    pe.wait_ge(S["weights_t"], h0 + h + 1)
                    out_product(h, pt_buf[h % 2]).then_inc(S["head_out"], 1)

        def attention_act(act, h0):
            for i in range(HEADS + 1):
                if i < HEADS:
                    act.wait_ge(S["maxima"], h0 + i + 1)
                    for t, (a, b) in enumerate(((0, P), (P, 3 * P))):
                        last = nc.scalar.activation(sc_buf[i % 2][:, a:b], sc_buf[i % 2][:, a:b], ACT.Exp,
                                                    bias=nmx[:, i, t:t + 1], accum_out=sums[:, i, t:t + 1])
                    last.then_inc(S["exps"], 1)
                if i >= 1:
                    h = i - 1
                    act.wait_ge(S["weights_turned"], h0 + h + 1)
                    if h0 + h >= 2:
                        act.wait_ge(S["head_out"], h0 + h - 1)
                    nc.scalar.activation(pt_buf[h % 2], ps[:, 2 + h % 2, 0:3 * P], ACT.Copy).then_inc(S["weights_t"], 1)

        def attention_dve(dve, h0, scale, take_out):
            for i in range(HEADS + 2):
                if i < HEADS:
                    dve.wait_ge(S["scores"], h0 + i + 1)
                    if h0 + i >= 2:
                        dve.wait_ge(S["weights_turned"], h0 + i - 1)
                    nc.vector.scalar_tensor_tensor(out=sc_buf[i % 2], in0=ps[:, i % 2, 0:3 * P], scalar=scale,
                                                   in1=con("causal"), op0=ALU.mult, op1=ALU.add).then_inc(S["scores_read"], 1)
                    dve.wait_ge(S["scores_read"], h0 + i + 1)
                    dve_step(nc.vector.tensor_reduce(nmx[:, i, 0:1], sc_buf[i % 2][:, 0:P], AX, ALU.max, negate=True))
                    nc.vector.tensor_reduce(nmx[:, i, 1:2], sc_buf[i % 2][:, P:3 * P], AX, ALU.max, negate=True).then_inc(S["maxima"], 1)
                if 1 <= i <= HEADS:
                    h = i - 1
                    dve.wait_ge(S["exps"], h0 + h + 1)
                    dve_step(nc.vector.reciprocal(rsum[:, h, :], sums[:, h, :]))
                    b = sc_buf[h % 2]
                    nc.vector.tensor_scalar(b[:, 0:P], b[:, 0:P], rsum[:, h, 0:1], None, ALU.mult)
                    nc.vector.tensor_scalar(b[:, P:3 * P], b[:, P:3 * P], rsum[:, h, 1:2], None, ALU.mult).then_inc(S["weights"], 1)
                if i >= 2:
                    take_out(i - 2)

        bt, gd, Gc, Gd, eG, bG = (bd[:, i, :] for i in range(6))
        gl = sb("gl", [P, 4, HEADS])
        SYS = NT * HEADS

        def systems(buf):
            return buf.rearrange("p (s i) -> p s i", s=SYS)

        kbg, kdec, vbt = (systems(extra[:, i, :]) for i in range(3))
        egr, dk, mt, qkt = (systems(arena(i)) for i in range(4))
        xi, xt, yy, bb = (systems(arena(i)) for i in range(4, 8))
        nwt, uu = yy, bb
        vnew = arena(2)[:, 0:D].rearrange("p (h i) -> p h i", h=HEADS)
        state = arena(2)[:, D:2 * D].rearrange("p (h i) -> p h i", h=HEADS)
        oo = xi
        obt_r, obt_low_r = (extra_r[:, i, :].rearrange("p (h n) -> p h n", h=HEADS) for i in range(2))
        oat_high_r = fm_r[:, 16:24, :]

        def four(b):
            return ps[:, b, :].rearrange("p (s i) -> p s i", s=4)

        def over4(col, g):
            return col[:, 4 * g:4 * g + 4].unsqueeze(2).to_broadcast([P, 4, P])

        def conv_act(act, c, moves):
            act.wait_ge(S["moved0"], moves.u // 2)
            act.wait_ge(S["moved1"], moves.u // 2)
            for i in range(4 * c, 4 * c + 4):
                last = nc.scalar.activation(conv_sum(i), fm[:, i, :], ACT.Copy, scale=cw[:, 72 + i:73 + i])
            last.then_inc(S["tap3"], 1)

        def conv_dve(dve, c):
            dve.wait_ge(S["tap3"], c + 1)
            for back in (1, 2, 3):
                for i in range(4 * c, 4 * c + 4):
                    k = 24 * (3 - back) + i
                    last = nc.vector.scalar_tensor_tensor(out=conv_sum(i)[:, back:T], in0=fm[:, i, 0:T - back], scalar=cw[:, k:k + 1],
                                                          in1=conv_sum(i)[:, back:T], op0=ALU.mult, op1=ALU.add)
                if back < 3:
                    dve_step(last)
            last.then_inc(S["conv"], 1)

        def conv_sum(i):
            return extra[:, i // 8, T * (i % 8):T * (i % 8) + T]

        def wide(buf):
            return buf.rearrange("p (c n) -> p c n", c=HEADS)

        def seen_by(t, h):
            return lambda base: fm[:, base + h, P * t:P * t + P]

        def gdn_pool(pool, stage):
            stage.end()
            pool.wait_ge(S["decay"], 1)
            nc.gpsimd.tensor_tensor(dk, dk, con("upto").unsqueeze(1).to_broadcast([P, SYS, P]), ALU.mult).then_inc(S["decay_masked"], 1)
            pool.wait_ge(S["glast"], 1)
            nc.gpsimd.tensor_tensor(egr.rearrange("p (t h) i -> p h t i", t=NT), egr.rearrange("p (t h) i -> p h t i", t=NT),
                                    fm[:, 0:8, :].rearrange("p h (t i) -> p h t i", t=NT), ALU.mult)
            stage.end()
            for n in range(len(LEVELS) * 4):
                l, g = n // 4, n % 4
                if n >= 8:
                    pool.wait_ge(S["y_ps"], n - 7)
                elif n >= 4:
                    pool.wait_ge(S["x_done"], n - 3)
                nc.gpsimd.tensor_tensor(bb[:, 4 * g:4 * g + 4, :], mt[:, 4 * g:4 * g + 4, :],
                                        con(f"level{LEVELS[l]}").unsqueeze(1).to_broadcast([P, 4, P]), ALU.mult).then_inc(S["b_ready"], 1)
            stage.end()
            nc.gpsimd.memset(arena(2), 0.0).then_inc(S["zeroed"], 1)
            stage.end()
            stage.end()

        def gdn_pe(pe, stage):
            for G in range(2):
                pe.wait_ge(S["squares"], G + 1)
                for s in range(SYS):
                    t, h = s // HEADS, s % HEADS
                    last = pe.matmul(ps[:, 0, SYS * G + s:SYS * G + s + 1], wide(arena(3 + G))[:, h, P * t:P * t + P], con("ones")[:, 0:1], start=True, stop=True)
            last.then_inc(S["sq_sums"], 1)
            pe.wait_ge(S["scales"], 1)
            for G in range(2):
                for h in range(HEADS):
                    for t in range(NT):
                        c = SYS * G + HEADS * t + h
                        last = pe.matmul(ps[:, 4 * G + h // 2, T * (h % 2) + P * t:T * (h % 2) + P * t + P], rsd[:, c:c + 1].to_broadcast([P, P]), ident,
                                         start=True, stop=True)
                last.then_inc(S["scale_rows"], 1)
            stage.end()
            for t in range(NT):
                cs = slice(HEADS * t, HEADS * t + HEADS)
                pe.matmul(ps[:, 0, HEADS * t:HEADS * t + HEADS], con("upto"), gd[:, cs], start=True, stop=True)
                last = pe.matmul(ps[:, 0, 16 + HEADS * t:16 + HEADS * t + HEADS], con("chunk"), gd[:, cs], start=True, stop=True)
            last.then_inc(S["g_sums"], 1)
            for s in range(SYS):
                t, h = s // HEADS, s % HEADS
                last = pe.transpose(four(4 + s // 4)[:, s % 4, :], seen_by(t, h)(8), ident)
                if s % 4 == 3:
                    last.then_inc(S["k_turned"], 1)
            pe.wait_ge(S["g_read"], 1)
            for s in range(SYS):
                t, h = s // HEADS, s % HEADS
                last = pe.transpose(four(s // 4)[:, s % 4, :], seen_by(t, h)(16), ident)
                if s % 4 == 3:
                    last.then_inc(S["v_turned"], 1)
            for s in range(SYS):
                if s % 4 == 0:
                    pe.wait_ge(S["k_read"], s // 4 + 1)
                last = pe.matmul(four(4 + s // 4)[:, s % 4, :], gd[:, s:s + 1].to_broadcast([P, P]), con("upto"), start=True, stop=True)
                if s % 4 == 3:
                    last.then_inc(S["g_rows"], 1)
            for s in range(SYS):
                if s % 4 == 0:
                    pe.wait_ge(S["v_read"], s // 4 + 1)
                last = pe.matmul(four(s // 4)[:, s % 4, :], bt[:, s:s + 1].to_broadcast([P, P]), ident, start=True, stop=True)
            last.then_inc(S["beta_rows"], 1)
            for s in range(SYS):
                t, h = s // HEADS, s % HEADS
                if s % 4 == 0:
                    pe.wait_ge(S["rows_read_act"], s // 4 + 1)
                    pe.wait_ge(S["rows_read_dve"], s // 4 + 1)
                last = pe.matmul(four(4 + s // 4)[:, s % 4, :], seen_by(t, h)(8), seen_by(t, h)(8), start=True, stop=True)
                if s % 4 == 3:
                    last.then_inc(S["kk"], 1)
            for s in range(SYS):
                t, h = s // HEADS, s % HEADS
                if s % 4 == 0:
                    pe.wait_ge(S["kk_read"], s // 4 + 1)
                last = pe.matmul(four(4 + s // 4)[:, s % 4, :], seen_by(t, h)(8), seen_by(t, h)(0), start=True, stop=True)
                if s % 4 == 3:
                    last.then_inc(S["qk"], 1)
            stage.end()
            for l in range(len(LEVELS)):
                for i in range(5):
                    if i < 4 and l > 0:
                        g = i
                        pe.wait_ge(S["b_ready"], 4 * l + g + 1)
                        pe.wait_ge(S["x_done"], 4 * (l - 1) + g + 1)
                        for q in range(4):
                            last = pe.matmul(four(g)[:, q, :], bb[:, 4 * g + q, :], xi[:, 4 * g + q, :], start=True, stop=True)
                        last.then_inc(S["y_ps"], 1)
                    if i >= 1:
                        g = i - 1
                        n = 4 * l + g
                        if n >= 2:
                            pe.wait_ge(S["x_done"], n - 1)
                        if l == 0:
                            pe.wait_ge(S["b_ready"], g + 1)
                            for q in range(4):
                                last = pe.matmul(four(4 + g % 2)[:, q, :], bb[:, 4 * g + q, :], ident, start=True, stop=True)
                        else:
                            pe.wait_ge(S["y_copied"], n - 3)
                            for q in range(4):
                                sys = 4 * g + q
                                if l < len(LEVELS) - 1:
                                    pe.matmul(four(4 + g % 2)[:, q, :], xt[:, sys, :], yy[:, sys, :], start=True, stop=True)
                                last = pe.matmul(four(6 + g % 2)[:, q, :], yy[:, sys, :], xt[:, sys, :], start=True, stop=True)
                        last.then_inc(S["z_ps"], 1)
            stage.end()
            for s in range(SYS):
                last = pe.matmul(four(s // 4)[:, s % 4, :], kbg[:, s, :], xt[:, s, :], start=True, stop=True)
                if s % 4 == 3:
                    last.then_inc(S["w_ps"], 1)
            for s in range(SYS):
                last = pe.matmul(four(4 + s // 4)[:, s % 4, :], xt[:, s, :], vbt[:, s, :], start=True, stop=True)
                if s % 4 == 3:
                    last.then_inc(S["u_ps"], 1)
            pe.wait_ge(S["w_moved"], 4)
            pe.wait_ge(S["u_moved"], 4)
            pe.wait_ge(S["zeroed"], 1)
            for c in range(4):
                t, r = c // 2, CHUNK * (c % 2)
                rows = slice(r, r + CHUNK)

                def at(b, h):
                    return ps[rows, b + h // 4, P * (h % 4):P * (h % 4) + P]

                if c:
                    pe.wait_ge(S["state"], c)
                for h in range(HEADS):
                    last = pe.matmul(at(0, h), nwt[:, HEADS * t + h, rows], state[:, h, :], start=True, stop=True)
                last.then_inc(S["ws"], 1)
                if c:
                    pe.wait_ge(S["o_moved"], c)
                for h in range(HEADS):
                    last = pe.matmul(at(2, h), egr[:, HEADS * t + h, rows], state[:, h, :], start=(h % 4 == 0), stop=False, skip_group_check=True)
                last.then_inc(S["state_read"], 1)
                pe.wait_ge(S["vnew"], c + 1)
                for h in range(HEADS):
                    last = pe.matmul(ps[:, 4 + h // 4, P * (h % 4):P * (h % 4) + P], kdec[rows, HEADS * t + h, :], vnew[rows, h, :], start=True, stop=True)
                last.then_inc(S["kv"], 1)
                for h in range(HEADS):
                    last = pe.matmul(at(2, h), qkt[:, HEADS * t + h, rows], vnew[:, h, :], start=False, stop=True, skip_group_check=True)
                last.then_inc(S["o_ps"], 1)
            stage.end()
            pe.wait_ge(S["o_gated"], 1)
            for s in range(SYS):
                t, h = s // HEADS, s % HEADS
                last = pe.transpose(ps[:, h // 2, T * (h % 2) + P * t:T * (h % 2) + P * t + P], oo[:, s, :], ident)
            last.then_inc(S["o_turned"], 1)
            stage.end()

        def gdn_act(act, stage, moves):
            act.wait_ge(S["abs_z"], 1)
            act_step(nc.scalar.activation(Gd, Gd, ACT.Exp, scale=-1.0))
            nc.scalar.activation(hsc[:, 8:16], hsc[:, 8:16], ACT.Exp)
            nc.scalar.activation(Gd, Gd, ACT.Ln, bias=con("small")[:, 2:3]).then_inc(S["log_part"], 1)
            nc.scalar.activation(bt, bt, ACT.Sigmoid)
            for G in range(2):
                nc.scalar.activation(wide(arena(3 + G)), fm[:, 8 * G:8 * G + 8, :], ACT.Square).then_inc(S["squares"], 1)
            act.wait_ge(S["sq_sums"], 1)
            for G in range(2):
                last = nc.scalar.activation(ssq[:, SYS * G:SYS * G + SYS], ps[:, 0, SYS * G:SYS * G + SYS], ACT.Sqrt,
                                            scale=(float(P), 1.0)[G], bias=con("small")[:, 1 - G:2 - G])
            last.then_inc(S["roots"], 1)
            stage.end()
            act.wait_ge(S["g_read"], 1)
            nc.scalar.activation(eG, Gc, ACT.Exp)
            nc.scalar.activation(Gd, Gd, ACT.Exp).then_inc(S["g_exp"], 1)
            for g in range(4):
                act.wait_ge(S["rows_read_dve"], g + 1)
                nc.scalar.activation(egr[:, 4 * g:4 * g + 4, :], four(4 + g), ACT.Exp).then_inc(S["rows_read_act"], 1)
            act.wait_ge(S["diffs"], 1)
            nc.scalar.activation(dk, dk, ACT.Exp).then_inc(S["decay"], 1)
            stage.end()
            for n in range(4 * (len(LEVELS) - 1)):
                g = n % 4
                act.wait_ge(S["y_ps"], n + 1)
                nc.scalar.activation(yy[:, 4 * g:4 * g + 4, :], four(g), ACT.Copy).then_inc(S["y_copied"], 1)
            stage.end()
            for g in range(4):
                act.wait_ge(S["w_ps"], g + 1)
                nc.scalar.activation(nwt[:, 4 * g:4 * g + 4, :], four(g), ACT.Copy, scale=-1.0).then_inc(S["w_moved"], 1)
            for c in range(4):
                t, r = c // 2, CHUNK * (c % 2)
                act.wait_ge(S["o_ps"], c + 1)
                nc.scalar.activation(oo[r:r + CHUNK, HEADS * t:HEADS * t + HEADS, :],
                                     ps[r:r + CHUNK, 2:4, :].rearrange("p b (h i) -> p (b h) i", h=4), ACT.Copy).then_inc(S["o_moved"], 1)
            stage.end()
            nc.scalar.activation(egr, oo, ACT.Square).then_inc(S["o_sq"], 1)
            nc.scalar.activation(zb[:, :, :], zb[:, :, :], ACT.Silu).then_inc(S["silu_zb"], 1)
            act.wait_ge(S["o_sums"], 1)
            nc.scalar.activation(rsd[:, 0:SYS], ssq[:, 0:SYS], ACT.Sqrt, scale=1.0 / P, bias=con("small")[:, 0:1]).then_inc(S["o_root"], 1)
            moves.split(after_gdn)
            moves.split(after_gdn + 1)
            stage.end()

        def gdn_dve(dve, stage, moves):
            heads2 = [P, NT, HEADS]

            def by_head(a):
                return a.unsqueeze(1).to_broadcast(heads2)

            def th(a):
                return a.rearrange("p (t h) -> p t h", t=NT)

            dve_step(nc.vector.tensor_tensor(th(Gc), th(gd), by_head(hsc[:, 0:8]), ALU.add))
            nc.vector.scalar_tensor_tensor(out=Gd, in0=Gc, scalar=-1.0, in1=Gc, op0=ALU.mult, op1=ALU.max).then_inc(S["abs_z"], 1)
            dve_step(nc.vector.tensor_scalar(Gc, Gc, 0.0, None, ALU.max))
            dve.wait_ge(S["log_part"], 1)
            dve_step(nc.vector.tensor_tensor(Gc, Gc, Gd, ALU.add))
            nc.vector.scalar_tensor_tensor(out=th(gd), in0=th(Gc), scalar=-1.0, in1=by_head(hsc[:, 8:16]), op0=ALU.mult, op1=ALU.mult)
            dve.wait_ge(S["roots"], 1)
            nc.vector.reciprocal(rsd[:, 0:2 * SYS], ssq[:, 0:2 * SYS]).then_inc(S["scales"], 1)
            for G in range(2):
                dve.wait_ge(S["scale_rows"], G + 1)
                nc.vector.tensor_tensor(fm[:, 8 * G:8 * G + 8, :], fm[:, 8 * G:8 * G + 8, :],
                                        ps[:, 4 * G:4 * G + 4, :].rearrange("p b (h n) -> p (b h) n", h=2), ALU.mult)
            stage.end()
            dve.wait_ge(S["g_sums"], 1)
            dve_step(nc.vector.tensor_copy(Gc, ps[:, 0, 0:16]))
            nc.vector.tensor_tensor(Gd, ps[:, 0, 16:32], Gc, ALU.subtract).then_inc(S["g_read"], 1)
            dve.wait_ge(S["g_exp"], 1)
            dve_step(nc.vector.tensor_tensor(bG, bt, eG, ALU.mult))
            for g in range(4):
                dve.wait_ge(S["k_turned"], g + 1)
                nc.vector.tensor_tensor(kbg[:, 4 * g:4 * g + 4, :], four(4 + g), over4(bG, g), ALU.mult)
                nc.vector.tensor_tensor(kdec[:, 4 * g:4 * g + 4, :], four(4 + g), over4(Gd, g), ALU.mult).then_inc(S["k_read"], 1)
            for g in range(4):
                dve.wait_ge(S["v_turned"], g + 1)
                nc.vector.tensor_tensor(vbt[:, 4 * g:4 * g + 4, :], four(g), over4(bt, g), ALU.mult).then_inc(S["v_read"], 1)
            for g in range(4):
                dve.wait_ge(S["g_rows"], g + 1)
                nc.vector.tensor_tensor(dk[:, 4 * g:4 * g + 4, :], four(4 + g), over4(Gc, g), ALU.subtract).then_inc(S["rows_read_dve"], 1)
            dve.wait_ge(S["rows_read_dve"], 4)
            nc.vector.tensor_scalar(dk, dk, 0.0, None, ALU.min).then_inc(S["diffs"], 1)
            dve.wait_ge(S["decay_masked"], 1)
            dve.wait_ge(S["beta_rows"], 1)
            for g in range(4):
                dve.wait_ge(S["kk"], g + 1)
                nc.vector.tensor_tensor(mt[:, 4 * g:4 * g + 4, :], four(4 + g), dk[:, 4 * g:4 * g + 4, :], ALU.mult).then_inc(S["kk_read"], 1)
                dve.wait_ge(S["kk_read"], g + 1)
                nc.vector.tensor_tensor(mt[:, 4 * g:4 * g + 4, :], four(g), mt[:, 4 * g:4 * g + 4, :], ALU.mult)
            for g in range(4):
                dve.wait_ge(S["qk"], g + 1)
                nc.vector.tensor_tensor(qkt[:, 4 * g:4 * g + 4, :], four(4 + g), dk[:, 4 * g:4 * g + 4, :], ALU.mult)
            dve.wait_ge(S["rows_read_act"], 4)
            nc.vector.tensor_copy(gl[:, :, :].rearrange("p (t c) h -> p t h c", t=NT),
                                  egr.rearrange("p (t h) (c i) -> p t h c i", t=NT, c=2)[:, :, :, :, CHUNK - 1]).then_inc(S["glast"], 1)
            stage.end()
            eye4 = ident.unsqueeze(1).to_broadcast([P, 4, P])
            for n in range(4 * len(LEVELS)):
                g = n % 4
                gs = slice(4 * g, 4 * g + 4)
                dve.wait_ge(S["z_ps"], n + 1)
                if n < 4:
                    nc.vector.tensor_tensor(xt[:, gs, :], eye4, bb[:, gs, :], ALU.subtract)
                    last = nc.vector.tensor_tensor(xi[:, gs, :], eye4, four(4 + g % 2), ALU.subtract)
                else:
                    if n < 4 * (len(LEVELS) - 1):
                        nc.vector.tensor_tensor(xi[:, gs, :], xi[:, gs, :], four(4 + g % 2), ALU.subtract)
                    last = nc.vector.tensor_tensor(xt[:, gs, :], xt[:, gs, :], four(6 + g % 2), ALU.subtract)
                last.then_inc(S["x_done"], 1)
            stage.end()
            for g in range(4):
                dve.wait_ge(S["u_ps"], g + 1)
                nc.vector.tensor_copy(uu[:, 4 * g:4 * g + 4, :], four(4 + g)).then_inc(S["u_moved"], 1)
            dve.wait_ge(S["u_moved"], 4)
            dve.wait_ge(S["zeroed"], 1)
            for c in range(4):
                t, r = c // 2, CHUNK * (c % 2)
                rows = slice(r, r + CHUNK)
                dve.wait_ge(S["ws"], c + 1)
                if c:
                    dve.wait_ge(S["o_ps"], c)
                nc.vector.tensor_tensor(vnew[rows, :, :], uu[rows, HEADS * t:HEADS * t + HEADS, :],
                                        ps[rows, 0:2, :].rearrange("p b (h i) -> p (b h) i", h=4), ALU.add).then_inc(S["vnew"], 1)
                dve.wait_ge(S["state_read"], c + 1)
                dve_step(nc.vector.tensor_tensor(state, state, gl[:, c, :].unsqueeze(2).to_broadcast([P, HEADS, P]), ALU.mult))
                dve.wait_ge(S["kv"], c + 1)
                nc.vector.tensor_tensor(state, state, ps[:, 4:6, :].rearrange("p b (h i) -> p (b h) i", h=4), ALU.add).then_inc(S["state"], 1)
                dve.wait_ge(S["state"], c + 1)
            stage.end()
            dve.wait_ge(S["o_sq"], 1)
            nc.vector.tensor_reduce(ssq[:, 0:SYS], egr, AX, ALU.add).then_inc(S["o_sums"], 1)
            dve.wait_ge(S["o_root"], 1)
            dve_step(nc.vector.reciprocal(ssq[:, 0:SYS], rsd[:, 0:SYS]))
            dve_step(nc.vector.tensor_tensor(oo, oo, ssq[:, 0:SYS].unsqueeze(2).to_broadcast([P, SYS, P]), ALU.mult))
            dve.wait_ge(S["silu_zb"], 1)
            nc.vector.tensor_tensor(oo, oo, zb[:, :, :].rearrange("p t (h i) -> p (t h) i", h=HEADS), ALU.mult).then_inc(S["o_gated"], 1)
            moves.split(after_gdn)
            dve.wait_ge(S["o_turned"], 1)
            for h in range(HEADS):
                split_dve(obt_r[:, h, :], obt_low_r[:, h, :], ps[:, h // 2, T * (h % 2):T * (h % 2) + T], w_gdn)
            moves.split(after_gdn + 1)
            stage.end()

        rs = slice(64, 96)
        posf, s_arg, c_arg = (arena(4)[rs, T * i:T * i + T] for i in range(3))
        kr = extra[rs, 2, 1536:1536 + T]
        turns, angle = (arena(5)[rs, T * i:T * i + T] for i in range(2))
        cq, ckv = extra[:, 0, 0:NT * QR].rearrange("p (t n) -> p t n", t=NT), extra[:, 0, 768:768 + NT * KVR].rearrange("p (t n) -> p t n", t=NT)
        cqn, ckvn = extra[:, 1, 0:NT * QR].rearrange("p (t n) -> p t n", t=NT), extra[:, 1, 768:768 + NT * KVR].rearrange("p (t n) -> p t n", t=NT)
        cqt, ckvt = extra[:, 2, 0:768].rearrange("p (k n) -> p k n", k=3), extra[:, 2, 768:1280].rearrange("p (k n) -> p k n", k=2)

        def stick(h, i):
            return arena(h % 4)[:, 384 * i:384 * i + 384]

        def block2_pool(pool, stage):
            for _ in range(14, 19):
                stage.end()
            pool.dma_start(g_row, I["g_moe_2"][0].partition_broadcast(P)).then_inc(S["row_in"], 16)
            pool.dma_start(bdn, I["b_dn_2"][0]).then_inc(S["row_in"], 16)
            for i in range(3):
                pool.dma_start(extra[NEXP * i:NEXP * i + NEXP, 0, :], I["b_gu_2"][0]).then_inc(S["bias_in"], 16)
            for i in range(HEADS + 2):
                if 1 <= i <= HEADS:
                    h = i - 1
                    pool.wait_ge(S["softplus"], h + 1)
                    if h >= 4:
                        pool.wait_ge(S["after"], h - 3)
                    nc.gpsimd.tensor_tensor(stick(h, 2), stick(h, 1), con("strict"), ALU.mult).then_inc(S["masked_sp"], 1)
                if i >= 2:
                    h = i - 2
                    pool.wait_ge(S["stick_exp"], h + 1)
                    nc.gpsimd.tensor_tensor(stick(h, 3), stick(h, 3), con("strict"), ALU.mult).then_inc(S["stick_w"], 1)
            stage.end()
            stage.end()
            stage.end()

        def block2_pe(pe, stage, prod):
            pe.wait_ge(S["normed"], 2)
            turn_pe(pe, oat_tm, KD)
            stage.end()
            prod.token_major(ht_parts2, QR)
            prod.chunk(prod.tm_units(KVR, lambda w, j: w[:, j, 0:KVR]) + prod.fm_units(1, 96, at=KVR - 64), ht_parts2)
            prod.feature_major(ht_parts2)
            prod.feature_major(ht_parts2)
            prod.token_major(ht_parts2)
            stage.end()
            pe.wait_ge(S["normed"], 3)
            turn_pe(pe, cqn, QR // P)
            pe.wait_ge(S["normed"], 4)
            turn_pe(pe, ckvn, KVR // P, 2)
            stage.end()
            prod.chunk(prod.fm_units(8, 96), cqt)
            prod.chunk(prod.fm_units(8, 64, step=P) +
                       prod.tm_units(BANK, lambda w, j: w[:, j, :].rearrange("p (h n) -> p h n", h=HEADS)[:, :, 64:P]), ckvt)
            stage.end()
            for m in range(4):
                pe.matmul(ps[rs, m, :], con("rot", rs), fm[rs, 8 + 2 * m:10 + 2 * m, :], start=True, stop=True).then_inc(S["rotated2"], 1)
            pe.matmul(ps[rs, 4, 0:T], con("rot", rs), kr, start=True, stop=True).then_inc(S["rotated2"], 1)
            pe.wait_ge(S["roped2"], 5)

            def out_mla(h, pt):
                v = [va[:, t, 512 + 64 * h:576 + 64 * h] for t in range(NT)]
                pe.matmul(ps[:, 4, 64 * h:64 * h + 64], pt[:, 0:P], v[0], start=True, stop=True)
                pe.matmul(ps[:, 5, 64 * h:64 * h + 64], pt[:, P:T], v[0], start=True, stop=False)
                return pe.matmul(ps[:, 5, 64 * h:64 * h + 64], pt[:, T:3 * P], v[1], start=False, stop=True)

            attention_pe(pe, HEADS, lambda h: fm[0:96, 8 + h, :], lambda h: fm[0:96, 16 + h, :], out_mla)
            stage.end()
            for i in range(HEADS + 3):
                if i < HEADS:
                    r = slice(64 * (i % 2), 64 * (i % 2) + 64)
                    q, k, b = fm[r, i // 2, :], fm[r, 4 + i // 2, :], ps[:, i % 2, :]
                    if i >= 2:
                        pe.wait_ge(S["z_read"], i - 1)
                    pe.matmul(b[:, 0:T], k[:, 0:P], q[:, 0:T], start=True, stop=True)
                    pe.matmul(b[:, T:3 * P], k[:, P:T], q[:, P:T], start=True, stop=True).then_inc(S["stick_z"], 1)
                if 1 <= i <= HEADS:
                    h = i - 1
                    b, sp = ps[:, 2 + h % 2, :], stick(h, 2)
                    pe.wait_ge(S["masked_sp"], h + 1)
                    if h >= 2:
                        pe.wait_ge(S["after_read"], h - 1)
                    pe.matmul(b[:, 0:T], con("later"), sp[:, 0:T], start=True, stop=False, skip_group_check=True)
                    pe.matmul(b[:, P:T], con("ones"), sp[:, T:3 * P], start=False, stop=False, skip_group_check=True)
                    pe.matmul(b[:, T:3 * P], con("later"), sp[:, T:3 * P], start=False, stop=True, skip_group_check=True).then_inc(S["after"], 1)
                if i >= 3:
                    h = i - 3
                    pe.wait_ge(S["stick_w"], h + 1)
                    w = stick(h, 3)
                    v = [va[:, t, 64 * h:64 * h + 64] for t in range(NT)]
                    pe.matmul(ps[:, 4, 64 * h:64 * h + 64], w[:, 0:P], v[0], start=True, stop=True)
                    pe.matmul(ps[:, 5, 64 * h:64 * h + 64], w[:, P:T], v[0], start=True, stop=False)
                    pe.matmul(ps[:, 5, 64 * h:64 * h + 64], w[:, T:3 * P], v[1], start=False, stop=True).then_inc(S["stick_out"], 1)
            stage.end()
            pe.wait_ge(S["normed"], 5)
            turn_pe(pe, oat_tm, KD)
            stage.end()
            for c in range(2):
                prod.token_major(ht)
            stage.end()

        def block2_act(act, stage, moves):
            norm_act(act, xs, [(0, D)], extra[:, 0, :])
            stage.end()
            moves.take(2, lambda i, b: copy_out(act, cq[:, i, :], ps[:, b, 0:QR]))
            moves.take(2, lambda i, b: copy_out(act, ckv[:, i, :], ps[:, b, 0:KVR]))
            moves.take(1, lambda i, b: copy_out(act, kr, ps[rs, b, 0:T]))
            moves.take(8, lambda i, b: copy_out(act, fm[:, i, :], ps[:, b, 0:T]))
            moves.take(2, lambda i, b: copy_out(act, va[:, i, 0:BANK], ps[:, b, :]))
            stage.end()
            norm_act(act, cq, [(0, QR)], arena(0))
            act.wait_ge(S["normed"], 3)
            norm_act(act, ckv, [(0, KVR)], arena(0))
            act.wait_ge(S["angles"], 1)
            nc.scalar.activation(s_arg, s_arg, ACT.Sin)
            nc.scalar.activation(c_arg, c_arg, ACT.Sin)
            stage.end()
            moves.take(8, lambda i, b: copy_out(act, fm[0:96, 8 + i, :], ps[0:96, b, 0:T]))
            moves.take(8, lambda i, b: copy_out(act, fm[0:64, 16 + i, :], ps[0:64, b, 0:T]))
            moves.take(2, lambda i, b: copy_out(act, va[:, i, BANK:D], ps[:, b, :]))
            stage.end()
            attention_act(act, HEADS)
            stage.end()
            for i in range(HEADS + 2):
                if i < HEADS:
                    act.wait_ge(S["minus_abs"], i + 1)
                    act_step(nc.scalar.activation(stick(i, 1), stick(i, 1), ACT.Exp))
                    nc.scalar.activation(stick(i, 1), stick(i, 1), ACT.Ln, bias=con("small")[:, 2:3]).then_inc(S["log1p"], 1)
                if i >= 2:
                    h = i - 2
                    act.wait_ge(S["after_read"], h + 1)
                    nc.scalar.activation(stick(h, 3), stick(h, 0), ACT.Exp).then_inc(S["stick_exp"], 1)
            stage.end()
            norm_act(act, zb, [(0, BANK), (BANK, BANK)], arena(0))
            stage.end()
            moves.skip(4)
            stage.end()

        def block2_dve(dve, stage, moves):
            norm_dve(dve, xs, [(0, D)], oat_tm)
            turn_dve(dve, ht_r, KD, g_attn, low=ht_low2_r)
            stage.end()
            moves.take(2, lambda i, b: copy_out(dve, cq[:, i, :], ps[:, b, 0:QR]))
            moves.take(2, lambda i, b: copy_out(dve, ckv[:, i, :], ps[:, b, 0:KVR]))
            moves.take(1, lambda i, b: copy_out(dve, kr, ps[rs, b, 0:T]))
            moves.take(8, lambda i, b: copy_out(dve, fm[:, i, :], ps[:, b, 0:T]))
            moves.take(2, lambda i, b: copy_out(dve, va[:, i, 0:BANK], ps[:, b, :]))
            stage.end()
            norm_dve(dve, cq, [(0, QR)], cqn)
            norm_dve(dve, ckv, [(0, KVR)], ckvn)
            turn_dve(dve, cqt, QR // P, g_cq)
            turn_dve(dve, ckvt, KVR // P, g_ckv, 2)
            dve_step(nc.vector.tensor_copy(posf, posi[rs, :]))
            dve_step(nc.vector.tensor_scalar(angle, posf, con("freq", rs), None, ALU.mult))
            for arg, quarter in ((s_arg, 0.0), (c_arg, 0.25)):
                dve_step(nc.vector.tensor_scalar(turns, angle, 1.0 / TWO_PI, quarter, ALU.mult, ALU.add))
                dve_step(nc.vector.tensor_scalar(turns, turns, ROUND, None, ALU.add))
                dve_step(nc.vector.tensor_scalar(turns, turns, ROUND, None, ALU.subtract))
                dve_step(nc.vector.scalar_tensor_tensor(out=arg, in0=turns, scalar=-PI_A, in1=angle, op0=ALU.mult, op1=ALU.add))
                dve_step(nc.vector.scalar_tensor_tensor(out=arg, in0=turns, scalar=-PI_B, in1=arg, op0=ALU.mult, op1=ALU.add))
                dve_step(nc.vector.scalar_tensor_tensor(out=arg, in0=turns, scalar=-PI_C, in1=arg, op0=ALU.mult, op1=ALU.add))
                if quarter:
                    dve_step(nc.vector.tensor_scalar(arg, arg, np.pi / 2, None, ALU.add))
                last = nc.vector.tensor_scalar(arg, arg, PI_IN, -PI_IN, ALU.min, ALU.max)
            last.then_inc(S["angles"], 1)
            stage.end()
            moves.take(8, lambda i, b: copy_out(dve, fm[0:96, 8 + i, :], ps[0:96, b, 0:T]))
            moves.take(8, lambda i, b: copy_out(dve, fm[0:64, 16 + i, :], ps[0:64, b, 0:T]))
            moves.take(2, lambda i, b: copy_out(dve, va[:, i, BANK:D], ps[:, b, :]))
            stage.end()
            r1, r2 = (arena(5)[rs, 512 * i:512 * i + 512].rearrange("p (a b) -> p a b", a=2) for i in range(2))
            sin2, cos2 = (a.unsqueeze(1).to_broadcast([32, 2, T]) for a in (s_arg, c_arg))
            for m in range(4):
                q2 = fm[rs, 8 + 2 * m:10 + 2 * m, :]
                dve.wait_ge(S["rotated2"], m + 1)
                nc.vector.tensor_tensor(r1, ps[rs, m, :].rearrange("p (a b) -> p a b", a=2), sin2, ALU.mult)
                dve_step(nc.vector.tensor_tensor(r2, q2, cos2, ALU.mult))
                nc.vector.tensor_tensor(q2, r1, r2, ALU.add).then_inc(S["roped2"], 1)
                dve.wait_ge(S["roped2"], m + 1)
            dve.wait_ge(S["rotated2"], 5)
            nc.vector.tensor_tensor(r1[:, 0, :], ps[rs, 4, 0:T], s_arg, ALU.mult)
            dve_step(nc.vector.tensor_tensor(r2[:, 0, :], kr, c_arg, ALU.mult))
            nc.vector.tensor_tensor(fm[rs, 16:24, :], r1[:, 0, :].unsqueeze(1).to_broadcast([32, HEADS, T]),
                                    r2[:, 0, :].unsqueeze(1).to_broadcast([32, HEADS, T]), ALU.add).then_inc(S["roped2"], 1)
            attention_dve(dve, HEADS, 96.0 ** -0.5, lambda h: None)
            dve.wait_ge(S["head_out"], 2 * HEADS)
            for t in range(NT):
                nc.vector.tensor_copy(zb[:, t, 0:BANK], ps[:, 4 + t, :])
            stage.end()
            for i in range(HEADS + 2):
                if i < HEADS:
                    dve.wait_ge(S["stick_z"], i + 1)
                    if i >= 4:
                        dve.wait_ge(S["stick_out"], i - 3)
                    nc.vector.tensor_scalar(stick(i, 0), ps[:, i % 2, 0:3 * P], 0.125, None, ALU.mult).then_inc(S["z_read"], 1)
                    dve.wait_ge(S["z_read"], i + 1)
                    nc.vector.scalar_tensor_tensor(out=stick(i, 1), in0=stick(i, 0), scalar=-1.0, in1=stick(i, 0), op0=ALU.mult, op1=ALU.min).then_inc(S["minus_abs"], 1)
                if 1 <= i <= HEADS:
                    h = i - 1
                    dve.wait_ge(S["log1p"], h + 1)
                    nc.vector.scalar_tensor_tensor(out=stick(h, 1), in0=stick(h, 0), scalar=0.0, in1=stick(h, 1), op0=ALU.max, op1=ALU.add).then_inc(S["softplus"], 1)
                    dve.wait_ge(S["softplus"], h + 1)
                    dve_step(nc.vector.tensor_tensor(stick(h, 0), stick(h, 0), stick(h, 1), ALU.subtract))
                if i >= 2:
                    h = i - 2
                    dve.wait_ge(S["after"], h + 1)
                    nc.vector.tensor_tensor(stick(h, 0), stick(h, 0), ps[:, 2 + h % 2, 0:3 * P], ALU.subtract).then_inc(S["after_read"], 1)
            dve.wait_ge(S["stick_out"], HEADS)
            for t in range(NT):
                nc.vector.tensor_copy(zb[:, t, BANK:D], ps[:, 4 + t, :])
            stage.end()
            norm_dve(dve, zb, [(0, BANK), (BANK, BANK)], oat_tm)
            turn_dve(dve, ht, KD, g_mix)
            stage.end()
            dve.wait_ge(S["bias_in"], 48)
            dve_step(nc.vector.tensor_copy(bgp[:, :], bgu))
            for g in (1, 2):
                dve_step(nc.vector.tensor_tensor(bgu_rest, (bgu, bgu_rest)[g - 1], bgp[:, :], ALU.subtract))
                for q in range(g, 3):
                    last = nc.vector.tensor_copy(bgp[NEXP * q:NEXP * q + NEXP, :], bgu_rest[NEXP * q:NEXP * q + NEXP, :])
                dve_step(last)
            moves.take(4, lambda i, b: nc.vector.tensor_tensor(xs[:, i % 2, BANK * (i // 2):BANK * (i // 2) + BANK], ps[:, b, :],
                                                               xs[:, i % 2, BANK * (i // 2):BANK * (i // 2) + BANK], ALU.add), whole=True)
            stage.end()

        NLIST = NEXP + MAXOVER + 1
        ub = fm[:, :, :].rearrange("p a b -> p (a b)").bitcast(BF16)[:, 0:3 * NT * D].rearrange("p (s t d) -> p s t d", s=3, t=NT)
        u_tok, rest = va, zb
        g_row = extra[:, 2, 0:D]
        bdn = extra[0:NEXP, 2, D:2 * D]
        bgu, bgu_rest = extra[0:3 * NEXP, 0, :], extra[0:3 * NEXP, 1, :]
        bgp = sb("bgp", [3 * NEXP, 2048], BF16)
        wr = sb("wr", [P, KD, NEXP])
        lg, gate, pick, posx = (sb(n, [P, NT, NEXP]) for n in ("lg", "gate", "pick", "posx"))
        mx8 = sb("mx8", [P, NT, 8])
        ix8 = sb("ix8", [P, NT, 8], U32)
        ixf = sb("ixf", [P, NT, 8])
        gsm = sb("gsm", [P, NT])
        over = sb("over", [NEXP, 8])
        hot = extra[0:NEXP, 1, 0:3 * MAXOVER].rearrange("p (r k) -> p r k", r=3)
        wlist = sb("wlist", [1, 2, NLIST], I32)
        wcount = sb("wcount", [1, 1], I32)
        tmp4 = zb[:, 1, 0:512].rearrange("p (a j e) -> p a j e", a=4, j=4)
        gate_t = zb[0:NEXP, 1, 512:512 + T]
        xst = zb[:, 0, 0:KD * CAP].rearrange("p (k s) -> p k s", k=KD)
        glu, lin, sig, act_b = extra[:, 0, 0:512], extra[:, 0, 512:1024], extra[:, 0, 1024:1536], extra[:, 0, 1536:2048]
        act_t = extra[:, 1, 0:512].rearrange("p (j m) -> p j m", j=4)
        pgt = extra[:, 1, 512:512 + T]
        y_sb = extra[:, 1, 1024:1536]
        pg = extra[:, 1, 1536:1536 + NT * 2 * CAP].rearrange("p (t a s) -> p t a s", t=NT, a=2)
        pick_s = sb("pick_s", [P, NT, CAP], BF16)
        bsel = sb("bsel", [3 * NEXP, CAP], BF16)
        w_gu, w_dn = I["w_gu_2"][0], I["w_dn_2"][0]

        def expert_chunk(e, c):
            if c < 4:
                src = w_gu[e].rearrange("(p k) n -> p k n", k=KD)[:, 2 * c:2 * c + 2, :]
                return ring[:, c, :].rearrange("p (k n) -> p k n", k=2), src
            src = w_dn[e].rearrange("(a p j) n -> a p j n", a=2, j=4)[c - 4]
            return ring[:, c, :].rearrange("p (j n) -> p j n", j=4), src

        class LoopSteps:

            def __init__(self, eng, sem, it, per):
                self.eng, self.sem, self.it, self.per, self.n = eng, sem, it, per, 0

            def __call__(self, ins):
                self.n += 1
                ins.then_inc(self.sem, 1)
                self.eng.wait_ge(self.sem, self.it * self.per + self.n)

            def close(self):
                assert self.n == self.per, self.n

        def item_count(eng):
            return eng.value_load(wcount[0:1, 0:1], min_val=NEXP, max_val=NEXP + MAXOVER)

        def moe_pool(pool, stage):
            stage.end()
            stage.end()
            pool.dma_start(p_tok, I["p_2"][0, 0].rearrange("(t p) n -> p t n", p=P)).then_inc(S["p_in"], 16)
            stage.end()

        def moe_pe(pe, stage):
            pe.wait_ge(S["normed"], 6)
            turn_pe(pe, oat_tm, KD)
            pe.wait_ge(S["u_t"], 1)
            for t in range(NT):
                for j in range(KD):
                    last = pe.matmul(ps[:, 4, NEXP * t:NEXP * t + NEXP], ht[:, j, P * t:P * t + P], wr[:, j, :], start=(j == 0), stop=(j == KD - 1))
            last.then_inc(S["logits"], 1)
            stage.end()
            pe.wait_ge(S["picked"], 1)
            pe.matmul(ps[:, 0, 0:NEXP], con("earlier"), pick[:, 0, :], start=True, stop=True)
            pe.matmul(ps[:, 0, NEXP:2 * NEXP], con("earlier"), pick[:, 1, :], start=True, stop=False)
            pe.matmul(ps[:, 0, NEXP:2 * NEXP], con("ones"), pick[:, 0, :], start=False, stop=True).then_inc(S["positions"], 1)
            for t in range(NT):
                last = pe.matmul(ps[0:NEXP, 1, 0:1], pick[:, t, :], con("ones")[:, 0:1], start=(t == 0), stop=(t == NT - 1))
            last.then_inc(S["counts"], 1)
            pe.wait_ge(S["gated"], 1)
            for t in range(NT):
                last = pe.transpose(ps[0:NEXP, 5, P * t:P * t + P], gate[:, t, :], ident)
            last.then_inc(S["gate_turned"], 1)
            pe.wait_ge(S["overs"], 1)
            pe.matmul(ps[0:NEXP, 2, 0:3], con("earlier", slice(0, NEXP))[:, 0:NEXP], over[:, 0:3], start=True, stop=True).then_inc(S["before"], 1)
            pe.wait_ge(S["hots"], 1)
            for a in range(2):
                for r in range(3):
                    lhs = con("row", slice(0, NEXP)) if a == 0 else con("small", slice(0, NEXP))[:, 3 + r:4 + r]
                    pe.matmul(ps[0:1, 3, MAXOVER * a:MAXOVER * a + MAXOVER], lhs, hot[:, r, :], start=(r == 0), stop=(r == 2))
            for r in range(3):
                last = pe.matmul(ps[0:1, 3, 2 * MAXOVER:2 * MAXOVER + 1], over[:, r:r + 1], con("ones", slice(0, NEXP))[:, 0:1], start=(r == 0), stop=(r == 2))
            last.then_inc(S["listed"], 1)
            stage.end()
            for t in range(NT):
                for n in range(2):
                    pe.matmul(ps[:, 2 * t + n, :], gate_t[:, P * t:P * t + P], bdn[:, BANK * n:BANK * n + BANK], start=True, stop=False, skip_group_check=True)
            total = item_count(pe)

            def gather():
                for k in range(KD):
                    for i in range(3 * NT):
                        last = pe.matmul(ps[:, 7, CAP * k:CAP * k + CAP], ub[:, i // NT, i % NT, k:k + KD * (P - 1) + 1:KD], pick_s[:, i % NT, :],
                                         start=(i == 0), stop=(i == 3 * NT - 1))
                last.then_inc(S["gathered"], 1)

            def spread(wait):
                wait()
                for t in range(NT):
                    for n in range(2):
                        r = slice(64 * n, 64 * n + CAP)
                        last = pe.matmul(ps[:, 2 * t + n, :], pgt[r, P * t:P * t + P], y_sb[r, :], start=False, stop=False, skip_group_check=True)
                last.then_inc(S["spread"], 1)

            pe.wait_ge(S["pick_s"], 1)
            gather()
            with pe.Fori(0, total) as it:
                pe.wait_ge(S["xst"], it + 1)
                pe.wait_ge(S["bsel"], it + 1)
                for n in range(4):
                    pe.matmul(ps[64 * (n % 2):64 * (n % 2) + CAP, 4 + n // 2, :], bsel[:, :], bgp[:, BANK * n:BANK * n + BANK], start=True, stop=False, skip_group_check=True)
                for c in range(4):
                    pe.wait_ge(S[f"expert_in{c}"], it * 16 + 16)
                    for k in (2 * c, 2 * c + 1):
                        for n in range(4):
                            last = pe.matmul(ps[64 * (n % 2):64 * (n % 2) + CAP, 4 + n // 2, :], xst[:, k, :],
                                             ring[:, c, 2048 * (k % 2) + BANK * n:2048 * (k % 2) + BANK * n + BANK], start=False, stop=(k == KD - 1), skip_group_check=True)
                    last.then_inc(S["w_used"], 1)
                    if c == 1:
                        spread(lambda: pe.wait_ge(S["y_sb"], it + 1))
                    if c == 2:
                        pe.wait_ge(S["pg"], it + 1)
                        for t in range(NT):
                            last = pe.transpose(ps[:, 6, P * t:P * t + P], pg[:, t, :, :].rearrange("p a s -> p (a s)"), ident)
                        last.then_inc(S["pg_turned"], 1)
                pe.wait_ge(S["pick_s"], it + 2)
                gather()
                pe.wait_ge(S["act"], it + 1)
                for j in range(4):
                    last = pe.transpose(ps[:, 4, P * j:P * j + P], act_b[:, j:j + 4 * (P - 1) + 1:4], ident)
                last.then_inc(S["act_turned"], 1)
                pe.wait_ge(S["act_t"], it + 1)
                pe.wait_ge(S["pgt"], it + 1)
                for c in range(2):
                    pe.wait_ge(S[f"expert_in{4 + c}"], it * 16 + 16)
                    for j in range(4):
                        for n in range(2):
                            last = pe.matmul(ps[64 * n:64 * n + CAP, 6, :], act_t[:, j, 64 * c:64 * c + CAP],
                                             ring[:, 4 + c, D * j + BANK * n:D * j + BANK * n + BANK], start=(c == 0 and j == 0), stop=(c == 1 and j == 3), skip_group_check=True)
                    last.then_inc(S["w_used"], 1)
            spread(lambda: (pe.wait_ge(S["y_sb"], total + 1), pe.wait_ge(S["pgt"], total)))
            stage.end()

        def moe_act(act, stage):
            norm_act(act, xs, [(0, D)], zb[:, 0, :])
            act.wait_ge(S["u_tok"], 1)
            nc.scalar.activation(ub[:, 0], u_tok[:, :, :], ACT.Copy).then_inc(S["part"], 1)
            act.wait_ge(S["rest"], 1)
            nc.scalar.activation(ub[:, 1], rest[:, :, :], ACT.Copy).then_inc(S["part"], 1)
            act.wait_ge(S["rest"], 2)
            nc.scalar.activation(ub[:, 2], rest[:, :, :], ACT.Copy)
            stage.end()
            act.wait_ge(S["less_max"], 1)
            nc.scalar.activation(mx8[:, :, 0:4], mx8[:, :, 0:4], ACT.Exp).then_inc(S["gate_exp"], 1)
            act.wait_ge(S["gate_turned"], 1)
            nc.scalar.activation(gate_t, ps[0:NEXP, 5, 0:T], ACT.Copy)
            nc.scalar.activation(y_sb, con("causal")[:, 0:1].to_broadcast([P, 512]), ACT.Copy, scale=0.0).then_inc(S["y_sb"], 1)
            nc.scalar.activation(pgt, con("causal")[:, 0:1].to_broadcast([P, T]), ACT.Copy, scale=0.0)
            stage.end()
            total = item_count(act)
            act.wait_ge(S["gathered"], 1)
            nc.scalar.activation(xst, ps[:, 7, 0:KD * CAP].rearrange("p (k s) -> p k s", k=KD), ACT.Copy).then_inc(S["xst"], 1)
            with act.Fori(0, total) as it:
                act.wait_ge(S["pg_turned"], it + 1)
                nc.scalar.activation(pgt, ps[:, 6, 0:T], ACT.Copy).then_inc(S["pgt"], 1)
                act.wait_ge(S["glu"], it + 1)
                nc.scalar.activation(sig, glu, ACT.Sigmoid, scale=1.702).then_inc(S["sig"], 1)
                act.wait_ge(S["gathered"], it + 2)
                nc.scalar.activation(xst, ps[:, 7, 0:KD * CAP].rearrange("p (k s) -> p k s", k=KD), ACT.Copy).then_inc(S["xst"], 1)
                act.wait_ge(S["w_used"], it * 6 + 6)
                nc.scalar.activation(y_sb, ps[:, 6, :], ACT.Copy).then_inc(S["y_sb"], 1)
            stage.end()

        def moe_dve(dve, stage):
            norm_dve(dve, xs, [(0, D)], oat_tm)
            dve.wait_ge(S["row_in"], 16 * 3)
            dve.wait_ge(S["normed"], 6)
            for t in range(NT):
                last = nc.vector.tensor_tensor(u_tok[:, t, :], oat_tm[:, t, :], g_row, ALU.mult)
            last.then_inc(S["u_tok"], 1)
            turn_dve(dve, ht, KD, g_moe, done="u_t")
            dve.wait_ge(S["part"], 1)
            nc.vector.tensor_tensor(rest[:, :, :], u_tok[:, :, :], ub[:, 0], ALU.subtract).then_inc(S["rest"], 1)
            dve.wait_ge(S["rest"], 1)
            dve.wait_ge(S["part"], 2)
            nc.vector.tensor_tensor(rest[:, :, :], rest[:, :, :], ub[:, 1], ALU.subtract).then_inc(S["rest"], 1)
            dve.wait_ge(S["logits"], 1)
            dve_step(nc.vector.tensor_tensor(lg[:, :, :], ps[:, 4, 0:2 * NEXP].rearrange("p (t e) -> p t e", t=NT), brow[:, :].unsqueeze(1).to_broadcast([P, NT, NEXP]), ALU.add))
            stage.end()
            for t in range(NT):
                dve_step(nc.vector.max(mx8[:, t, :], lg[:, t, :]))
                dve_step(nc.vector.max_index(ix8[:, t, :], mx8[:, t, :], lg[:, t, :]))
            dve_step(nc.vector.tensor_copy(ixf[:, :, :], ix8[:, :, :]))
            dve_step(nc.vector.tensor_copy(gsm[:, :], mx8[:, :, 0]))
            for t in range(NT):
                last = nc.vector.tensor_scalar(mx8[:, t, 0:4], mx8[:, t, 0:4], gsm[:, t:t + 1], None, ALU.subtract)
            last.then_inc(S["less_max"], 1)
            number = con("slots")[:, 0:NEXP]
            for t in range(NT):
                for j in range(4):
                    last = nc.vector.tensor_scalar(tmp4[:, t, j, :], number, ixf[:, t, j:j + 1], None, ALU.is_equal)
            dve_step(last)
            for t in range(NT):
                last = nc.vector.tensor_reduce(pick[:, t, :], tmp4[:, t].rearrange("p j e -> p e j"), AX, ALU.add)
            last.then_inc(S["picked"], 1)
            dve.wait_ge(S["gate_exp"], 1)
            dve_step(nc.vector.tensor_reduce(gsm[:, :], mx8[:, :, 0:4], AX, ALU.add))
            dve_step(nc.vector.reciprocal(gsm[:, :], gsm[:, :]))
            for t in range(NT):
                last = nc.vector.tensor_scalar(mx8[:, t, 0:4], mx8[:, t, 0:4], gsm[:, t:t + 1], None, ALU.mult)
            dve_step(last)
            for t in range(NT):
                for j in range(4):
                    last = nc.vector.tensor_scalar(tmp4[:, 2 + t, j, :], number, ixf[:, t, j:j + 1], mx8[:, t, j:j + 1], ALU.is_equal, ALU.mult)
            dve_step(last)
            for t in range(NT):
                last = nc.vector.tensor_reduce(gate[:, t, :], tmp4[:, 2 + t].rearrange("p j e -> p e j"), AX, ALU.add)
            last.then_inc(S["gated"], 1)
            dve.wait_ge(S["picked"], 1)
            dve_step(nc.vector.tensor_scalar(posx[:, :, :], pick[:, :, :], -4096.0, 4096.0, ALU.mult, ALU.add))
            dve.wait_ge(S["positions"], 1)
            dve_step(nc.vector.tensor_tensor(posx[:, :, :], posx[:, :, :], ps[:, 0, 0:2 * NEXP].rearrange("p (t e) -> p t e", t=NT), ALU.add))
            dve.wait_ge(S["counts"], 1)
            dve_step(nc.vector.tensor_copy(over[:, 7:8], ps[0:NEXP, 1, 0:1]))
            nc.vector.tensor_scalar(over[:, 0:3], con("small", slice(0, NEXP))[:, 3:6], over[:, 7:8], None, ALU.is_lt).then_inc(S["overs"], 1)
            dve.wait_ge(S["before"], 1)
            dve_step(nc.vector.tensor_reduce(over[:, 6:7], ps[0:NEXP, 2, 0:3], AX, ALU.add))
            dve_step(nc.vector.tensor_scalar(over[:, 3:6], con("slots", slice(0, NEXP))[:, 0:3], over[:, 6:7], None, ALU.add))
            for r in range(3):
                last = nc.vector.tensor_scalar(hot[:, r, :], con("slots", slice(0, NEXP))[:, 0:MAXOVER], over[:, 3 + r:4 + r], over[:, r:r + 1], ALU.is_equal, ALU.mult)
            last.then_inc(S["hots"], 1)
            dve_step(nc.vector.memset(wlist[:, :, :], 0))
            nc.vector.tensor_copy(wlist[:, 0, 0:NEXP], con("slots", slice(0, 1))[:, 0:NEXP])
            dve.wait_ge(S["listed"], 1)
            nc.vector.tensor_copy(wlist[:, :, NEXP:NEXP + MAXOVER], ps[0:1, 3, 0:2 * MAXOVER].rearrange("p (a k) -> p a k", a=2))
            nc.vector.tensor_scalar(wcount[:, :], ps[0:1, 3, 2 * MAXOVER:2 * MAXOVER + 1], float(NEXP), None, ALU.add).then_inc(S["items"], 1)
            stage.end()
            total = item_count(dve)

            def item(i):
                return (dve.value_load(wlist[0:1, 0, bass.ds(i, 1)], min_val=0, max_val=NEXP - 1),
                        dve.value_load(wlist[0:1, 1, bass.ds(i, 1)], min_val=0, max_val=T))

            def pick_tokens(e, base):
                for t in range(NT):
                    last = nc.vector.tensor_scalar(pick_s[:, t, :], con_at("slots", base, CAP), posx[:, t, bass.ds(e, 1)], None, ALU.is_equal)
                last.then_inc(S["pick_s"], 1)

            def pick_bias(e):
                nc.vector.tensor_copy(bsel[:, :], con("bsel", slice(0, 3 * NEXP))[:, bass.ds(e, 1)].to_broadcast([3 * NEXP, CAP])).then_inc(S["bsel"], 1)

            pick_tokens(0, 0)
            pick_bias(0)
            with dve.Fori(0, total) as it:
                e, base = item(it)
                e1, base1 = item(it + 1)
                step = LoopSteps(dve, S["moe_step"], it, 2)
                dve.wait_ge(S["pick_s"], it + 1)
                for t in range(NT):
                    last = nc.vector.tensor_scalar(pg[:, t, :, :], pick_s[:, t, :].unsqueeze(1).to_broadcast([P, 2, CAP]), gate[:, t, bass.ds(e, 1)], None, ALU.mult)
                last.then_inc(S["pg"], 1)
                dve.wait_ge(S["gathered"], it + 1)
                dve.wait_ge(S["pg"], it + 1)
                pick_tokens(e1, base1)
                dve.wait_ge(S["w_used"], it * 6 + 4)
                nc.vector.tensor_scalar(glu, ps[:, 4, :], 7.0, None, ALU.min).then_inc(S["glu"], 1)
                step(nc.vector.tensor_scalar(lin, ps[:, 5, :], 7.0, -7.0, ALU.min, ALU.max))
                pick_bias(e1)
                step(nc.vector.scalar_tensor_tensor(out=lin, in0=lin, scalar=1.0, in1=glu, op0=ALU.add, op1=ALU.mult))
                dve.wait_ge(S["sig"], it + 1)
                nc.vector.tensor_tensor(act_b, lin, sig, ALU.mult).then_inc(S["act"], 1)
                dve.wait_ge(S["act_turned"], it + 1)
                nc.vector.tensor_copy(act_t, ps[:, 4, :].rearrange("p (j m) -> p j m", j=4)).then_inc(S["act_t"], 1)
                step.close()
            stage.end()

        p_tok = va[:, 0, 0:NT * 256].rearrange("p (t n) -> p t n", t=NT)
        p_t = zb[:, 1, 0:2 * T].rearrange("p (k n) -> p k n", k=2)
        ple_gate = gates[:, 0]

        def tail_pool(pool, stage):
            pool.dma_start(g_row, I["g_final_2"].partition_broadcast(P)).then_inc(S["row_in"], 16)
            stage.end()
            stage.end()
            stage.end()

        def tail_pe(pe, stage, prod):
            pe.wait_ge(S["p_in"], 16)
            turn_pe(pe, p_tok, 2, 4)
            pe.wait_ge(S["normed"], 7)
            turn_pe(pe, oat_tm, KD)
            stage.end()
            for c in range(2):
                prod.token_major(ht)
            prod.chunk(prod.tm_units(BANK, lambda w, j: w[:, j, 0:BANK]) + prod.tm_units(BANK, lambda w, j: w[:, j, BANK:D]), p_t)
            stage.end()
            stage.end()

        def tail_act(act, stage, moves):
            act.wait_ge(S["summed"], NT)
            norm_act(act, xs, [(0, D)], zb[:, 0, :])
            stage.end()
            moves.take(4, lambda i, b: nc.scalar.activation(ple_gate[:, i % 2, BANK * (i // 2):BANK * (i // 2) + BANK], ps[:, b, :], ACT.Sigmoid), whole=True)
            moves.skip(4)
            stage.end()
            norm_act(act, xs, [(0, D)], zb[:, 0, :])
            stage.end()

        def tail_dve(dve, stage, moves):
            for t in range(NT):
                nc.vector.tensor_tensor(xs[:, t, :], xs[:, t, :], ps[:, 2 * t:2 * t + 2, :].rearrange("p b n -> p (b n)"), ALU.add).then_inc(S["summed"], 1)
            turn_dve(dve, p_t, 2, None, 4)
            norm_dve(dve, xs, [(0, D)], oat_tm)
            turn_dve(dve, ht, KD, g_ple)
            stage.end()
            moves.skip(4)
            dve.wait_ge(S["moved0"], moves.u // 2 + moves.u % 2)
            dve.wait_ge(S["moved1"], moves.u // 2)
            moves.take(4, lambda i, b: nc.vector.tensor_tensor(oat_tm[:, i % 2, BANK * (i // 2):BANK * (i // 2) + BANK], ps[:, b, :],
                                                               ple_gate[:, i % 2, BANK * (i // 2):BANK * (i // 2) + BANK], ALU.mult), whole=True)
            dve.wait_ge(S["moved0"], moves.u // 2 + moves.u % 2)
            dve.wait_ge(S["moved1"], moves.u // 2)
            nc.vector.tensor_tensor(xs[:, :, :], xs[:, :, :], oat_tm, ALU.add)
            stage.end()
            norm_dve(dve, xs, [(0, D)], None)
            dve.wait_ge(S["row_in"], 16 * 4)
            for t in range(NT):
                nc.vector.scalar_tensor_tensor(out=xs[:, t, :], in0=xs[:, t, :], scalar=ssq[:, t:t + 1], in1=g_row, op0=ALU.mult, op1=ALU.mult)
            stage.end()

        @block.sync
        def _(sp):
            def load_chunk(g):
                c = plan[g]
                if c.free:
                    sp.wait_ge(S["unit"], c.free)
                if c.slot == 2 and after_gdn <= g < after_gdn + 3:
                    sp.wait_ge(S["stage"], 4 * 9)
                sp.dma_start(c.dst, c.src).then_inc(S[f"chunk_in{c.slot}"], 16)

            sp.dma_start(xs[:, :, :], I["x"][0].rearrange("(t p) d -> p t d", p=P)).then_inc(S["x_in"], 16)
            sp.dma_start(cst[:, :], I["const"]).then_inc(S["const_in"], 16)
            for g in range(before_experts):
                load_chunk(g)
            sp.wait_ge(S["stage"], 4 * 20)
            sp.wait_ge(S["unit"], plan[before_experts - 1].done)
            for c in range(6):
                sp.dma_start(*expert_chunk(0, c)).then_inc(S[f"expert_in{c}"], 16)
            sp.wait_ge(S["stage"], 4 * 23)
            total = item_count(sp)
            with sp.Fori(1, total) as it:
                e = sp.value_load(wlist[0:1, 0, bass.ds(it, 1)], min_val=0, max_val=NEXP - 1)
                for c in range(6):
                    sp.wait_ge(S["w_used"], it * 6 + (c - 5))
                    sp.dma_start(*expert_chunk(e, c)).then_inc(S[f"expert_in{c}"], 16)
            sp.wait_ge(S["w_used"], total * 6)
            for g in range(before_experts, len(plan)):
                load_chunk(g)
            sp.wait_ge(S["stage"], 4 * LAST_STAGE)
            sp.dma_start(out[0].rearrange("(t p) d -> p t d", p=P), xs[:, :, :]).then_inc(S["stored"], 16)
            sp.wait_ge(S["stored"], 16)

        @block.gpsimd
        def _(pool):
            stage = Stage(pool, S["stage"])
            pool.dma_start(w_pre, I["pre_norm_w"][0].rearrange("(p k) -> p k", k=KD)).then_inc(S["w_pre_in"], 16)
            pool.dma_start(w_gdn, I["gdn_norm_w"][0].rearrange("(p k) -> p k", k=1)).then_inc(S["small_in"], 16)
            pool.dma_start(wbd[:, :, :], w_in[:, :, 16 * BANK:16 * BANK + 16]).then_inc(S["small_in"], 16)
            pool.dma_start(extra[0:96, 2, 0:P], I["conv_w"][0].rearrange("j (c p) -> (j c) p", p=P)).then_inc(S["small_in"], 16)
            pool.dma_start(hsc[:, 0:8], I["dt_bias"][0].partition_broadcast(P)).then_inc(S["small_in"], 16)
            pool.dma_start(hsc[:, 8:16], I["a_log"][0].partition_broadcast(P)).then_inc(S["small_in"], 16)
            pool.dma_start(g_attn, I["g_attn_2"][0].rearrange("(p k) -> p k", k=KD)).then_inc(S["small_in"], 16)
            pool.dma_start(g_cq, I["g_cq_2"][0].rearrange("(p k) -> p k", k=QR // P)).then_inc(S["small_in"], 16)
            pool.dma_start(g_ckv, I["g_ckv_2"][0].rearrange("(p k) -> p k", k=KVR // P)).then_inc(S["small_in"], 16)
            pool.dma_start(g_mix[0:64, :], I["g_out_mla_2"][0].rearrange("(p k) -> p k", k=KD)).then_inc(S["small_in"], 16)
            pool.dma_start(g_mix[64:P, :], I["g_out_sb_2"][0].rearrange("(p k) -> p k", k=KD)).then_inc(S["small_in"], 16)
            pool.dma_start(g_moe, I["g_moe_2"][0].rearrange("(p k) -> p k", k=KD)).then_inc(S["small_in"], 16)
            pool.dma_start(g_ple, I["g_ple_2"][0].rearrange("(p k) -> p k", k=KD)).then_inc(S["small_in"], 16)
            pool.dma_start(posi[64:96, :], I["positions_2"][0].partition_broadcast(32)).then_inc(S["small_in"], 16)
            pool.dma_start(wr[:, :, :], pk_rows("w_router_2", KD)).then_inc(S["small_in"], 16)
            pool.dma_start(brow[:, :], I["b_router_2"][0].partition_broadcast(P)).then_inc(S["small_in"], 16)
            pool.wait_ge(S["const_in"], 16)
            stage.end()
            pool.wait_ge(S["small_in"], SMALL_LOADS * 16)
            stage.end()
            stage.end()
            stage.end()
            gdn_pool(pool, stage)
            stage.end()
            stage.end()
            pool.dma_start(extra[:, 2, 0:D], I["post_norm_w"][0].partition_broadcast(P)).then_inc(S["row_in"], 16)
            stage.end()
            stage.end()
            block2_pool(pool, stage)
            moe_pool(pool, stage)
            tail_pool(pool, stage)

        @block.tensor
        def _(pe):
            stage = Stage(pe, S["stage"])
            prod = Products(pe)
            pe.wait_ge(S["const_in"], 16)
            pe.wait_ge(S["normed"], 1)
            turn_pe(pe, oat_tm, KD)
            stage.end()
            for c in range(6):
                prod.feature_major(ht_parts)
            for c in range(2):
                prod.token_major(ht_parts)
            stage.end()
            for m in range(8):
                pe.matmul(ps[0:32, m, :], con("rot", slice(0, 32)), fm[0:32, 2 * m:2 * m + 2, :], start=True, stop=True).then_inc(S["rotated"], 1)
            pe.wait_ge(S["roped"], 8)

            def out_a(h, pt):
                b = ps[:, 4 + h % 2, :]
                if h >= 2:
                    pe.wait_ge(S["head_taken"], h - 1)
                pe.matmul(b[:, 0:T], zb[:, 0, P * h:P * h + P], pt[:, 0:T], start=True, stop=False, skip_group_check=True)
                return pe.matmul(b[:, P:T], zb[:, 1, P * h:P * h + P], pt[:, T:3 * P], start=False, stop=True, skip_group_check=True)

            attention_pe(pe, 0, lambda h: fm[:, h, :], lambda h: fm[:, 8 + h, :], out_a)
            pe.transpose(ps[:, 7, 0:96], extra[0:96, 2, 0:P], ident[0:96, 0:96]).then_inc(S["conv_turned"], 1)
            stage.end()
            for c in range(6):
                prod.feature_major(ht_parts)
            for c in range(2):
                prod.token_major(ht_parts)
            pe.wait_ge(S["moved1"], prod.u // 2)
            for t in range(NT):
                for j in range(KD):
                    pe.matmul(ps[:, 7, 16 * t:16 * t + 16], ht_r[:, j, P * t:P * t + P].bitcast(F32), wbd[:, j, :], start=(j == 0), stop=False)
                    last = pe.matmul(ps[:, 7, 16 * t:16 * t + 16], ht_low_r[:, j, P * t:P * t + P].bitcast(F32), wbd[:, j, :], start=False, stop=(j == KD - 1))
            last.then_inc(S["bd_logits"], 1)
            stage.end()
            gdn_pe(pe, stage)
            for c in range(4):
                prod.token_major(ht_parts)
            pe.wait_ge(S["oat_low"], 1)
            for c in range(2):
                prod.token_major((oat_high_r, oat_r))
            for c in range(2):
                prod.token_major((obt_r, obt_low_r))
            stage.end()
            turn_pe(pe, va, KD)
            stage.end()
            for c in range(2):
                prod.token_major(ht_parts2)
            stage.end()
            stage.end()
            block2_pe(pe, stage, prod)
            moe_pe(pe, stage)
            tail_pe(pe, stage, prod)

        @block.scalar
        def _(act):
            act_steps[0] = Steps(act, S["act_step"])
            stage = Stage(act, S["stage"])
            moves = Moves(act, 0)
            act.wait_ge(S["x_in"], 16)
            act.wait_ge(S["const_in"], 16)
            norm_act(act, xs, [(0, D)], extra[:, 0, :])
            moves.split(0)
            moves.split(1)
            stage.end()
            moves.take(24, lambda i, b: copy_out(act, fm[:, i, :], ps[:, b, 0:T]))
            moves.take(4, lambda i, b: copy_out(act, zb[:, i % 2, BANK * (i // 2):BANK * (i // 2) + BANK], ps[:, b, :]))
            stage.end()
            nc.scalar.activation(fm[:, 16:24, :], fm[:, 16:24, :], ACT.Silu).then_inc(S["silu_za"], 1)
            attention_act(act, 0)
            stage.end()
            for c in range(8):
                if c < 6:
                    moves.take(4, lambda i, b: copy_out(act, fm[:, 4 * c + i, :], ps[:, b, 0:T]))
                    conv_act(act, c, moves)
                else:
                    moves.take(2, lambda i, b: copy_out(act, zb[:, i, BANK * (c - 6):BANK * (c - 6) + BANK], ps[:, b, :]))
                if c >= 2:
                    act.wait_ge(S["conv"], c - 1)
                    i = 4 * (c - 2)
                    nc.scalar.activation(fm[:, i:i + 4, :], extra[:, i // 8, T * (i % 8):T * (i % 8 + 4)].rearrange("p (c n) -> p c n", c=4), ACT.Silu)
            stage.end()
            gdn_act(act, stage, moves)
            nc.scalar.activation(oat_high_r, oat[:, :, :], ACT.Copy).then_inc(S["oat_high"], 1)
            moves.take(8, lambda i, b: nc.scalar.activation(gates[:, i // 4, i % 2, BANK * (i % 4 // 2):BANK * (i % 4 // 2) + BANK], ps[:, b, :], ACT.Sigmoid), whole=True)
            moves.skip(8)
            stage.end()
            stage.end()
            moves.take(4, lambda i, b: copy_out(act, va[:, i % 2, BANK * (i // 2):BANK * (i // 2) + BANK], ps[:, b, :]))
            stage.end()
            norm_act(act, va, [(0, D)], extra[:, 0, :])
            stage.end()
            block2_act(act, stage, moves)
            moe_act(act, stage)
            tail_act(act, stage, moves)

        @block.vector
        def _(dve):
            dve_steps[0] = Steps(dve, S["dve_step"])
            stage = Stage(dve, S["stage"])
            moves = Moves(dve, 1)
            norm_dve(dve, xs, [(0, D)], oat_tm)
            dve.wait_ge(S["w_pre_in"], 16)
            turn_dve(dve, ht_r, KD, w_pre, low=ht_low_r)
            moves.split(0)
            stage.end()
            moves.split(1)
            moves.take(24, lambda i, b: copy_out(dve, fm[:, i, :], ps[:, b, 0:T]))
            moves.take(4, lambda i, b: copy_out(dve, zb[:, i % 2, BANK * (i // 2):BANK * (i // 2) + BANK], ps[:, b, :]))
            stage.end()
            cosb = con("cos", slice(0, 32)).unsqueeze(1).to_broadcast([32, 2, T])
            sinb = con("sin", slice(0, 32)).unsqueeze(1).to_broadcast([32, 2, T])
            r1, r2 = (extra[0:32, 1, 512 * i:512 * i + 512].rearrange("p (a b) -> p a b", a=2) for i in range(2))
            for m in range(8):
                dve.wait_ge(S["rotated"], m + 1)
                nc.vector.tensor_tensor(r1, ps[0:32, m, :].rearrange("p (a b) -> p a b", a=2), sinb, ALU.mult)
                dve_step(nc.vector.tensor_tensor(r2, fm[0:32, 2 * m:2 * m + 2, :], cosb, ALU.mult))
                nc.vector.tensor_tensor(fm[0:32, 2 * m:2 * m + 2, :], r1, r2, ALU.add).then_inc(S["roped"], 1)
                dve.wait_ge(S["roped"], m + 1)

            def take_a(h):
                if h == 0:
                    dve.wait_ge(S["silu_za"], 1)
                dve.wait_ge(S["head_out"], h + 1)
                nc.vector.tensor_tensor(oat[:, h, :], ps[:, 4 + h % 2, 0:T], fm[:, 16 + h, :], ALU.mult).then_inc(S["head_taken"], 1)

            attention_dve(dve, 0, float(P) ** -0.5, take_a)
            dve.wait_ge(S["conv_turned"], 1)
            nc.vector.tensor_copy(cw[:, :], ps[:, 7, 0:96])
            stage.end()
            for c in range(8):
                if c < 6:
                    moves.take(4, lambda i, b: copy_out(dve, fm[:, 4 * c + i, :], ps[:, b, 0:T]))
                else:
                    moves.take(2, lambda i, b: copy_out(dve, zb[:, i, BANK * (c - 6):BANK * (c - 6) + BANK], ps[:, b, :]))
                if 1 <= c < 7:
                    conv_dve(dve, c - 1)
            dve.wait_ge(S["bd_logits"], 1)
            nc.vector.tensor_copy(bd[:, 0, :].rearrange("p (t h) -> p t h", t=NT), ps[:, 7, 0:32].rearrange("p (t a h) -> p t a h", t=NT, a=2)[:, :, 0, :])
            nc.vector.tensor_copy(bd[:, 1, :].rearrange("p (t h) -> p t h", t=NT), ps[:, 7, 0:32].rearrange("p (t a h) -> p t a h", t=NT, a=2)[:, :, 1, :])
            stage.end()
            gdn_dve(dve, stage, moves)
            dve.wait_ge(S["oat_high"], 1)
            nc.vector.tensor_tensor(oat_r[:, :, :], oat[:, :, :], oat_high_r.bitcast(F32), ALU.subtract).then_inc(S["oat_low"], 1)
            moves.skip(8)
            dve.wait_ge(S["moved0"], moves.u // 2)
            dve.wait_ge(S["moved1"], moves.u // 2)

            def gated(i, b):
                t, c = i % 2, BANK * (i % 4 // 2)
                return nc.vector.tensor_tensor((va, zb)[i // 4][:, t, c:c + BANK], ps[:, b, :], gates[:, i // 4, t, c:c + BANK], ALU.mult)

            moves.take(8, gated, whole=True)
            dve.wait_ge(S["moved1"], moves.u // 2)
            nc.vector.tensor_tensor(va[:, :, :], va[:, :, :], zb[:, :, :], ALU.add)
            stage.end()
            turn_dve(dve, ht_r, KD, low=ht_low2_r)
            stage.end()
            moves.take(4, lambda i, b: copy_out(dve, va[:, i % 2, BANK * (i // 2):BANK * (i // 2) + BANK], ps[:, b, :]))
            stage.end()
            norm_dve(dve, va, [(0, D)], None)
            dve.wait_ge(S["row_in"], 16)
            for t in range(NT):
                dve_step(nc.vector.scalar_tensor_tensor(out=va[:, t, :], in0=va[:, t, :], scalar=ssq[:, t:t + 1], in1=extra[:, 2, 0:D], op0=ALU.mult, op1=ALU.mult))
            nc.vector.tensor_tensor(xs[:, :, :], xs[:, :, :], va[:, :, :], ALU.add)
            stage.end()
            block2_dve(dve, stage, moves)
            moe_dve(dve, stage)
            tail_dve(dve, stage, moves)


_INS = ["x", "pre_norm_w", "w_in", "conv_w", "a_log", "dt_bias", "gdn_norm_w", "w_branch_a", "w_branch_b", "w_out",
        "post_norm_w", "p_2", "positions_2", "w_in_2", "g_attn_2", "g_cq_2", "w_uq_2", "g_ckv_2", "w_ukv_2",
        "g_out_mla_2", "g_out_sb_2", "w_o_2", "g_moe_2", "w_router_2", "b_router_2", "w_gu_2", "b_gu_2", "w_dn_2",
        "b_dn_2", "g_ple_2", "w_ple_gate_2", "w_ple_proj_2", "g_final_2"]
_OUT = ((1, T, D), "float32")


def kernel(**inputs):
    import numpy as _np
    import concourse.bacc as _bacc
    from concourse import mybir as _mybir
    from concourse.bass_utils import run_bass_kernel_spmd as _run

    nc = _bacc.Bacc("TRN2", target_bir_lowering=False, num_devices=1)
    arrays, tensors = {}, {}
    for name in _INS + ["const"]:
        a = constants()[0] if name == "const" else _np.ascontiguousarray(inputs[name])
        arrays[f"in_{name}_dram"] = a
        tensors[name] = nc.dram_tensor(f"in_{name}_dram", a.shape, _mybir.dt.from_np(a.dtype), kind="ExternalInput").ap()
    shape, dtype = _OUT
    out = nc.dram_tensor("out_0_dram", shape, _mybir.dt.from_np(_np.dtype(dtype)), kind="ExternalOutput").ap()
    hybrid_two_block_kernel(nc, tensors, out)
    r = _run(nc, [arrays], core_ids=[0])
    return r.results[0]["out_0_dram"]
```

```python
from contextlib import ExitStack

import numpy as np

import concourse.bass as bass
from concourse import mybir

P = 128
T = 256
NT = T // P
D = 1024
KD = D // P
HEADS = 8
CHUNK = 64
BANK = 512
NEXP = 32
CAP = 64
LAST_STAGE = 26
SMALL_LOADS = 15
AHEAD = 6
MAXROUND = T // CAP
MAXOVER = 1024 // CAP
QR, KVR = 384, 256
TWO_PI = 2.0 * np.pi
EPS = 1e-6
NEG = -1e30

F32 = mybir.dt.float32
BF16 = mybir.dt.bfloat16
F32R = mybir.dt.float32r
I32 = mybir.dt.int32
U32 = mybir.dt.uint32
ALU = mybir.AluOpType
ACT = mybir.ActivationFunctionType
AX = mybir.AxisListType.X

PI_A, PI_B = 6.28125, 0.00193023681640625
PI_C = TWO_PI - PI_A - PI_B
PI_IN = 3.1415925
ROUND = 1.5 * 2.0 ** 23

LEVELS = (1, 2, 4, 8, 16, 32)


def constants():
    r, c = np.arange(P)[:, None], np.arange(P)[None, :]
    same = (r // CHUNK) == (c // CHUNK)
    causal = np.where(c <= r, 0.0, NEG)
    parts = {
        "ident": r == c,
        "ones": np.ones((P, P)),
        "causal": np.concatenate([causal, np.zeros((P, P)), causal], 1),
        "strict": np.concatenate([r < c, np.ones((P, P)), r < c], 1),
        "upto": same & (r <= c),
        "chunk": same,
        "later": r > c,
        "earlier": r < c,
    }
    for s in LEVELS:
        parts[f"level{s}"] = (c // s % 2 == 1) & (r // s == c // s - 1)
    rot = np.zeros((P, 32))
    for base in (0, 64):
        for i in range(16):
            rot[base + 16 + i, i] = -1.0
            rot[base + i, 16 + i] = 1.0
    parts["rot"] = rot
    half = np.arange(P) % 16
    inv1 = np.power(np.float32(500000.0), -half.astype(np.float32) * np.float32(2.0 / 32)).astype(np.float32)
    ang = np.arange(T, dtype=np.float32)[None, :] * inv1[:, None]
    parts["cos"], parts["sin"] = np.cos(ang), np.sin(ang)
    parts["freq"] = np.power(np.float32(10000.0), -(2 * half).astype(np.float32) / np.float32(32))[:, None]
    parts["slots"] = np.broadcast_to(np.arange(CAP * (MAXROUND + 1)), (P, CAP * (MAXROUND + 1)))
    parts["row"] = np.arange(P)[:, None]
    parts["small"] = np.broadcast_to([EPS, P * EPS, 1.0, CAP, 2.0 * CAP, 3.0 * CAP], (P, 6))
    parts["bsel"] = (r % NEXP == c[:, :NEXP]) & (r < 3 * NEXP)
    at, cols = 0, {}
    for name, a in parts.items():
        cols[name] = (at, at + a.shape[1])
        at += a.shape[1]
    return np.concatenate([np.asarray(a, np.float32) for a in parts.values()], 1), cols


class Steps:

    def __init__(self, eng, sem):
        self.eng, self.sem, self.n = eng, sem, 0

    def __call__(self, ins):
        self.n += 1
        ins.then_inc(self.sem, 1)
        self.eng.wait_ge(self.sem, self.n)


class Stage:

    def __init__(self, eng, sem):
        self.eng, self.sem, self.n = eng, sem, 0

    def end(self):
        self.n += 1
        self.eng.drain().then_inc(self.sem, 1)
        self.eng.wait_ge(self.sem, 4 * self.n)


def hybrid_two_block_kernel(nc, I, out):
    const_np, CC = constants()
    with ExitStack() as ctx:
        def sb(name, shape, dt=F32):
            return ctx.enter_context(nc.sbuf_tensor(name, shape, dt))

        def sb_both(name, shape):
            at = nc.sbuf_base + -nc.sbuf_base % 32
            plain = sb(name, shape)
            return plain, nc.alloc_sbuf_tensor_at(name + "_r", shape, F32R, offset=at)

        class Sems(dict):
            def __missing__(self, name):
                self[name] = ctx.enter_context(nc.semaphore(name))
                return self[name]

        S = Sems()

        ring, ring_r = sb_both("ring", [P, 6, 4096])
        fm, fm_r = sb_both("fm", [P, 24, T])
        va, va_r = sb_both("va", [P, NT, D])
        zb, zb_r = sb_both("zb", [P, NT, D])
        oat, oat_r = sb_both("oat", [P, HEADS, T])
        xs = sb("xs", [P, NT, D])
        ht, ht_r = sb_both("ht", [P, KD, T])
        extra, extra_r = sb_both("extra", [P, 3, 2048])
        cst = sb("cst", [P, const_np.shape[1]])
        cw = sb("cw", [P, 96])
        wbd = sb("wbd", [P, KD, 16])
        cols = sb("cols", [P, 64])
        hsc = sb("hsc", [P, 16])
        ssq = sb("ssq", [P, 32])
        rsd = sb("rsd", [P, 32])
        nmx = sb("nmx", [P, HEADS, 2])
        sums = sb("sums", [P, HEADS, 2])
        rsum = sb("rsum", [P, HEADS, 2])
        bd = sb("bd", [P, 6, NT * HEADS])
        ps = ctx.enter_context(nc.psum_tensor("ps", [P, 8, BANK], F32))

        def con(name, rows=slice(0, P)):
            a, b = CC[name]
            return cst[rows, a:b]

        def con_at(name, first, n):
            return cst[:, bass.ds(first + CC[name][0], n)]

        def arena(i):
            return ring[:, 2 + i // 2, 2048 * (i % 2):2048 * (i % 2) + 2048]

        ident = con("ident")
        gates = fm[:, 0:16, :].rearrange("p a b -> p (a b)").rearrange("p (g t d) -> p g t d", g=2, t=NT)
        w_pre, w_gdn, g_attn, g_cq, g_ckv = (cols[:, a:b] for a, b in ((0, 8), (8, 9), (10, 18), (18, 21), (21, 23)))
        g_mix, g_moe, g_ple = (cols[:, a:b] for a, b in ((24, 32), (32, 40), (40, 48)))
        brow = sb("brow", [P, NEXP])
        posi = sb("posi", [P, T], I32)

        w_in = I["w_in"][0].rearrange("(p k) n -> p k n", k=KD)

        def pk_rows(name, k):
            return I[name][0].rearrange("(p k) n -> p k n", k=k)

        def head_rows(name):
            return I[name][0].rearrange("(h p) n -> p h n", p=P)

        class Chunk:
            pass

        plan = []
        slot_user, slot_loads = {}, {}

        def stream(src, c0, units, n=BANK, k=KD, split=True, slots=None):
            c = Chunk()
            g = c.g = len(plan)
            c.k, c.n, c.split = k, n, split
            c.first = plan[-1].done if plan else 0
            c.done = c.first + units
            c.slot = (g + 2) % 3 if split else g % 2
            c.high_slot = 3 + (g + 1) % 3 if split else None
            if slots:
                c.slot, c.high_slot = slots
            c.free = slot_user.get(c.slot)
            c.high_free = slot_user.get(c.high_slot)
            slot_user[c.slot] = c.done
            if split:
                slot_user[c.high_slot] = c.done
            c.load = slot_loads[c.slot] = slot_loads.get(c.slot, 0) + 1
            c.flat = ring[:, c.slot, 0:k * n]
            c.dst = c.flat.rearrange("p (k n) -> p k n", k=k)
            c.src = src[:, :, c0:c0 + n]
            c.nth = sum(q.split for q in plan) + 1
            plan.append(c)

        for c in (0, 1, 2, 3, 6, 7):
            stream(w_in, BANK * c, 4)
        for c in (4, 5):
            stream(w_in, BANK * c, 2)
        in_attention = len(plan)
        stream(w_in, BANK * 14, 2)
        for c in range(8, 14):
            stream(w_in, BANK * c, 4)
        stream(w_in, BANK * 15, 2)
        after_gdn = len(plan)
        for c in range(4):
            stream(w_in, 16 * BANK + 16 + BANK * c, 2)
        for name in ("w_branch_a", "w_branch_b"):
            for c in (0, 1):
                stream(head_rows(name), BANK * c, 2)
        for c in (0, 1):
            stream(pk_rows("w_out", KD), BANK * c, 2)
        w_in2 = pk_rows("w_in_2", KD)
        stream(w_in2, 0, 2, QR)
        stream(w_in2, QR, 3, KVR + 32)
        stream(w_in2, QR + KVR + 32, 4)
        stream(w_in2, QR + KVR + 32 + BANK, 4)
        stream(w_in2, QR + KVR + 32 + 2 * BANK, 2)
        stream(pk_rows("w_uq_2", QR // P), 0, 8, 96 * HEADS, QR // P, split=False)
        stream(pk_rows("w_ukv_2", KVR // P), 0, 10, P * HEADS, KVR // P, split=False)
        for c in (0, 1):
            stream(pk_rows("w_o_2", KD), BANK * c, 2, split=False)

        before_experts = len(plan)
        stream(pk_rows("w_ple_proj_2", 2), 0, 4, D, 2, split=False, slots=(4, None))
        for c in (0, 1):
            stream(pk_rows("w_ple_gate_2", KD), BANK * c, 2, slots=(c, 2 + c))

        def bank_of(u):
            tail = plan[before_experts].first
            return (u - tail + 4) % 8 if u >= tail else u % 8


        block = ctx.enter_context(nc.Block())

        class Products:

            def __init__(self, pe):
                self.pe, self.g, self.u = pe, 0, 0

            def chunk(self, units, a):
                c = plan[self.g]
                if c.split:
                    self.pe.wait_ge(S["split_low"], c.nth)
                    high, low = (ring_r[:, q, 0:c.k * c.n].rearrange("p (k n) -> p k n", k=c.k) for q in (c.high_slot, c.slot))
                    terms = ((high, a[0]), (high, a[1]), (low, a[0]))
                else:
                    self.pe.wait_ge(S[f"chunk_in{c.slot}"], 16 * c.load)
                    terms = ((c.dst, a),)
                for r0, rows, width, lhs, rhs in units:
                    if self.u >= 8:
                        self.pe.wait_ge(S[f"moved{self.u % 2}"], (self.u - 8) // 2 + 1)
                    for j in range(c.k):
                        for i, (w, x) in enumerate(terms):
                            last = self.pe.matmul(ps[r0:r0 + rows, bank_of(self.u), 0:width], lhs(w, x, j), rhs(w, x, j),
                                                  start=(j == 0 and i == 0), stop=(j == c.k - 1 and i == len(terms) - 1))
                    last.then_inc(S["unit"], 1)
                    self.u += 1
                assert self.u == c.done
                self.g += 1

            def slice(self, a, i, slices, bank):
                c = plan[self.g]
                if i == 0:
                    self.pe.wait_ge(S["split_low"], c.nth)
                high, low = (ring_r[:, q, :].rearrange("p (k n) -> p k n", k=c.k) for q in (c.high_slot, c.slot))
                for step in range(NT * c.k * i // slices, NT * c.k * (i + 1) // slices):
                    t, j = step // c.k, step % c.k
                    for m, (w, x) in enumerate(((high, a[0]), (high, a[1]), (low, a[0]))):
                        last = self.pe.matmul(ps[:, bank + t, :], x[:, j, P * t:P * t + P], w[:, j, :], start=(j == 0 and m == 0), stop=(j == c.k - 1 and m == 2))
                    if j == c.k - 1:
                        last.then_inc(S["unit"], 1)
                        self.u += 1
                if self.u == c.done:
                    self.g += 1

            def fm_units(self, tiles=4, m=P, at=0, step=None):
                return [(0, m, T, lambda w, x, j, f=f: w[:, j, at + (step or m) * f:at + (step or m) * f + m],
                         lambda w, x, j: x[:, j, :]) for f in range(tiles)]

            def tm_units(self, width=BANK, cols=lambda w, j: w[:, j, :]):
                return [(0, P, width, lambda w, x, j, t=t: x[:, j, P * t:P * t + P], lambda w, x, j: cols(w, j)) for t in range(NT)]

            def feature_major(self, a, tiles=4):
                self.chunk(self.fm_units(tiles), a)

            def token_major(self, a, n=BANK):
                self.chunk(self.tm_units(n), a)

        class Moves:

            def __init__(self, eng, parity):
                self.eng, self.parity, self.u = eng, parity, 0

            def split(self, g):
                c = plan[g]
                high_r, low_r = (ring_r[:, q, 0:c.k * c.n] for q in (c.high_slot, c.slot))
                if self.parity == 0:
                    self.eng.wait_ge(S[f"chunk_in{c.slot}"], 16 * c.load)
                    if c.high_free:
                        self.eng.wait_ge(S["unit"], c.high_free)
                    nc.scalar.activation(high_r, c.flat, ACT.Copy).then_inc(S["split_high"], 1)
                elif g != in_attention + 2 or self.eng is nc.gpsimd:
                    self.eng.wait_ge(S["split_high"], c.nth)
                    self.eng.tensor_tensor(low_r, c.flat, high_r.bitcast(F32), ALU.subtract).then_inc(S["split_low"], 1)

            def ahead(self):
                for c in plan:
                    if c.first == self.u and c.g + 2 != in_attention + 1 and c.g + 2 < before_experts and plan[c.g + 2].split and not c.g < after_gdn <= c.g + 2:
                        self.split(c.g + 2)

            def take(self, n, move, whole=False):
                for i in range(n):
                    self.ahead()
                    if whole or self.u % 2 == self.parity:
                        self.eng.wait_ge(S["unit"], self.u + 1)
                        move(i, bank_of(self.u)).then_inc(S[f"moved{self.u % 2}"], 1)
                    self.u += 1

            def skip(self, n):
                for _ in range(n):
                    self.ahead()
                    self.u += 1

        def copy_out(eng, dst, src):
            if eng is nc.scalar:
                return nc.scalar.activation(dst, src, ACT.Copy)
            return nc.vector.tensor_copy(dst, src)

        def as_token_major(buf):
            return buf.rearrange("p a b -> p (a b)").rearrange("p (t d) -> p t d", t=NT)

        oat_tm = as_token_major(oat[:, :, :])

        norm_calls = {"act": 0, "dve": 0, "pe": 0}

        def norm_act(act, src, segs, junk, t0=0):
            n = norm_calls["act"]; norm_calls["act"] += 1
            for t in range(NT):
                for s, (c0, w) in enumerate(segs):
                    last = nc.scalar.activation(junk[:, 0:w], src[:, t, c0:c0 + w], ACT.Square,
                                                accum_out=ssq[:, t * len(segs) + s:t * len(segs) + s + 1])
                    act_step(last)
            m = NT * len(segs)
            w = segs[0][1]
            nc.scalar.activation(rsd[:, 0:m], ssq[:, 0:m], ACT.Sqrt, scale=1.0 / w,
                                 bias=con("small")[:, 0:1]).then_inc(S["rms_root"], 1)

        def norm_dve(dve, src, segs, dst):
            n = norm_calls["dve"]; norm_calls["dve"] += 1
            m = NT * len(segs)
            dve.wait_ge(S["rms_root"], n + 1)
            dve_step(nc.vector.reciprocal(ssq[:, 0:m], rsd[:, 0:m]))
            if dst is None:
                return
            for t in range(NT):
                for s, (c0, w) in enumerate(segs):
                    i = t * len(segs) + s
                    last = nc.vector.tensor_scalar(dst[:, t, c0:c0 + w], src[:, t, c0:c0 + w], ssq[:, i:i + 1], None, ALU.mult)
            last.then_inc(S["normed"], 1)

        turned = {"pe": 0, "act": 0, "dve": 0, "high": 0}

        def turn_pe(pe, src, K, b0=0):
            for k in range(K):
                for t in range(NT):
                    last = pe.transpose(ps[:, b0 + k // 2, (k % 2) * T + P * t:(k % 2) * T + P * t + P],
                                        src[:, t, k:k + K * (P - 1) + 1:K], ident)
                if k % 2 or k == K - 1:
                    last.then_inc(S["turned"], 1)
            turned["pe"] += (K + 1) // 2

        def turn_dve(dve, dst, K, w_col=None, b0=0, done=None):
            for k in range(K):
                src = ps[:, b0 + k // 2, (k % 2) * T:(k % 2) * T + T]
                if k % 2 == 0:
                    turned["dve"] += 1
                    dve.wait_ge(S["turned"], turned["dve"])
                if w_col is None:
                    last = nc.vector.tensor_copy(dst[:, k, :], src)
                else:
                    last = nc.vector.tensor_scalar(dst[:, k, :], src, w_col[:, k:k + 1], None, ALU.mult)
            if done:
                last.then_inc(S[done], 1)

        def turn_high(act, dst_r, w_col, b0=0, before=0, heads=False):
            turned["act"] += before
            for b in range(KD // 2):
                turned["act"] += 1
                act.wait_ge(S["turned"], turned["act"])
                for k in (2 * b, 2 * b + 1):
                    scale = 1.0 if w_col is None else w_col[:, 0:1] if heads else w_col[:, k:k + 1]
                    last = nc.scalar.activation(dst_r[:, k, :], ps[:, b0 + b, (k % 2) * T:(k % 2) * T + T], ACT.Copy, scale=scale)
                last.then_inc(S["high"], 1)

        def turn_low(dve, high_r, low_r, w_col, b0=0, heads=False):
            for b in range(KD // 2):
                turned["dve"] += 1
                turned["high"] += 1
                dve.wait_ge(S["high"], turned["high"])
                for k in (2 * b, 2 * b + 1):
                    scale = 1.0 if w_col is None else w_col[:, 0:1] if heads else w_col[:, k:k + 1]
                    last = nc.vector.scalar_tensor_tensor(out=low_r[:, k, :], in0=ps[:, b0 + b, (k % 2) * T:(k % 2) * T + T], scalar=scale,
                                                          in1=high_r[:, k, :].bitcast(F32), op0=ALU.mult, op1=ALU.subtract)
            return last

        def as_feature_major(buf):
            return buf.rearrange("p t d -> p (t d)").rearrange("p (k n) -> p k n", k=KD)

        ht_low_r, ht_low2_r = (as_feature_major(b[:, :, :]) for b in (va_r, zb_r))
        ht_parts, ht_parts2 = (ht_r, ht_low_r), (ht_r, ht_low2_r)

        ROPE_POOL = (1, 3, 5, 7)
        cosb = con("cos", slice(0, 32)).unsqueeze(1).to_broadcast([32, 2, T])

        def rope_scratch(m):
            blocks = [extra[0:32, i, 512 * q:512 * q + 512].rearrange("p (a b) -> p a b", a=2)
                      for i, q in ((1, 0), (1, 1), (2, 1), (1, 2), (1, 3), (2, 2), (2, 3))]
            if m in ROPE_POOL:
                return blocks[2], blocks[3 + ROPE_POOL.index(m)]
            return blocks[0], blocks[1]

        dve_steps, act_steps = [None], [None]

        def dve_step(ins):
            dve_steps[0](ins)

        def act_step(ins):
            act_steps[0](ins)

        sc_buf, pt_buf = [extra[:, 0, 384 * i:384 * i + 384] for i in range(2)], [extra[:, 0, 768 + 384 * i:1152 + 384 * i] for i in range(2)]

        def attention_pe(pe, h0, q, k, out_product, between=None):
            def scores(i):
                if h0 + i >= 2:
                    pe.wait_ge(S["scores_read"], h0 + i - 1)
                b = ps[:, i % 2, :]
                pe.matmul(b[:, 0:P], q(i)[:, 0:P], k(i)[:, 0:P], start=True, stop=True)
                pe.matmul(b[:, P:3 * P], q(i)[:, P:T], k(i)[:, 0:T], start=True, stop=True).then_inc(S["scores"], 1)

            scores(0)
            for i in range(HEADS + 2):
                if i + 1 < HEADS:
                    scores(i + 1)
                if between and i < HEADS:
                    between(i)
                if 1 <= i <= HEADS:
                    h = i - 1
                    pe.wait_ge(S["weights"], h0 + h + 1)
                    if h0 + h >= 2:
                        pe.wait_ge(S["weights_t"], h0 + h - 1)
                    for j in range(3):
                        last = pe.transpose(ps[:, 2 + h % 2, P * j:P * j + P], sc_buf[h % 2][:, P * j:P * j + P], ident)
                    last.then_inc(S["weights_turned"], 1)
                if i >= 2:
                    h = i - 2
                    pe.wait_ge(S["weights_t"], h0 + h + 1)
                    out_product(h, pt_buf[h % 2]).then_inc(S["head_out"], 1)

        def attention_act(act, h0, between=None):
            for i in range(HEADS + 1):
                if between:
                    between(i)
                if i < HEADS:
                    act.wait_ge(S["maxima"], h0 + i + 1)
                    for t, (a, b) in enumerate(((0, P), (P, 3 * P))):
                        last = nc.scalar.activation(sc_buf[i % 2][:, a:b], sc_buf[i % 2][:, a:b], ACT.Exp,
                                                    bias=nmx[:, i, t:t + 1], accum_out=sums[:, i, t:t + 1])
                    last.then_inc(S["exps"], 1)
                if i >= 1:
                    h = i - 1
                    act.wait_ge(S["weights_turned"], h0 + h + 1)
                    if h0 + h >= 2:
                        act.wait_ge(S["head_out"], h0 + h - 1)
                    nc.scalar.activation(pt_buf[h % 2], ps[:, 2 + h % 2, 0:3 * P], ACT.Copy).then_inc(S["weights_t"], 1)

        def attention_dve(dve, h0, scale, take_out, between=None):
            for i in range(HEADS + 2):
                if between:
                    between(i)
                if i < HEADS:
                    dve.wait_ge(S["scores"], h0 + i + 1)
                    if h0 + i >= 2:
                        dve.wait_ge(S["weights_turned"], h0 + i - 1)
                    nc.vector.scalar_tensor_tensor(out=sc_buf[i % 2], in0=ps[:, i % 2, 0:3 * P], scalar=scale,
                                                   in1=con("causal"), op0=ALU.mult, op1=ALU.add).then_inc(S["scores_read"], 1)
                    dve.wait_ge(S["scores_read"], h0 + i + 1)
                    dve_step(nc.vector.tensor_reduce(nmx[:, i, 0:1], sc_buf[i % 2][:, 0:P], AX, ALU.max, negate=True))
                    nc.vector.tensor_reduce(nmx[:, i, 1:2], sc_buf[i % 2][:, P:3 * P], AX, ALU.max, negate=True).then_inc(S["maxima"], 1)
                if 1 <= i <= HEADS:
                    h = i - 1
                    dve.wait_ge(S["exps"], h0 + h + 1)
                    dve_step(nc.vector.reciprocal(rsum[:, h, :], sums[:, h, :]))
                    b = sc_buf[h % 2]
                    nc.vector.tensor_scalar(b[:, 0:P], b[:, 0:P], rsum[:, h, 0:1], None, ALU.mult)
                    nc.vector.tensor_scalar(b[:, P:3 * P], b[:, P:3 * P], rsum[:, h, 1:2], None, ALU.mult).then_inc(S["weights"], 1)
                if i >= 2:
                    take_out(i - 2)

        bt, gd, Gc, Gd, eG, bG = (bd[:, i, :] for i in range(6))
        gl = sb("gl", [P, 4, HEADS])
        SYS = NT * HEADS

        def systems(buf):
            return buf.rearrange("p (s i) -> p s i", s=SYS)

        kbg, kdec, vbt = (systems(extra[:, i, :]) for i in range(3))
        egr, dk, mt, qkt = (systems(arena(i)) for i in range(4))
        xi, xt, yy, bb = (systems(arena(i)) for i in range(4, 8))
        nwt, uu = yy, bb
        vnew = arena(2)[:, 0:D].rearrange("p (h i) -> p h i", h=HEADS)
        state = arena(2)[:, D:2 * D].rearrange("p (h i) -> p h i", h=HEADS)
        oo = xi
        obt_r, obt_low_r = (extra_r[:, i, :].rearrange("p (h n) -> p h n", h=HEADS) for i in range(2))
        oat_high_r = fm_r[:, 16:24, :]

        def four(b):
            return ps[:, b, :].rearrange("p (s i) -> p s i", s=4)

        def over4(col, g):
            return col[:, 4 * g:4 * g + 4].unsqueeze(2).to_broadcast([P, 4, P])

        def conv_act(act, c, moves):
            act.wait_ge(S["moved0"], moves.u // 2)
            act.wait_ge(S["moved1"], moves.u // 2)
            if c == 2:
                act.wait_ge(S["zb_moved"], 1)
            for i in range(4 * c, 4 * c + 4):
                last = nc.scalar.activation(conv_sum(i), fm[:, i, :], ACT.Copy, scale=cw[:, 72 + i:73 + i])
            last.then_inc(S["tap3"], 1)

        def conv_dve(dve, c):
            dve.wait_ge(S["tap3"], c + 1)
            for back in (1, 2, 3):
                for i in range(4 * c, 4 * c + 4):
                    k = 24 * (3 - back) + i
                    last = nc.vector.scalar_tensor_tensor(out=conv_sum(i)[:, back:T], in0=fm[:, i, 0:T - back], scalar=cw[:, k:k + 1],
                                                          in1=conv_sum(i)[:, back:T], op0=ALU.mult, op1=ALU.add)
                if back < 3:
                    dve_step(last)
            last.then_inc(S["conv"], 1)

        def conv_sum(i):
            return extra[:, i // 8, T * (i % 8):T * (i % 8) + T]

        def wide(buf):
            return buf.rearrange("p (c n) -> p c n", c=HEADS)

        def seen_by(t, h):
            return lambda base: fm[:, base + h, P * t:P * t + P]

        def gdn_pool(pool, stage):
            stage.end()
            pool.wait_ge(S["decay"], 1)
            nc.gpsimd.tensor_tensor(dk, dk, con("upto").unsqueeze(1).to_broadcast([P, SYS, P]), ALU.mult).then_inc(S["decay_masked"], 1)
            pool.wait_ge(S["glast"], 1)
            nc.gpsimd.tensor_tensor(egr.rearrange("p (t h) i -> p h t i", t=NT), egr.rearrange("p (t h) i -> p h t i", t=NT),
                                    fm[:, 0:8, :].rearrange("p h (t i) -> p h t i", t=NT), ALU.mult)
            stage.end()
            for n in range(len(LEVELS) * 4):
                l, g = n // 4, n % 4
                if n >= 8:
                    pool.wait_ge(S["y_ps"], n - 7)
                elif n >= 4:
                    pool.wait_ge(S["x_done"], n - 3)
                nc.gpsimd.tensor_tensor(bb[:, 4 * g:4 * g + 4, :], mt[:, 4 * g:4 * g + 4, :],
                                        con(f"level{LEVELS[l]}").unsqueeze(1).to_broadcast([P, 4, P]), ALU.mult).then_inc(S["b_ready"], 1)
            stage.end()
            nc.gpsimd.memset(arena(2), 0.0).then_inc(S["zeroed"], 1)
            stage.end()

        def gdn_pe(pe, stage):
            for G in range(2):
                pe.wait_ge(S["squares"], G + 1)
                for s in range(SYS):
                    t, h = s // HEADS, s % HEADS
                    last = pe.matmul(ps[:, 0, SYS * G + s:SYS * G + s + 1], wide(arena(3 + G))[:, h, P * t:P * t + P], con("ones")[:, 0:1], start=True, stop=True)
            last.then_inc(S["sq_sums"], 1)
            pe.wait_ge(S["scales"], 1)
            for G in range(2):
                for h in range(HEADS):
                    for t in range(NT):
                        c = SYS * G + HEADS * t + h
                        last = pe.matmul(ps[:, 4 * G + h // 2, T * (h % 2) + P * t:T * (h % 2) + P * t + P], rsd[:, c:c + 1].to_broadcast([P, P]), ident,
                                         start=True, stop=True)
                last.then_inc(S["scale_rows"], 1)
            stage.end()
            for t in range(NT):
                cs = slice(HEADS * t, HEADS * t + HEADS)
                pe.matmul(ps[:, 0, HEADS * t:HEADS * t + HEADS], con("upto"), gd[:, cs], start=True, stop=True)
                last = pe.matmul(ps[:, 0, 16 + HEADS * t:16 + HEADS * t + HEADS], con("chunk"), gd[:, cs], start=True, stop=True)
            last.then_inc(S["g_sums"], 1)
            for s in range(SYS):
                t, h = s // HEADS, s % HEADS
                last = pe.transpose(four(4 + s // 4)[:, s % 4, :], seen_by(t, h)(8), ident)
                if s % 4 == 3:
                    last.then_inc(S["k_turned"], 1)
            pe.wait_ge(S["g_read"], 1)
            for s in range(SYS):
                t, h = s // HEADS, s % HEADS
                last = pe.transpose(four(s // 4)[:, s % 4, :], seen_by(t, h)(16), ident)
                if s % 4 == 3:
                    last.then_inc(S["v_turned"], 1)
            for s in range(SYS):
                if s % 4 == 0:
                    pe.wait_ge(S["k_read"], s // 4 + 1)
                last = pe.matmul(four(4 + s // 4)[:, s % 4, :], gd[:, s:s + 1].to_broadcast([P, P]), con("upto"), start=True, stop=True)
                if s % 4 == 3:
                    last.then_inc(S["g_rows"], 1)
            for s in range(SYS):
                if s % 4 == 0:
                    pe.wait_ge(S["v_read"], s // 4 + 1)
                last = pe.matmul(four(s // 4)[:, s % 4, :], bt[:, s:s + 1].to_broadcast([P, P]), ident, start=True, stop=True)
            last.then_inc(S["beta_rows"], 1)
            for s in range(SYS):
                t, h = s // HEADS, s % HEADS
                if s % 4 == 0:
                    pe.wait_ge(S["rows_read_act"], s // 4 + 1)
                    pe.wait_ge(S["rows_read_dve"], s // 4 + 1)
                last = pe.matmul(four(4 + s // 4)[:, s % 4, :], seen_by(t, h)(8), seen_by(t, h)(8), start=True, stop=True)
                if s % 4 == 3:
                    last.then_inc(S["kk"], 1)
            for s in range(SYS):
                t, h = s // HEADS, s % HEADS
                if s % 4 == 0:
                    pe.wait_ge(S["kk_read"], s // 4 + 1)
                last = pe.matmul(four(4 + s // 4)[:, s % 4, :], seen_by(t, h)(8), seen_by(t, h)(0), start=True, stop=True)
                if s % 4 == 3:
                    last.then_inc(S["qk"], 1)
            stage.end()
            for l in range(len(LEVELS)):
                for i in range(5):
                    if i < 4 and l > 0:
                        g = i
                        pe.wait_ge(S["b_ready"], 4 * l + g + 1)
                        pe.wait_ge(S["x_done"], 4 * (l - 1) + g + 1)
                        for q in range(4):
                            last = pe.matmul(four(g)[:, q, :], bb[:, 4 * g + q, :], xi[:, 4 * g + q, :], start=True, stop=True)
                        last.then_inc(S["y_ps"], 1)
                    if i >= 1:
                        g = i - 1
                        n = 4 * l + g
                        if n >= 2:
                            pe.wait_ge(S["x_done"], n - 1)
                        if l == 0:
                            pe.wait_ge(S["b_ready"], g + 1)
                            for q in range(4):
                                last = pe.transpose(four(4 + g % 2)[:, q, :], bb[:, 4 * g + q, :], ident)
                        else:
                            pe.wait_ge(S["y_copied"], n - 3)
                            for q in range(4):
                                sys = 4 * g + q
                                if l < len(LEVELS) - 1:
                                    pe.matmul(four(4 + g % 2)[:, q, :], xt[:, sys, :], yy[:, sys, :], start=True, stop=True)
                                last = pe.matmul(four(6 + g % 2)[:, q, :], yy[:, sys, :], xt[:, sys, :], start=True, stop=True)
                        last.then_inc(S["z_ps"], 1)
            stage.end()
            for s in range(SYS):
                last = pe.matmul(four(s // 4)[:, s % 4, :], kbg[:, s, :], xt[:, s, :], start=True, stop=True)
                if s % 4 == 3:
                    last.then_inc(S["w_ps"], 1)
            for s in range(SYS):
                last = pe.matmul(four(4 + s // 4)[:, s % 4, :], xt[:, s, :], vbt[:, s, :], start=True, stop=True)
                if s % 4 == 3:
                    last.then_inc(S["u_ps"], 1)
            pe.wait_ge(S["w_moved"], 4)
            pe.wait_ge(S["u_moved"], 4)
            pe.wait_ge(S["zeroed"], 1)
            for c in range(4):
                t, r = c // 2, CHUNK * (c % 2)
                rows = slice(r, r + CHUNK)

                def at(b, h):
                    return ps[rows, b + h // 4, P * (h % 4):P * (h % 4) + P]

                if c:
                    pe.wait_ge(S["state"], c)
                for h in range(HEADS):
                    last = pe.matmul(at(0, h), nwt[:, HEADS * t + h, rows], state[:, h, :], start=True, stop=True)
                last.then_inc(S["ws"], 1)
                if c:
                    pe.wait_ge(S["o_moved"], c)
                for h in range(HEADS):
                    last = pe.matmul(at(2, h), egr[:, HEADS * t + h, rows], state[:, h, :], start=(h % 4 == 0), stop=False, skip_group_check=True)
                last.then_inc(S["state_read"], 1)
                pe.wait_ge(S["vnew"], c + 1)
                for h in range(HEADS):
                    last = pe.matmul(ps[:, 4 + h // 4, P * (h % 4):P * (h % 4) + P], kdec[rows, HEADS * t + h, :], vnew[rows, h, :], start=True, stop=True)
                last.then_inc(S["kv"], 1)
                for h in range(HEADS):
                    last = pe.matmul(at(2, h), qkt[:, HEADS * t + h, rows], vnew[:, h, :], start=False, stop=True, skip_group_check=True)
                last.then_inc(S["o_ps"], 1)
            stage.end()

        def gdn_act(act, stage, moves):
            for G in range(2):
                nc.scalar.activation(wide(arena(3 + G)), fm[:, 8 * G:8 * G + 8, :], ACT.Square).then_inc(S["squares"], 1)
            act.wait_ge(S["abs_z"], 1)
            act_step(nc.scalar.activation(Gd, Gd, ACT.Exp, scale=-1.0))
            nc.scalar.activation(hsc[:, 8:16], hsc[:, 8:16], ACT.Exp)
            nc.scalar.activation(Gd, Gd, ACT.Ln, bias=con("small")[:, 2:3]).then_inc(S["log_part"], 1)
            nc.scalar.activation(bt, bt, ACT.Sigmoid)
            act.wait_ge(S["sq_sums"], 1)
            for G in range(2):
                last = nc.scalar.activation(ssq[:, SYS * G:SYS * G + SYS], ps[:, 0, SYS * G:SYS * G + SYS], ACT.Sqrt,
                                            scale=(float(P), 1.0)[G], bias=con("small")[:, 1 - G:2 - G])
            last.then_inc(S["roots"], 1)
            stage.end()
            act.wait_ge(S["g_read"], 1)
            nc.scalar.activation(eG, Gc, ACT.Exp)
            nc.scalar.activation(Gd, Gd, ACT.Exp).then_inc(S["g_exp"], 1)
            for g in range(4):
                act.wait_ge(S["rows_read_dve"], g + 1)
                nc.scalar.activation(egr[:, 4 * g:4 * g + 4, :], four(4 + g), ACT.Exp).then_inc(S["rows_read_act"], 1)
            act.wait_ge(S["diffs"], 1)
            nc.scalar.activation(dk, dk, ACT.Exp).then_inc(S["decay"], 1)
            stage.end()
            for n in range(4 * (len(LEVELS) - 1)):
                g = n % 4
                act.wait_ge(S["y_ps"], n + 1)
                nc.scalar.activation(yy[:, 4 * g:4 * g + 4, :], four(g), ACT.Copy).then_inc(S["y_copied"], 1)
            stage.end()
            for g in range(4):
                act.wait_ge(S["w_ps"], g + 1)
                nc.scalar.activation(nwt[:, 4 * g:4 * g + 4, :], four(g), ACT.Copy, scale=-1.0).then_inc(S["w_moved"], 1)
            for c in range(4):
                t, r = c // 2, CHUNK * (c % 2)
                act.wait_ge(S["o_ps"], c + 1)
                nc.scalar.activation(oo[r:r + CHUNK, HEADS * t:HEADS * t + HEADS, :],
                                     ps[r:r + CHUNK, 2:4, :].rearrange("p b (h i) -> p (b h) i", h=4), ACT.Copy).then_inc(S["o_moved"], 1)
            stage.end()
            moves.split(after_gdn)
            nc.scalar.activation(egr, oo, ACT.Square).then_inc(S["o_sq"], 1)
            nc.scalar.activation(zb[:, :, :], zb[:, :, :], ACT.Silu).then_inc(S["silu_zb"], 1)
            act.wait_ge(S["o_sums"], 1)
            nc.scalar.activation(rsd[:, 0:SYS], ssq[:, 0:SYS], ACT.Sqrt, scale=1.0 / P, bias=con("small")[:, 0:1]).then_inc(S["o_root"], 1)
            moves.split(after_gdn + 1)
            turn_high(act, obt_r, w_gdn, 4, heads=True)

        def gdn_dve(dve, stage, moves):
            heads2 = [P, NT, HEADS]

            def by_head(a):
                return a.unsqueeze(1).to_broadcast(heads2)

            def th(a):
                return a.rearrange("p (t h) -> p t h", t=NT)

            dve_step(nc.vector.tensor_tensor(th(Gc), th(gd), by_head(hsc[:, 0:8]), ALU.add))
            nc.vector.scalar_tensor_tensor(out=Gd, in0=Gc, scalar=-1.0, in1=Gc, op0=ALU.mult, op1=ALU.max).then_inc(S["abs_z"], 1)
            dve_step(nc.vector.tensor_scalar(Gc, Gc, 0.0, None, ALU.max))
            dve.wait_ge(S["log_part"], 1)
            dve_step(nc.vector.tensor_tensor(Gc, Gc, Gd, ALU.add))
            nc.vector.scalar_tensor_tensor(out=th(gd), in0=th(Gc), scalar=-1.0, in1=by_head(hsc[:, 8:16]), op0=ALU.mult, op1=ALU.mult)
            dve.wait_ge(S["roots"], 1)
            nc.vector.reciprocal(rsd[:, 0:2 * SYS], ssq[:, 0:2 * SYS]).then_inc(S["scales"], 1)
            for G in range(2):
                dve.wait_ge(S["scale_rows"], G + 1)
                nc.vector.tensor_tensor(fm[:, 8 * G:8 * G + 8, :], fm[:, 8 * G:8 * G + 8, :],
                                        ps[:, 4 * G:4 * G + 4, :].rearrange("p b (h n) -> p (b h) n", h=2), ALU.mult)
            stage.end()
            dve.wait_ge(S["g_sums"], 1)
            dve_step(nc.vector.tensor_copy(Gc, ps[:, 0, 0:16]))
            nc.vector.tensor_tensor(Gd, ps[:, 0, 16:32], Gc, ALU.subtract).then_inc(S["g_read"], 1)
            dve.wait_ge(S["g_exp"], 1)
            dve_step(nc.vector.tensor_tensor(bG, bt, eG, ALU.mult))
            for g in range(4):
                dve.wait_ge(S["k_turned"], g + 1)
                nc.vector.tensor_tensor(kbg[:, 4 * g:4 * g + 4, :], four(4 + g), over4(bG, g), ALU.mult)
                nc.vector.tensor_tensor(kdec[:, 4 * g:4 * g + 4, :], four(4 + g), over4(Gd, g), ALU.mult).then_inc(S["k_read"], 1)
            for g in range(4):
                dve.wait_ge(S["v_turned"], g + 1)
                nc.vector.tensor_tensor(vbt[:, 4 * g:4 * g + 4, :], four(g), over4(bt, g), ALU.mult).then_inc(S["v_read"], 1)
            for g in range(4):
                dve.wait_ge(S["g_rows"], g + 1)
                nc.vector.tensor_tensor(dk[:, 4 * g:4 * g + 4, :], four(4 + g), over4(Gc, g), ALU.subtract).then_inc(S["rows_read_dve"], 1)
            dve.wait_ge(S["rows_read_dve"], 4)
            nc.vector.tensor_scalar(dk, dk, 0.0, None, ALU.min).then_inc(S["diffs"], 1)
            dve.wait_ge(S["decay_masked"], 1)
            dve.wait_ge(S["beta_rows"], 1)
            for g in range(4):
                dve.wait_ge(S["kk"], g + 1)
                nc.vector.tensor_tensor(mt[:, 4 * g:4 * g + 4, :], four(4 + g), dk[:, 4 * g:4 * g + 4, :], ALU.mult).then_inc(S["kk_read"], 1)
                dve.wait_ge(S["kk_read"], g + 1)
                nc.vector.tensor_tensor(mt[:, 4 * g:4 * g + 4, :], four(g), mt[:, 4 * g:4 * g + 4, :], ALU.mult)
            for g in range(4):
                dve.wait_ge(S["qk"], g + 1)
                nc.vector.tensor_tensor(qkt[:, 4 * g:4 * g + 4, :], four(4 + g), dk[:, 4 * g:4 * g + 4, :], ALU.mult)
            dve.wait_ge(S["rows_read_act"], 4)
            nc.vector.tensor_copy(gl[:, :, :].rearrange("p (t c) h -> p t h c", t=NT),
                                  egr.rearrange("p (t h) (c i) -> p t h c i", t=NT, c=2)[:, :, :, :, CHUNK - 1]).then_inc(S["glast"], 1)
            stage.end()
            eye4 = ident.unsqueeze(1).to_broadcast([P, 4, P])
            for n in range(4 * len(LEVELS)):
                g = n % 4
                gs = slice(4 * g, 4 * g + 4)
                dve.wait_ge(S["z_ps"], n + 1)
                if n < 4:
                    nc.vector.tensor_tensor(xt[:, gs, :], eye4, bb[:, gs, :], ALU.subtract)
                    last = nc.vector.tensor_tensor(xi[:, gs, :], eye4, four(4 + g % 2), ALU.subtract)
                else:
                    if n < 4 * (len(LEVELS) - 1):
                        nc.vector.tensor_tensor(xi[:, gs, :], xi[:, gs, :], four(4 + g % 2), ALU.subtract)
                    last = nc.vector.tensor_tensor(xt[:, gs, :], xt[:, gs, :], four(6 + g % 2), ALU.subtract)
                last.then_inc(S["x_done"], 1)
            stage.end()
            for g in range(4):
                dve.wait_ge(S["u_ps"], g + 1)
                nc.vector.tensor_copy(uu[:, 4 * g:4 * g + 4, :], four(4 + g)).then_inc(S["u_moved"], 1)
            dve.wait_ge(S["u_moved"], 4)
            dve.wait_ge(S["zeroed"], 1)
            for c in range(4):
                t, r = c // 2, CHUNK * (c % 2)
                rows = slice(r, r + CHUNK)
                dve.wait_ge(S["ws"], c + 1)
                if c:
                    dve.wait_ge(S["o_ps"], c)
                nc.vector.tensor_tensor(vnew[rows, :, :], uu[rows, HEADS * t:HEADS * t + HEADS, :],
                                        ps[rows, 0:2, :].rearrange("p b (h i) -> p (b h) i", h=4), ALU.add).then_inc(S["vnew"], 1)
                dve.wait_ge(S["state_read"], c + 1)
                dve_step(nc.vector.tensor_tensor(state, state, gl[:, c, :].unsqueeze(2).to_broadcast([P, HEADS, P]), ALU.mult))
                dve.wait_ge(S["kv"], c + 1)
                nc.vector.tensor_tensor(state, state, ps[:, 4:6, :].rearrange("p b (h i) -> p (b h) i", h=4), ALU.add).then_inc(S["state"], 1)
                dve.wait_ge(S["state"], c + 1)
            stage.end()
            moves.split(after_gdn)
            dve.wait_ge(S["o_sq"], 1)
            nc.vector.tensor_reduce(ssq[:, 0:SYS], egr, AX, ALU.add).then_inc(S["o_sums"], 1)
            dve.wait_ge(S["silu_zb"], 1)
            dve_step(nc.vector.tensor_tensor(oo, oo, zb[:, :, :].rearrange("p t (h i) -> p (t h) i", h=HEADS), ALU.mult))
            dve.wait_ge(S["o_root"], 1)
            dve_step(nc.vector.reciprocal(ssq[:, 0:SYS], rsd[:, 0:SYS]))
            nc.vector.tensor_tensor(oo, oo, ssq[:, 0:SYS].unsqueeze(2).to_broadcast([P, SYS, P]), ALU.mult).then_inc(S["o_gated"], 1)
            moves.split(after_gdn + 1)
            turn_low(dve, obt_r, obt_low_r, w_gdn, 4, heads=True).then_inc(S["obt_low"], 1)

        rs = slice(64, 96)
        posf, s_arg, c_arg = (arena(4)[rs, T * i:T * i + T] for i in range(3))
        kr = extra[rs, 2, 1536:1536 + T]
        turns, angle = (arena(5)[rs, T * i:T * i + T] for i in range(2))
        cq, ckv = extra[:, 0, 0:NT * QR].rearrange("p (t n) -> p t n", t=NT), extra[:, 0, 768:768 + NT * KVR].rearrange("p (t n) -> p t n", t=NT)
        cqn, ckvn = extra[:, 1, 0:NT * QR].rearrange("p (t n) -> p t n", t=NT), extra[:, 1, 768:768 + NT * KVR].rearrange("p (t n) -> p t n", t=NT)
        cqt, ckvt = extra[:, 2, 0:768].rearrange("p (k n) -> p k n", k=3), extra[:, 2, 768:1280].rearrange("p (k n) -> p k n", k=2)

        def stick(h, i):
            return arena(h)[:, 384 * i:384 * i + 384]

        def block2_pool(pool, stage):
            for _ in range(13, 18):
                stage.end()
            pool.dma_start(g_row, I["g_moe_2"][0].partition_broadcast(P)).then_inc(S["row_in"], 16)
            pool.dma_start(bdn, I["b_dn_2"][0]).then_inc(S["row_in"], 16)
            for i in range(3):
                pool.dma_start(extra[NEXP * i:NEXP * i + NEXP, 0, :], I["b_gu_2"][0]).then_inc(S["bias_in"], 16)
            for h in range(HEADS):
                pool.wait_ge(S["softplus"], h + 1)
                nc.gpsimd.tensor_tensor(stick(h, 2), stick(h, 1), con("strict"), ALU.mult).then_inc(S["masked_sp"], 1)
            stage.end()
            stage.end()
            stage.end()

        def block2_pe(pe, stage, prod):
            pe.wait_ge(S["normed"], 2)
            turn_pe(pe, oat_tm, KD)
            stage.end()
            prod.token_major(ht_parts2, QR)
            prod.chunk(prod.tm_units(KVR, lambda w, j: w[:, j, 0:KVR]) + prod.fm_units(1, 96, at=KVR - 64), ht_parts2)
            prod.feature_major(ht_parts2)
            prod.feature_major(ht_parts2)
            prod.token_major(ht_parts2)
            stage.end()
            pe.wait_ge(S["normed"], 3)
            turn_pe(pe, cqn, QR // P)
            pe.wait_ge(S["normed"], 4)
            turn_pe(pe, ckvn, KVR // P, 2)
            stage.end()
            prod.chunk(prod.fm_units(8, 96), cqt)
            prod.chunk(prod.fm_units(8, 64, step=P) +
                       prod.tm_units(BANK, lambda w, j: w[:, j, :].rearrange("p (h n) -> p h n", h=HEADS)[:, :, 64:P]), ckvt)
            stage.end()
            for m in range(4):
                pe.matmul(ps[rs, m, :], con("rot", rs), fm[rs, 8 + 2 * m:10 + 2 * m, :], start=True, stop=True).then_inc(S["rotated2"], 1)
            pe.matmul(ps[rs, 4, 0:T], con("rot", rs), kr, start=True, stop=True).then_inc(S["rotated2"], 1)
            pe.wait_ge(S["roped2"], 5)

            def out_mla(h, pt):
                v = [va[:, t, 512 + 64 * h:576 + 64 * h] for t in range(NT)]
                pe.matmul(ps[:, 4, 64 * h:64 * h + 64], pt[:, 0:P], v[0], start=True, stop=True)
                pe.matmul(ps[:, 5, 64 * h:64 * h + 64], pt[:, P:T], v[0], start=True, stop=False)
                return pe.matmul(ps[:, 5, 64 * h:64 * h + 64], pt[:, T:3 * P], v[1], start=False, stop=True)

            def stick_scores(h):
                r = slice(64 * (h % 2), 64 * (h % 2) + 64)
                q, k, b = fm[r, h // 2, :], fm[r, 4 + h // 2, :], ps[:, 6 + h % 2, :]
                if h >= 2:
                    pe.wait_ge(S["z_read"], h - 1)
                pe.matmul(b[:, 0:T], k[:, 0:P], q[:, 0:T], start=True, stop=True)
                pe.matmul(b[:, T:3 * P], k[:, P:T], q[:, P:T], start=True, stop=True).then_inc(S["stick_z"], 1)

            attention_pe(pe, HEADS, lambda h: fm[0:96, 8 + h, :], lambda h: fm[0:96, 16 + h, :], out_mla, stick_scores)
            stage.end()
            for h in range(HEADS):
                b, sp = ps[:, h, :], stick(h, 2)
                pe.wait_ge(S["masked_sp"], h + 1)
                pe.matmul(b[:, 0:T], con("later"), sp[:, 0:T], start=True, stop=False, skip_group_check=True)
                pe.matmul(b[:, P:T], con("ones"), sp[:, T:3 * P], start=False, stop=False, skip_group_check=True)
                pe.matmul(b[:, T:3 * P], con("later"), sp[:, T:3 * P], start=False, stop=True, skip_group_check=True).then_inc(S["after"], 1)
            pe.wait_ge(S["after_read"], 2)
            for h in range(HEADS):
                pe.wait_ge(S["stick_w"], h + 1)
                w = stick(h, 3)
                v = [va[:, t, 64 * h:64 * h + 64] for t in range(NT)]
                pe.matmul(ps[:, 0, 64 * h:64 * h + 64], w[:, 0:P], v[0], start=True, stop=True)
                pe.matmul(ps[:, 1, 64 * h:64 * h + 64], w[:, P:T], v[0], start=True, stop=False)
                pe.matmul(ps[:, 1, 64 * h:64 * h + 64], w[:, T:3 * P], v[1], start=False, stop=True).then_inc(S["stick_out"], 1)
            stage.end()
            pe.wait_ge(S["normed"], 5)
            turn_pe(pe, oat_tm, KD)
            stage.end()
            for c in range(2):
                prod.token_major(ht)
            stage.end()

        def block2_act(act, stage, moves):
            norm_act(act, xs, [(0, D)], extra[:, 0, :])
            turn_high(act, ht_r, g_attn)
            stage.end()
            moves.take(2, lambda i, b: copy_out(act, cq[:, i, :], ps[:, b, 0:QR]))
            moves.take(2, lambda i, b: copy_out(act, ckv[:, i, :], ps[:, b, 0:KVR]))
            moves.take(1, lambda i, b: copy_out(act, kr, ps[rs, b, 0:T]))
            moves.take(8, lambda i, b: copy_out(act, fm[:, i, :], ps[:, b, 0:T]))
            moves.take(2, lambda i, b: copy_out(act, va[:, i, 0:BANK], ps[:, b, :]))
            stage.end()
            norm_act(act, cq, [(0, QR)], arena(0))
            act.wait_ge(S["normed"], 3)
            norm_act(act, ckv, [(0, KVR)], arena(0))
            act.wait_ge(S["angles"], 1)
            nc.scalar.activation(s_arg, s_arg, ACT.Sin)
            nc.scalar.activation(c_arg, c_arg, ACT.Sin)
            stage.end()
            moves.take(8, lambda i, b: copy_out(act, fm[0:96, 8 + i, :], ps[0:96, b, 0:T]))
            moves.take(8, lambda i, b: copy_out(act, fm[0:64, 16 + i, :], ps[0:64, b, 0:T]))
            moves.take(2, lambda i, b: copy_out(act, va[:, i, BANK:D], ps[:, b, :]))
            stage.end()
            def stick_exp_abs(i):
                if 0 <= i < HEADS:
                    act.wait_ge(S["minus_abs"], i + 1)
                    nc.scalar.activation(stick(i, 1), stick(i, 1), ACT.Exp).then_inc(S["exp_abs"], 1)

            attention_act(act, HEADS, lambda i: stick_exp_abs(i - 2))
            stick_exp_abs(HEADS - 1)
            stage.end()
            for h in range(HEADS):
                act.wait_ge(S["exp_abs"], h + 1)
                nc.scalar.activation(stick(h, 1), stick(h, 1), ACT.Ln, bias=con("small")[:, 2:3]).then_inc(S["log1p"], 1)
            for h in range(HEADS):
                act.wait_ge(S["after_read"], h + 1)
                nc.scalar.activation(stick(h, 3), stick(h, 0), ACT.Exp).then_inc(S["stick_exp"], 1)
            stage.end()
            norm_act(act, zb, [(0, BANK), (BANK, BANK)], extra[:, 1, :])
            stage.end()
            moves.skip(4)
            stage.end()

        def block2_dve(dve, stage, moves):
            norm_dve(dve, xs, [(0, D)], oat_tm)
            turn_low(dve, ht_r, ht_low2_r, g_attn)
            stage.end()
            moves.take(2, lambda i, b: copy_out(dve, cq[:, i, :], ps[:, b, 0:QR]))
            moves.take(2, lambda i, b: copy_out(dve, ckv[:, i, :], ps[:, b, 0:KVR]))
            moves.take(1, lambda i, b: copy_out(dve, kr, ps[rs, b, 0:T]))
            moves.take(8, lambda i, b: copy_out(dve, fm[:, i, :], ps[:, b, 0:T]))
            moves.take(2, lambda i, b: copy_out(dve, va[:, i, 0:BANK], ps[:, b, :]))
            stage.end()
            norm_dve(dve, cq, [(0, QR)], cqn)
            norm_dve(dve, ckv, [(0, KVR)], ckvn)
            turn_dve(dve, cqt, QR // P, g_cq)
            turn_dve(dve, ckvt, KVR // P, g_ckv, 2)
            dve_step(nc.vector.tensor_copy(posf, posi[rs, :]))
            dve_step(nc.vector.tensor_scalar(angle, posf, con("freq", rs), None, ALU.mult))
            for arg, quarter in ((s_arg, 0.0), (c_arg, 0.25)):
                dve_step(nc.vector.tensor_scalar(turns, angle, 1.0 / TWO_PI, quarter, ALU.mult, ALU.add))
                dve_step(nc.vector.tensor_scalar(turns, turns, ROUND, None, ALU.add))
                dve_step(nc.vector.tensor_scalar(turns, turns, ROUND, None, ALU.subtract))
                dve_step(nc.vector.scalar_tensor_tensor(out=arg, in0=turns, scalar=-PI_A, in1=angle, op0=ALU.mult, op1=ALU.add))
                dve_step(nc.vector.scalar_tensor_tensor(out=arg, in0=turns, scalar=-PI_B, in1=arg, op0=ALU.mult, op1=ALU.add))
                dve_step(nc.vector.scalar_tensor_tensor(out=arg, in0=turns, scalar=-PI_C, in1=arg, op0=ALU.mult, op1=ALU.add))
                if quarter:
                    dve_step(nc.vector.tensor_scalar(arg, arg, np.pi / 2, None, ALU.add))
                last = nc.vector.tensor_scalar(arg, arg, PI_IN, -PI_IN, ALU.min, ALU.max)
            last.then_inc(S["angles"], 1)
            stage.end()
            moves.take(8, lambda i, b: copy_out(dve, fm[0:96, 8 + i, :], ps[0:96, b, 0:T]))
            moves.take(8, lambda i, b: copy_out(dve, fm[0:64, 16 + i, :], ps[0:64, b, 0:T]))
            moves.take(2, lambda i, b: copy_out(dve, va[:, i, BANK:D], ps[:, b, :]))
            stage.end()
            r1, r2 = (arena(5)[rs, 512 * i:512 * i + 512].rearrange("p (a b) -> p a b", a=2) for i in range(2))
            sin2, cos2 = (a.unsqueeze(1).to_broadcast([32, 2, T]) for a in (s_arg, c_arg))
            for m in range(4):
                q2 = fm[rs, 8 + 2 * m:10 + 2 * m, :]
                dve.wait_ge(S["rotated2"], m + 1)
                nc.vector.tensor_tensor(r1, ps[rs, m, :].rearrange("p (a b) -> p a b", a=2), sin2, ALU.mult)
                dve_step(nc.vector.tensor_tensor(r2, q2, cos2, ALU.mult))
                nc.vector.tensor_tensor(q2, r1, r2, ALU.add).then_inc(S["roped2"], 1)
                dve.wait_ge(S["roped2"], m + 1)
            dve.wait_ge(S["rotated2"], 5)
            nc.vector.tensor_tensor(r1[:, 0, :], ps[rs, 4, 0:T], s_arg, ALU.mult)
            dve_step(nc.vector.tensor_tensor(r2[:, 0, :], kr, c_arg, ALU.mult))
            nc.vector.tensor_tensor(fm[rs, 16:24, :], r1[:, 0, :].unsqueeze(1).to_broadcast([32, HEADS, T]),
                                    r2[:, 0, :].unsqueeze(1).to_broadcast([32, HEADS, T]), ALU.add).then_inc(S["roped2"], 1)
            def stick_minus_abs(h):
                if 0 <= h < HEADS:
                    dve.wait_ge(S["stick_z"], h + 1)
                    nc.vector.tensor_scalar(stick(h, 0), ps[:, 6 + h % 2, 0:3 * P], 0.125, None, ALU.mult).then_inc(S["z_read"], 1)
                    dve.wait_ge(S["z_read"], h + 1)
                    nc.vector.scalar_tensor_tensor(out=stick(h, 1), in0=stick(h, 0), scalar=-1.0, in1=stick(h, 0), op0=ALU.mult, op1=ALU.min).then_inc(S["minus_abs"], 1)

            attention_dve(dve, HEADS, 96.0 ** -0.5, lambda h: None, lambda i: stick_minus_abs(i - 1))
            dve.wait_ge(S["head_out"], 2 * HEADS)
            for t in range(NT):
                nc.vector.tensor_copy(zb[:, t, 0:BANK], ps[:, 4 + t, :])
            stage.end()
            for i in range(HEADS + 2):
                if i < HEADS:
                    dve.wait_ge(S["log1p"], i + 1)
                    nc.vector.scalar_tensor_tensor(out=stick(i, 1), in0=stick(i, 0), scalar=0.0, in1=stick(i, 1), op0=ALU.max, op1=ALU.add).then_inc(S["softplus"], 1)
                    dve.wait_ge(S["softplus"], i + 1)
                    dve_step(nc.vector.tensor_tensor(stick(i, 0), stick(i, 0), stick(i, 1), ALU.subtract))
                if i >= 2:
                    h = i - 2
                    dve.wait_ge(S["after"], h + 1)
                    nc.vector.tensor_tensor(stick(h, 0), stick(h, 0), ps[:, h, 0:3 * P], ALU.subtract).then_inc(S["after_read"], 1)
            for h in range(HEADS):
                dve.wait_ge(S["stick_exp"], h + 1)
                nc.vector.tensor_tensor(stick(h, 3), stick(h, 3), con("strict"), ALU.mult).then_inc(S["stick_w"], 1)
            dve.wait_ge(S["stick_out"], HEADS)
            for t in range(NT):
                nc.vector.tensor_copy(zb[:, t, BANK:D], ps[:, t, :])
            stage.end()
            norm_dve(dve, zb, [(0, BANK), (BANK, BANK)], oat_tm)
            turn_dve(dve, ht, KD, g_mix)
            stage.end()
            dve.wait_ge(S["bias_in"], 48)
            dve_step(nc.vector.tensor_copy(bgp[:, :], bgu))
            for g in (1, 2):
                dve_step(nc.vector.tensor_tensor(bgu_rest, (bgu, bgu_rest)[g - 1], bgp[:, :], ALU.subtract))
                for q in range(g, 3):
                    last = nc.vector.tensor_copy(bgp[NEXP * q:NEXP * q + NEXP, :], bgu_rest[NEXP * q:NEXP * q + NEXP, :])
                dve_step(last)
            moves.take(4, lambda i, b: nc.vector.tensor_tensor(xs[:, i % 2, BANK * (i // 2):BANK * (i // 2) + BANK], ps[:, b, :],
                                                               xs[:, i % 2, BANK * (i // 2):BANK * (i // 2) + BANK], ALU.add), whole=True)
            stage.end()

        NLIST = NEXP + MAXOVER + 1
        ub = fm[:, :, :].rearrange("p a b -> p (a b)").bitcast(BF16)[:, 0:3 * NT * D].rearrange("p (s t d) -> p s t d", s=3, t=NT)
        u_tok, rest = va, zb
        g_row = extra[:, 2, 0:D]
        bdn = extra[0:NEXP, 2, D:2 * D]
        bgu, bgu_rest = extra[0:3 * NEXP, 0, :], extra[0:3 * NEXP, 1, :]
        bgp = sb("bgp", [3 * NEXP, 2048], BF16)
        wr = sb("wr", [P, KD, NEXP])
        lg, gate, pick, posx = (sb(n, [P, NT, NEXP]) for n in ("lg", "gate", "pick", "posx"))
        mx8 = sb("mx8", [P, NT, 8])
        ix8 = sb("ix8", [P, NT, 8], U32)
        ixf = sb("ixf", [P, NT, 8])
        gsm = sb("gsm", [P, NT])
        over = sb("over", [NEXP, 8])
        hot = extra[0:NEXP, 1, 0:3 * MAXOVER].rearrange("p (r k) -> p r k", r=3)
        wlist = sb("wlist", [1, 2, NLIST], I32)
        wcount = sb("wcount", [1, 1], I32)
        tmp4 = zb[:, 1, 0:512].rearrange("p (a j e) -> p a j e", a=4, j=4)
        gate_t = zb[0:NEXP, 1, 512:512 + T]
        xst = zb[:, 0, 0:KD * CAP].rearrange("p (k s) -> p k s", k=KD)
        glu, lin, sig, act_b = extra[:, 0, 0:512], extra[:, 0, 512:1024], extra[:, 0, 1024:1536], extra[:, 0, 1536:2048]
        act_t = extra[:, 1, 0:512].rearrange("p (j m) -> p j m", j=4)
        pgt = extra[:, 1, 512:512 + T]
        y_sb = extra[:, 1, 1024:1536]
        pg = extra[:, 1, 1536:1536 + NT * 2 * CAP].rearrange("p (t a s) -> p t a s", t=NT, a=2)
        pick_s = sb("pick_s", [P, NT, CAP], BF16)
        bsel = sb("bsel", [3 * NEXP, CAP], BF16)
        w_gu, w_dn = I["w_gu_2"][0], I["w_dn_2"][0]

        def expert_chunk(e, c):
            if c < 4:
                src = w_gu[e].rearrange("(p k) n -> p k n", k=KD)[:, 2 * c:2 * c + 2, :]
                return ring[:, c, :].rearrange("p (k n) -> p k n", k=2), src
            src = w_dn[e].rearrange("(a p j) n -> a p j n", a=2, j=4)[c - 4]
            return ring[:, c, :].rearrange("p (j n) -> p j n", j=4), src

        class LoopSteps:

            def __init__(self, eng, sem, it, per):
                self.eng, self.sem, self.it, self.per, self.n = eng, sem, it, per, 0

            def __call__(self, ins):
                self.n += 1
                ins.then_inc(self.sem, 1)
                self.eng.wait_ge(self.sem, self.it * self.per + self.n)

            def close(self):
                assert self.n == self.per, self.n

        def item_count(eng):
            return eng.value_load(wcount[0:1, 0:1], min_val=NEXP, max_val=NEXP + MAXOVER)

        def moe_pool(pool, stage):
            stage.end()
            stage.end()
            pool.dma_start(p_tok, I["p_2"][0, 0].rearrange("(t p) n -> p t n", p=P)).then_inc(S["p_in"], 16)
            stage.end()

        def moe_pe(pe, stage):
            pe.wait_ge(S["normed"], 6)
            turn_pe(pe, oat_tm, KD)
            pe.wait_ge(S["u_t"], 1)
            for t in range(NT):
                for j in range(KD):
                    last = pe.matmul(ps[:, 4, NEXP * t:NEXP * t + NEXP], ht[:, j, P * t:P * t + P], wr[:, j, :], start=(j == 0), stop=(j == KD - 1))
            last.then_inc(S["logits"], 1)
            stage.end()
            pe.wait_ge(S["picked"], 1)
            pe.matmul(ps[:, 0, 0:NEXP], con("earlier"), pick[:, 0, :], start=True, stop=True)
            pe.matmul(ps[:, 0, NEXP:2 * NEXP], con("earlier"), pick[:, 1, :], start=True, stop=False)
            pe.matmul(ps[:, 0, NEXP:2 * NEXP], con("ones"), pick[:, 0, :], start=False, stop=True).then_inc(S["positions"], 1)
            for t in range(NT):
                last = pe.matmul(ps[0:NEXP, 1, 0:1], pick[:, t, :], con("ones")[:, 0:1], start=(t == 0), stop=(t == NT - 1))
            last.then_inc(S["counts"], 1)
            pe.wait_ge(S["gated"], 1)
            for t in range(NT):
                last = pe.transpose(ps[0:NEXP, 5, P * t:P * t + P], gate[:, t, :], ident)
            last.then_inc(S["gate_turned"], 1)
            pe.wait_ge(S["overs"], 1)
            pe.matmul(ps[0:NEXP, 2, 0:3], con("earlier", slice(0, NEXP))[:, 0:NEXP], over[:, 0:3], start=True, stop=True).then_inc(S["before"], 1)
            pe.wait_ge(S["hots"], 1)
            for a in range(2):
                for r in range(3):
                    lhs = con("row", slice(0, NEXP)) if a == 0 else con("small", slice(0, NEXP))[:, 3 + r:4 + r]
                    pe.matmul(ps[0:1, 3, MAXOVER * a:MAXOVER * a + MAXOVER], lhs, hot[:, r, :], start=(r == 0), stop=(r == 2))
            for r in range(3):
                last = pe.matmul(ps[0:1, 3, 2 * MAXOVER:2 * MAXOVER + 1], over[:, r:r + 1], con("ones", slice(0, NEXP))[:, 0:1], start=(r == 0), stop=(r == 2))
            last.then_inc(S["listed"], 1)
            stage.end()
            for t in range(NT):
                for n in range(2):
                    last = pe.matmul(ps[:, 2 * t + n, :], gate_t[:, P * t:P * t + P], bdn[:, BANK * n:BANK * n + BANK], start=True, stop=False, skip_group_check=True)
            last.then_inc(S["w_used"], AHEAD)
            total = item_count(pe)

            def gather():
                for k in range(KD):
                    for i in range(3 * NT):
                        last = pe.matmul(ps[:, 7, CAP * k:CAP * k + CAP], ub[:, i // NT, i % NT, k:k + KD * (P - 1) + 1:KD], pick_s[:, i % NT, :],
                                         start=(i == 0), stop=(i == 3 * NT - 1))
                last.then_inc(S["gathered"], 1)

            def spread(wait):
                wait()
                for t in range(NT):
                    for n in range(2):
                        r = slice(64 * n, 64 * n + CAP)
                        last = pe.matmul(ps[:, 2 * t + n, :], pgt[r, P * t:P * t + P], y_sb[r, :], start=False, stop=False, skip_group_check=True)
                last.then_inc(S["spread"], 1)

            pe.wait_ge(S["pick_s"], 1)
            gather()
            with pe.Fori(0, total) as it:
                pe.wait_ge(S["xst"], it + 1)
                pe.wait_ge(S["bsel"], it + 1)
                for n in range(4):
                    pe.matmul(ps[64 * (n % 2):64 * (n % 2) + CAP, 4 + n // 2, :], bsel[:, :], bgp[:, BANK * n:BANK * n + BANK], start=True, stop=False, skip_group_check=True)
                for c in range(4):
                    pe.wait_ge(S[f"expert_in{c}"], it * 16 + 16)
                    for k in (2 * c, 2 * c + 1):
                        for n in range(4):
                            last = pe.matmul(ps[64 * (n % 2):64 * (n % 2) + CAP, 4 + n // 2, :], xst[:, k, :],
                                             ring[:, c, 2048 * (k % 2) + BANK * n:2048 * (k % 2) + BANK * n + BANK], start=False, stop=(k == KD - 1), skip_group_check=True)
                    last.then_inc(S["w_used"], 1)
                    if c == 1:
                        spread(lambda: pe.wait_ge(S["y_sb"], it + 1))
                    if c == 2:
                        pe.wait_ge(S["pg"], it + 1)
                        for t in range(NT):
                            last = pe.transpose(ps[:, 6, P * t:P * t + P], pg[:, t, :, :].rearrange("p a s -> p (a s)"), ident)
                        last.then_inc(S["pg_turned"], 1)
                pe.wait_ge(S["pick_s"], it + 2)
                gather()
                pe.wait_ge(S["act"], it + 1)
                for j in range(4):
                    last = pe.transpose(ps[:, 4, P * j:P * j + P], act_b[:, j:j + 4 * (P - 1) + 1:4], ident)
                last.then_inc(S["act_turned"], 1)
                pe.wait_ge(S["act_t"], it + 1)
                pe.wait_ge(S["pgt"], it + 1)
                for c in range(2):
                    pe.wait_ge(S[f"expert_in{4 + c}"], it * 16 + 16)
                    for j in range(4):
                        for n in range(2):
                            last = pe.matmul(ps[64 * n:64 * n + CAP, 6, :], act_t[:, j, 64 * c:64 * c + CAP],
                                             ring[:, 4 + c, D * j + BANK * n:D * j + BANK * n + BANK], start=(c == 0 and j == 0), stop=(c == 1 and j == 3), skip_group_check=True)
                    last.then_inc(S["w_used"], 1)
            spread(lambda: (pe.wait_ge(S["y_sb"], total + 1), pe.wait_ge(S["pgt"], total)))
            stage.end()

        def moe_act(act, stage, moves):
            norm_act(act, xs, [(0, D)], zb[:, 0, :])
            act.wait_ge(S["u_tok"], 1)
            nc.scalar.activation(ub[:, 0], u_tok[:, :, :], ACT.Copy).then_inc(S["part"], 1)
            act.wait_ge(S["rest"], 1)
            nc.scalar.activation(ub[:, 1], rest[:, :, :], ACT.Copy).then_inc(S["part"], 1)
            act.wait_ge(S["rest"], 2)
            nc.scalar.activation(ub[:, 2], rest[:, :, :], ACT.Copy)
            stage.end()
            act.wait_ge(S["less_max"], 1)
            nc.scalar.activation(mx8[:, :, 0:4], mx8[:, :, 0:4], ACT.Exp).then_inc(S["gate_exp"], 1)
            act.wait_ge(S["gate_turned"], 1)
            nc.scalar.activation(gate_t, ps[0:NEXP, 5, 0:T], ACT.Copy)
            nc.scalar.activation(y_sb, con("causal")[:, 0:1].to_broadcast([P, 512]), ACT.Copy, scale=0.0).then_inc(S["y_sb"], 1)
            nc.scalar.activation(pgt, con("causal")[:, 0:1].to_broadcast([P, T]), ACT.Copy, scale=0.0)
            stage.end()
            total = item_count(act)
            act.wait_ge(S["gathered"], 1)
            nc.scalar.activation(xst, ps[:, 7, 0:KD * CAP].rearrange("p (k s) -> p k s", k=KD), ACT.Copy).then_inc(S["xst"], 1)
            with act.Fori(0, total) as it:
                act.wait_ge(S["pg_turned"], it + 1)
                nc.scalar.activation(pgt, ps[:, 6, 0:T], ACT.Copy).then_inc(S["pgt"], 1)
                act.wait_ge(S["glu"], it + 1)
                nc.scalar.activation(sig, glu, ACT.Sigmoid, scale=1.702).then_inc(S["sig"], 1)
                act.wait_ge(S["gathered"], it + 2)
                nc.scalar.activation(xst, ps[:, 7, 0:KD * CAP].rearrange("p (k s) -> p k s", k=KD), ACT.Copy).then_inc(S["xst"], 1)
                act.wait_ge(S["w_used"], it * 6 + 6 + AHEAD)
                nc.scalar.activation(y_sb, ps[:, 6, :], ACT.Copy).then_inc(S["y_sb"], 1)
            moves.split(before_experts + 1)
            stage.end()

        def moe_dve(dve, stage, moves):
            norm_dve(dve, xs, [(0, D)], oat_tm)
            dve.wait_ge(S["row_in"], 16 * 3)
            dve.wait_ge(S["normed"], 6)
            for t in range(NT):
                last = nc.vector.tensor_tensor(u_tok[:, t, :], oat_tm[:, t, :], g_row, ALU.mult)
            last.then_inc(S["u_tok"], 1)
            turn_dve(dve, ht, KD, g_moe, done="u_t")
            dve.wait_ge(S["part"], 1)
            nc.vector.tensor_tensor(rest[:, :, :], u_tok[:, :, :], ub[:, 0], ALU.subtract).then_inc(S["rest"], 1)
            dve.wait_ge(S["rest"], 1)
            dve.wait_ge(S["part"], 2)
            nc.vector.tensor_tensor(rest[:, :, :], rest[:, :, :], ub[:, 1], ALU.subtract).then_inc(S["rest"], 1)
            dve.wait_ge(S["logits"], 1)
            dve_step(nc.vector.tensor_tensor(lg[:, :, :], ps[:, 4, 0:2 * NEXP].rearrange("p (t e) -> p t e", t=NT), brow[:, :].unsqueeze(1).to_broadcast([P, NT, NEXP]), ALU.add))
            stage.end()
            for t in range(NT):
                dve_step(nc.vector.max(mx8[:, t, :], lg[:, t, :]))
                dve_step(nc.vector.max_index(ix8[:, t, :], mx8[:, t, :], lg[:, t, :]))
            dve_step(nc.vector.tensor_copy(ixf[:, :, :], ix8[:, :, :]))
            dve_step(nc.vector.tensor_copy(gsm[:, :], mx8[:, :, 0]))
            for t in range(NT):
                last = nc.vector.tensor_scalar(mx8[:, t, 0:4], mx8[:, t, 0:4], gsm[:, t:t + 1], None, ALU.subtract)
            last.then_inc(S["less_max"], 1)
            number = con("slots")[:, 0:NEXP]
            for t in range(NT):
                for j in range(4):
                    last = nc.vector.tensor_scalar(tmp4[:, t, j, :], number, ixf[:, t, j:j + 1], None, ALU.is_equal)
            dve_step(last)
            for t in range(NT):
                last = nc.vector.tensor_reduce(pick[:, t, :], tmp4[:, t].rearrange("p j e -> p e j"), AX, ALU.add)
            last.then_inc(S["picked"], 1)
            dve.wait_ge(S["gate_exp"], 1)
            dve_step(nc.vector.tensor_reduce(gsm[:, :], mx8[:, :, 0:4], AX, ALU.add))
            dve_step(nc.vector.reciprocal(gsm[:, :], gsm[:, :]))
            for t in range(NT):
                last = nc.vector.tensor_scalar(mx8[:, t, 0:4], mx8[:, t, 0:4], gsm[:, t:t + 1], None, ALU.mult)
            dve_step(last)
            for t in range(NT):
                for j in range(4):
                    last = nc.vector.tensor_scalar(tmp4[:, 2 + t, j, :], number, ixf[:, t, j:j + 1], mx8[:, t, j:j + 1], ALU.is_equal, ALU.mult)
            dve_step(last)
            for t in range(NT):
                last = nc.vector.tensor_reduce(gate[:, t, :], tmp4[:, 2 + t].rearrange("p j e -> p e j"), AX, ALU.add)
            last.then_inc(S["gated"], 1)
            dve.wait_ge(S["picked"], 1)
            dve_step(nc.vector.tensor_scalar(posx[:, :, :], pick[:, :, :], -4096.0, 4096.0, ALU.mult, ALU.add))
            dve.wait_ge(S["positions"], 1)
            dve_step(nc.vector.tensor_tensor(posx[:, :, :], posx[:, :, :], ps[:, 0, 0:2 * NEXP].rearrange("p (t e) -> p t e", t=NT), ALU.add))
            dve.wait_ge(S["counts"], 1)
            dve_step(nc.vector.tensor_copy(over[:, 7:8], ps[0:NEXP, 1, 0:1]))
            nc.vector.tensor_scalar(over[:, 0:3], con("small", slice(0, NEXP))[:, 3:6], over[:, 7:8], None, ALU.is_lt).then_inc(S["overs"], 1)
            dve.wait_ge(S["before"], 1)
            dve_step(nc.vector.tensor_reduce(over[:, 6:7], ps[0:NEXP, 2, 0:3], AX, ALU.add))
            dve_step(nc.vector.tensor_scalar(over[:, 3:6], con("slots", slice(0, NEXP))[:, 0:3], over[:, 6:7], None, ALU.add))
            for r in range(3):
                last = nc.vector.tensor_scalar(hot[:, r, :], con("slots", slice(0, NEXP))[:, 0:MAXOVER], over[:, 3 + r:4 + r], over[:, r:r + 1], ALU.is_equal, ALU.mult)
            last.then_inc(S["hots"], 1)
            dve_step(nc.vector.memset(wlist[:, :, :], 0))
            nc.vector.tensor_copy(wlist[:, 0, 0:NEXP], con("slots", slice(0, 1))[:, 0:NEXP])
            dve.wait_ge(S["listed"], 1)
            nc.vector.tensor_copy(wlist[:, :, NEXP:NEXP + MAXOVER], ps[0:1, 3, 0:2 * MAXOVER].rearrange("p (a k) -> p a k", a=2))
            nc.vector.tensor_scalar(wcount[:, :], ps[0:1, 3, 2 * MAXOVER:2 * MAXOVER + 1], float(NEXP), None, ALU.add).then_inc(S["items"], 1)
            stage.end()
            total = item_count(dve)

            def item(i):
                return (dve.value_load(wlist[0:1, 0, bass.ds(i, 1)], min_val=0, max_val=NEXP - 1),
                        dve.value_load(wlist[0:1, 1, bass.ds(i, 1)], min_val=0, max_val=T))

            def pick_tokens(e, base):
                for t in range(NT):
                    last = nc.vector.tensor_scalar(pick_s[:, t, :], con_at("slots", base, CAP), posx[:, t, bass.ds(e, 1)], None, ALU.is_equal)
                last.then_inc(S["pick_s"], 1)

            def pick_bias(e):
                nc.vector.tensor_copy(bsel[:, :], con("bsel", slice(0, 3 * NEXP))[:, bass.ds(e, 1)].to_broadcast([3 * NEXP, CAP])).then_inc(S["bsel"], 1)

            pick_tokens(0, 0)
            pick_bias(0)
            with dve.Fori(0, total) as it:
                e, base = item(it)
                e1, base1 = item(it + 1)
                step = LoopSteps(dve, S["moe_step"], it, 2)
                dve.wait_ge(S["pick_s"], it + 1)
                for t in range(NT):
                    last = nc.vector.tensor_scalar(pg[:, t, :, :], pick_s[:, t, :].unsqueeze(1).to_broadcast([P, 2, CAP]), gate[:, t, bass.ds(e, 1)], None, ALU.mult)
                last.then_inc(S["pg"], 1)
                dve.wait_ge(S["gathered"], it + 1)
                dve.wait_ge(S["pg"], it + 1)
                pick_tokens(e1, base1)
                dve.wait_ge(S["w_used"], it * 6 + 4 + AHEAD)
                nc.vector.tensor_scalar(glu, ps[:, 4, :], 7.0, None, ALU.min).then_inc(S["glu"], 1)
                step(nc.vector.tensor_scalar(lin, ps[:, 5, :], 7.0, -7.0, ALU.min, ALU.max))
                pick_bias(e1)
                step(nc.vector.scalar_tensor_tensor(out=lin, in0=lin, scalar=1.0, in1=glu, op0=ALU.add, op1=ALU.mult))
                dve.wait_ge(S["sig"], it + 1)
                nc.vector.tensor_tensor(act_b, lin, sig, ALU.mult).then_inc(S["act"], 1)
                dve.wait_ge(S["act_turned"], it + 1)
                nc.vector.tensor_copy(act_t, ps[:, 4, :].rearrange("p (j m) -> p j m", j=4)).then_inc(S["act_t"], 1)
                step.close()
            moves.split(before_experts + 1)
            stage.end()

        p_tok = va[:, 0, 0:NT * 256].rearrange("p (t n) -> p t n", t=NT)
        p_t = zb[:, 1, 0:2 * T].rearrange("p (k n) -> p k n", k=2)
        ple_gate = gates[:, 0]

        def tail_pool(pool, stage):
            pool.dma_start(g_row, I["g_final_2"].partition_broadcast(P)).then_inc(S["row_in"], 16)
            stage.end()
            stage.end()
            stage.end()

        def tail_pe(pe, stage, prod):
            pe.wait_ge(S["p_in"], 16)
            turn_pe(pe, p_tok, 2, 4)
            pe.wait_ge(S["p_t"], 1)
            prod.chunk(prod.tm_units(BANK, lambda w, j: w[:, j, 0:BANK]) + prod.tm_units(BANK, lambda w, j: w[:, j, BANK:D]), p_t)
            pe.wait_ge(S["normed"], 7)
            turn_pe(pe, oat_tm, KD)
            stage.end()
            for c in range(2):
                prod.token_major((ht_r, fm_r[:, 16:24, :]))
            stage.end()
            stage.end()

        def tail_act(act, stage, moves):
            act.wait_ge(S["summed"], NT)
            norm_act(act, xs, [(0, D)], zb[:, 0, :])
            turn_high(act, ht_r, g_ple, before=2 + 1 + 4 + 4 + 1)
            moves.split(before_experts + 2)
            stage.end()
            for i in range(4):
                act.wait_ge(S["unit"], plan[-2].first + i + 1)
                nc.scalar.activation(ple_gate[:, i % 2, BANK * (i // 2):BANK * (i // 2) + BANK], ps[:, i, :], ACT.Sigmoid).then_inc(S["ple_gate"], 1)
            stage.end()
            norm_act(act, xs, [(0, D)], zb[:, 0, :])
            stage.end()

        def tail_dve(dve, stage, moves):
            for t in range(NT):
                nc.vector.tensor_tensor(xs[:, t, :], xs[:, t, :], ps[:, 2 * t:2 * t + 2, :].rearrange("p b n -> p (b n)"), ALU.add).then_inc(S["summed"], 1)
            turn_dve(dve, p_t, 2, None, 4, done="p_t")
            norm_dve(dve, xs, [(0, D)], oat_tm)
            turn_low(dve, ht_r, fm_r[:, 16:24, :], g_ple)
            moves.split(before_experts + 2)
            stage.end()
            for i in range(4):
                t, cols = i % 2, slice(BANK * (i // 2), BANK * (i // 2) + BANK)
                dve.wait_ge(S["ple_gate"], i + 1)
                dve_step(nc.vector.tensor_tensor(oat_tm[:, t, cols], ps[:, 4 + i, :], ple_gate[:, t, cols], ALU.mult))
                nc.vector.tensor_tensor(xs[:, t, cols], xs[:, t, cols], oat_tm[:, t, cols], ALU.add)
            stage.end()
            norm_dve(dve, xs, [(0, D)], None)
            dve.wait_ge(S["row_in"], 16 * 4)
            for t in range(NT):
                nc.vector.scalar_tensor_tensor(out=xs[:, t, :], in0=xs[:, t, :], scalar=ssq[:, t:t + 1], in1=g_row, op0=ALU.mult, op1=ALU.mult)
            stage.end()

        @block.sync
        def _(sp):
            def load_chunk(g):
                c = plan[g]
                if c.free:
                    sp.wait_ge(S["unit"], c.free)
                if c.slot == 2 and after_gdn <= g < after_gdn + 3:
                    sp.wait_ge(S["stage"], 4 * 8)
                    sp.wait_ge(S["o_sums"], 1)
                sp.dma_start(c.dst, c.src).then_inc(S[f"chunk_in{c.slot}"], 16)

            sp.dma_start(xs[:, :, :], I["x"][0].rearrange("(t p) d -> p t d", p=P)).then_inc(S["x_in"], 16)
            sp.dma_start(cst[:, :], I["const"]).then_inc(S["const_in"], 16)
            for g in range(before_experts):
                load_chunk(g)
            sp.wait_ge(S["stage"], 4 * 18)
            for c in range(2, 6):
                sp.dma_start(*expert_chunk(0, c)).then_inc(S[f"expert_in{c}"], 16)
            sp.wait_ge(S["unit"], plan[before_experts - 1].done)
            for c in range(2):
                sp.dma_start(*expert_chunk(0, c)).then_inc(S[f"expert_in{c}"], 16)
            sp.wait_ge(S["stage"], 4 * 22)
            total = item_count(sp)
            with sp.Fori(1, total) as it:
                e = sp.value_load(wlist[0:1, 0, bass.ds(it, 1)], min_val=0, max_val=NEXP - 1)
                for c in range(6):
                    sp.wait_ge(S["w_used"], it * 6 + (c - 5 + AHEAD))
                    sp.dma_start(*expert_chunk(e, c)).then_inc(S[f"expert_in{c}"], 16)
            for g in (before_experts + 1, before_experts + 2, before_experts):
                sp.wait_ge(S["w_used"], total * 6 + (plan[g].slot - 5 + AHEAD))
                load_chunk(g)
            sp.wait_ge(S["stage"], 4 * LAST_STAGE)
            sp.dma_start(out[0].rearrange("(t p) d -> p t d", p=P), xs[:, :, :]).then_inc(S["stored"], 16)
            sp.wait_ge(S["stored"], 16)

        @block.gpsimd
        def _(pool):
            stage = Stage(pool, S["stage"])
            pool.dma_start(w_pre, I["pre_norm_w"][0].rearrange("(p k) -> p k", k=KD)).then_inc(S["w_pre_in"], 16)
            pool.dma_start(w_gdn, I["gdn_norm_w"][0].rearrange("(p k) -> p k", k=1)).then_inc(S["small_in"], 16)
            pool.dma_start(wbd[:, :, :], w_in[:, :, 16 * BANK:16 * BANK + 16]).then_inc(S["small_in"], 16)
            pool.dma_start(extra[0:96, 2, 0:P], I["conv_w"][0].rearrange("j (c p) -> (j c) p", p=P)).then_inc(S["small_in"], 16)
            pool.dma_start(hsc[:, 0:8], I["dt_bias"][0].partition_broadcast(P)).then_inc(S["small_in"], 16)
            pool.dma_start(hsc[:, 8:16], I["a_log"][0].partition_broadcast(P)).then_inc(S["small_in"], 16)
            pool.dma_start(g_attn, I["g_attn_2"][0].rearrange("(p k) -> p k", k=KD)).then_inc(S["small_in"], 16)
            pool.dma_start(g_cq, I["g_cq_2"][0].rearrange("(p k) -> p k", k=QR // P)).then_inc(S["small_in"], 16)
            pool.dma_start(g_ckv, I["g_ckv_2"][0].rearrange("(p k) -> p k", k=KVR // P)).then_inc(S["small_in"], 16)
            pool.dma_start(g_mix[0:64, :], I["g_out_mla_2"][0].rearrange("(p k) -> p k", k=KD)).then_inc(S["small_in"], 16)
            pool.dma_start(g_mix[64:P, :], I["g_out_sb_2"][0].rearrange("(p k) -> p k", k=KD)).then_inc(S["small_in"], 16)
            pool.dma_start(g_moe, I["g_moe_2"][0].rearrange("(p k) -> p k", k=KD)).then_inc(S["small_in"], 16)
            pool.dma_start(g_ple, I["g_ple_2"][0].rearrange("(p k) -> p k", k=KD)).then_inc(S["small_in"], 16)
            pool.dma_start(posi[64:96, :], I["positions_2"][0].partition_broadcast(32)).then_inc(S["small_in"], 16)
            pool.dma_start(wr[:, :, :], pk_rows("w_router_2", KD)).then_inc(S["small_in"], 16)
            pool.dma_start(brow[:, :], I["b_router_2"][0].partition_broadcast(P)).then_inc(S["small_in"], 16)
            pool.wait_ge(S["const_in"], 16)
            stage.end()
            pool.wait_ge(S["small_in"], SMALL_LOADS * 16)
            stage.end()
            for m in ROPE_POOL:
                nc.gpsimd.tensor_tensor(rope_scratch(m)[1], fm[0:32, 2 * m:2 * m + 2, :], cosb, ALU.mult).then_inc(S["cos_part"], 1)
            moves = Moves(pool, 1)
            for g in (in_attention + 1, in_attention + 2):
                moves.split(g)
            stage.end()
            nc.gpsimd.tensor_copy(zb[:, :, 0:BANK], extra[:, 1, :].rearrange("p (t n) -> p t n", t=NT)[:, :, 0:BANK]).then_inc(S["zb_moved"], 1)
            stage.end()
            gdn_pool(pool, stage)
            stage.end()
            stage.end()
            pool.dma_start(extra[:, 2, 0:D], I["post_norm_w"][0].partition_broadcast(P)).then_inc(S["row_in"], 16)
            stage.end()
            stage.end()
            block2_pool(pool, stage)
            moe_pool(pool, stage)
            tail_pool(pool, stage)

        @block.tensor
        def _(pe):
            stage = Stage(pe, S["stage"])
            prod = Products(pe)
            pe.wait_ge(S["const_in"], 16)
            pe.wait_ge(S["normed"], 1)
            turn_pe(pe, oat_tm, KD)
            stage.end()
            for c in range(6):
                prod.feature_major(ht_parts)
            for c in range(2):
                prod.token_major(ht_parts)
            stage.end()
            for m in range(8):
                pe.matmul(ps[0:32, m, :], con("rot", slice(0, 32)), fm[0:32, 2 * m:2 * m + 2, :], start=True, stop=True).then_inc(S["rotated"], 1)
            pe.wait_ge(S["roped"], 8)

            def out_a(h, pt):
                b = ps[:, 4 + h % 2, :]
                if h >= 2:
                    pe.wait_ge(S["head_taken"], h - 1)
                pe.matmul(b[:, 0:T], zb[:, 0, P * h:P * h + P], pt[:, 0:T], start=True, stop=False, skip_group_check=True)
                return pe.matmul(b[:, P:T], zb[:, 1, P * h:P * h + P], pt[:, T:3 * P], start=False, stop=True, skip_group_check=True)

            attention_pe(pe, 0, lambda h: fm[:, h, :], lambda h: fm[:, 8 + h, :], out_a,
                         lambda i: prod.slice(ht_parts, i, HEADS, 6))
            pe.wait_ge(S["weights_t"], HEADS)
            pe.transpose(ps[:, 3, 0:96], extra[0:96, 2, 0:P], ident[0:96, 0:96]).then_inc(S["conv_turned"], 1)
            stage.end()
            for c in range(6):
                prod.feature_major(ht_parts)
            prod.token_major(ht_parts)
            pe.wait_ge(S["moved1"], prod.u // 2)
            for t in range(NT):
                for j in range(KD):
                    pe.matmul(ps[:, 7, 16 * t:16 * t + 16], ht_r[:, j, P * t:P * t + P].bitcast(F32), wbd[:, j, :], start=(j == 0), stop=False)
                    last = pe.matmul(ps[:, 7, 16 * t:16 * t + 16], ht_low_r[:, j, P * t:P * t + P].bitcast(F32), wbd[:, j, :], start=False, stop=(j == KD - 1))
            last.then_inc(S["bd_logits"], 1)
            stage.end()
            gdn_pe(pe, stage)
            assert prod.u % 8 == 0
            prod.token_major(ht_parts)
            pe.wait_ge(S["o_gated"], 1)
            for s in range(SYS):
                h, t = s // NT, s % NT
                last = pe.transpose(ps[:, 4 + h // 2, T * (h % 2) + P * t:T * (h % 2) + P * t + P], oo[:, HEADS * t + h, :], ident)
                if h % 2 and t == NT - 1:
                    last.then_inc(S["turned"], 1)
            turned["pe"] += HEADS // 2
            prod.token_major(ht_parts)
            pe.wait_ge(S["obt_low"], 1)
            for c in range(2):
                prod.token_major(ht_parts)
            pe.wait_ge(S["oat_low"], 1)
            for c in range(2):
                prod.token_major((oat_high_r, oat_r))
            for c in range(2):
                prod.token_major((obt_r, obt_low_r))
            stage.end()
            turn_pe(pe, va, KD)
            stage.end()
            for c in range(2):
                prod.token_major(ht_parts2)
            stage.end()
            stage.end()
            block2_pe(pe, stage, prod)
            moe_pe(pe, stage)
            tail_pe(pe, stage, prod)

        @block.scalar
        def _(act):
            act_steps[0] = Steps(act, S["act_step"])
            stage = Stage(act, S["stage"])
            moves = Moves(act, 0)
            act.wait_ge(S["x_in"], 16)
            act.wait_ge(S["const_in"], 16)
            norm_act(act, xs, [(0, D)], extra[:, 0, :])
            moves.split(0)
            act.wait_ge(S["w_pre_in"], 16)
            turn_high(act, ht_r, w_pre)
            moves.split(1)
            stage.end()
            moves.take(24, lambda i, b: copy_out(act, fm[:, i, :], ps[:, b, 0:T]))
            moves.take(4, lambda i, b: copy_out(act, zb[:, i % 2, BANK * (i // 2):BANK * (i // 2) + BANK], ps[:, b, :]))
            stage.end()
            nc.scalar.activation(fm[:, 16:24, :], fm[:, 16:24, :], ACT.Silu).then_inc(S["silu_za"], 1)
            zb_half = extra[:, 1, :].rearrange("p (t n) -> p t n", t=NT)[:, :, 0:BANK]

            def between_act(i):
                if i == 2:
                    moves.split(in_attention + 1)
                if i == 5:
                    moves.take(1, lambda j, b: copy_out(act, zb_half[:, 0, :], ps[:, 6, :]))
                    moves.skip(1)

            attention_act(act, 0, between_act)
            stage.end()
            for c in range(8):
                if c < 6:
                    moves.take(4, lambda i, b: copy_out(act, fm[:, 4 * c + i, :], ps[:, b, 0:T]))
                    conv_act(act, c, moves)
                elif c == 6:
                    moves.take(2, lambda i, b: copy_out(act, zb[:, i, BANK:D], ps[:, b, :]))
                if c >= 2:
                    act.wait_ge(S["conv"], c - 1)
                    i = 4 * (c - 2)
                    nc.scalar.activation(fm[:, i:i + 4, :], extra[:, i // 8, T * (i % 8):T * (i % 8 + 4)].rearrange("p (c n) -> p c n", c=4), ACT.Silu)
            stage.end()
            gdn_act(act, stage, moves)
            for g in range(2):
                moves.take(4, lambda i, b: nc.scalar.activation(gates[:, g, i % 2, BANK * (i // 2):BANK * (i // 2) + BANK], ps[:, b, :], ACT.Sigmoid), whole=True)
                if g == 0:
                    nc.scalar.activation(oat_high_r, oat[:, :, :], ACT.Copy).then_inc(S["oat_high"], 1)
            moves.skip(8)
            stage.end()
            turn_high(act, ht_r, None)
            stage.end()
            moves.take(4, lambda i, b: copy_out(act, va[:, i % 2, BANK * (i // 2):BANK * (i // 2) + BANK], ps[:, b, :]))
            stage.end()
            norm_act(act, va, [(0, D)], extra[:, 0, :])
            stage.end()
            block2_act(act, stage, moves)
            moe_act(act, stage, moves)
            tail_act(act, stage, moves)

        @block.vector
        def _(dve):
            dve_steps[0] = Steps(dve, S["dve_step"])
            stage = Stage(dve, S["stage"])
            moves = Moves(dve, 1)
            norm_dve(dve, xs, [(0, D)], oat_tm)
            dve.wait_ge(S["w_pre_in"], 16)
            turn_low(dve, ht_r, ht_low_r, w_pre)
            moves.split(0)
            stage.end()
            moves.split(1)
            moves.take(24, lambda i, b: copy_out(dve, fm[:, i, :], ps[:, b, 0:T]))
            moves.take(4, lambda i, b: copy_out(dve, zb[:, i % 2, BANK * (i // 2):BANK * (i // 2) + BANK], ps[:, b, :]))
            stage.end()
            sinb = con("sin", slice(0, 32)).unsqueeze(1).to_broadcast([32, 2, T])
            for m in range(8):
                r1, r2 = rope_scratch(m)
                dve.wait_ge(S["rotated"], m + 1)
                dve_step(nc.vector.tensor_tensor(r1, ps[0:32, m, :].rearrange("p (a b) -> p a b", a=2), sinb, ALU.mult))
                if m in ROPE_POOL:
                    dve.wait_ge(S["cos_part"], ROPE_POOL.index(m) + 1)
                else:
                    dve_step(nc.vector.tensor_tensor(r2, fm[0:32, 2 * m:2 * m + 2, :], cosb, ALU.mult))
                nc.vector.tensor_tensor(fm[0:32, 2 * m:2 * m + 2, :], r1, r2, ALU.add).then_inc(S["roped"], 1)

            def take_a(h):
                if h == 0:
                    dve.wait_ge(S["silu_za"], 1)
                dve.wait_ge(S["head_out"], h + 1)
                nc.vector.tensor_tensor(oat[:, h, :], ps[:, 4 + h % 2, 0:T], fm[:, 16 + h, :], ALU.mult).then_inc(S["head_taken"], 1)

            zb_half = extra[:, 1, :].rearrange("p (t n) -> p t n", t=NT)[:, :, 0:BANK]

            def between_dve(i):
                if i == HEADS + 1:
                    moves.skip(1)
                    moves.take(1, lambda j, b: copy_out(dve, zb_half[:, 1, :], ps[:, 7, :]))

            attention_dve(dve, 0, float(P) ** -0.5, take_a, between_dve)
            dve.wait_ge(S["conv_turned"], 1)
            nc.vector.tensor_copy(cw[:, :], ps[:, 3, 0:96])
            stage.end()
            for c in range(7):
                if c < 6:
                    moves.take(4, lambda i, b: copy_out(dve, fm[:, 4 * c + i, :], ps[:, b, 0:T]))
                else:
                    moves.take(2, lambda i, b: copy_out(dve, zb[:, i, BANK:D], ps[:, b, :]))
                if 1 <= c < 7:
                    conv_dve(dve, c - 1)
            dve.wait_ge(S["bd_logits"], 1)
            nc.vector.tensor_copy(bd[:, 0, :].rearrange("p (t h) -> p t h", t=NT), ps[:, 7, 0:32].rearrange("p (t a h) -> p t a h", t=NT, a=2)[:, :, 0, :])
            nc.vector.tensor_copy(bd[:, 1, :].rearrange("p (t h) -> p t h", t=NT), ps[:, 7, 0:32].rearrange("p (t a h) -> p t a h", t=NT, a=2)[:, :, 1, :])
            stage.end()
            gdn_dve(dve, stage, moves)
            moves.skip(4)
            dve.wait_ge(S["oat_high"], 1)
            nc.vector.tensor_tensor(oat_r[:, :, :], oat[:, :, :], oat_high_r.bitcast(F32), ALU.subtract).then_inc(S["oat_low"], 1)
            moves.skip(4)
            dve.wait_ge(S["moved0"], moves.u // 2)
            dve.wait_ge(S["moved1"], moves.u // 2)

            def gated(i, b):
                t, c = i % 2, BANK * (i % 4 // 2)
                return nc.vector.tensor_tensor((va, zb)[i // 4][:, t, c:c + BANK], ps[:, b, :], gates[:, i // 4, t, c:c + BANK], ALU.mult)

            moves.take(4, gated, whole=True)
            for i in range(4, 8):
                moves.take(1, lambda _, b: gated(i, b), whole=True)
                dve.wait_ge(S[f"moved{(moves.u - 1) % 2}"], (moves.u - 1) // 2 + 1)
                t, c = i % 2, BANK * (i % 4 // 2)
                nc.vector.tensor_tensor(va[:, t, c:c + BANK], va[:, t, c:c + BANK], zb[:, t, c:c + BANK], ALU.add)
            stage.end()
            turn_low(dve, ht_r, ht_low2_r, None)
            stage.end()
            moves.take(4, lambda i, b: copy_out(dve, va[:, i % 2, BANK * (i // 2):BANK * (i // 2) + BANK], ps[:, b, :]))
            stage.end()
            norm_dve(dve, va, [(0, D)], None)
            dve.wait_ge(S["row_in"], 16)
            for t in range(NT):
                dve_step(nc.vector.scalar_tensor_tensor(out=va[:, t, :], in0=va[:, t, :], scalar=ssq[:, t:t + 1], in1=extra[:, 2, 0:D], op0=ALU.mult, op1=ALU.mult))
                nc.vector.tensor_tensor(xs[:, t, :], xs[:, t, :], va[:, t, :], ALU.add).then_inc(S["x_summed"], 1)
            stage.end()
            block2_dve(dve, stage, moves)
            moe_dve(dve, stage, moves)
            tail_dve(dve, stage, moves)


_INS = ["x", "pre_norm_w", "w_in", "conv_w", "a_log", "dt_bias", "gdn_norm_w", "w_branch_a", "w_branch_b", "w_out",
        "post_norm_w", "p_2", "positions_2", "w_in_2", "g_attn_2", "g_cq_2", "w_uq_2", "g_ckv_2", "w_ukv_2",
        "g_out_mla_2", "g_out_sb_2", "w_o_2", "g_moe_2", "w_router_2", "b_router_2", "w_gu_2", "b_gu_2", "w_dn_2",
        "b_dn_2", "g_ple_2", "w_ple_gate_2", "w_ple_proj_2", "g_final_2"]
_OUT = ((1, T, D), "float32")


def kernel(**inputs):
    import numpy as _np
    import concourse.bacc as _bacc
    from concourse import mybir as _mybir
    from concourse.bass_utils import run_bass_kernel_spmd as _run

    nc = _bacc.Bacc("TRN2", target_bir_lowering=False, num_devices=1)
    arrays, tensors = {}, {}
    for name in _INS + ["const"]:
        a = constants()[0] if name == "const" else _np.ascontiguousarray(inputs[name])
        arrays[f"in_{name}_dram"] = a
        tensors[name] = nc.dram_tensor(f"in_{name}_dram", a.shape, _mybir.dt.from_np(a.dtype), kind="ExternalInput").ap()
    shape, dtype = _OUT
    out = nc.dram_tensor("out_0_dram", shape, _mybir.dt.from_np(_np.dtype(dtype)), kind="ExternalOutput").ap()
    hybrid_two_block_kernel(nc, tensors, out)
    r = _run(nc, [arrays], core_ids=[0])
    return r.results[0]["out_0_dram"]
```
